# Optimizing a Trainium2 kernel written in Bass

```python
import jax, jax.numpy as jnp
from jax import lax
import numpy as np
import math

D_MODEL = 1024
BATCH = 1
SEQ = 1024
DEPTH = 1

CHUNK = 64
D_MIX = D_MODEL

GLA_W = D_MIX // 2
GLA_HEADS = 4
GLA_DV = GLA_W // GLA_HEADS
GLA_DK = GLA_DV // 2
GLA_QK_W = GLA_HEADS * GLA_DK
GLA_GATE_RANK = 16
GLA_GATE_TAU = 16.0

HGRN_W = D_MIX // 4
HGRN_HEADS = 4
HGRN_DV = HGRN_W // HGRN_HEADS
HGRN_DK = 64
HGRN_QK_W = HGRN_HEADS * HGRN_DK

SB_W = D_MIX - GLA_W - HGRN_W
SB_HEADS = 4
SB_DH = SB_W // SB_HEADS
SB_BLOCK = 128

IN_WIDTHS = (GLA_QK_W, GLA_QK_W, GLA_W, GLA_GATE_RANK, GLA_W,
             HGRN_QK_W, HGRN_QK_W, HGRN_W, HGRN_W,
             SB_W, SB_W, SB_W, SB_W)
D_IN = sum(IN_WIDTHS)
EPS = 1e-6


def rms_norm(x):
    xf = x.astype(jnp.float32)
    y = xf * lax.rsqrt(jnp.mean(xf * xf, axis=-1, keepdims=True) + EPS)
    return y.astype(x.dtype)

def split_heads(a, n_heads):
    b, t, w = a.shape
    return a.reshape(b, t, n_heads, w // n_heads).transpose(0, 2, 1, 3)

def merge_heads(a):
    b, h, t, d = a.shape
    return a.transpose(0, 2, 1, 3).reshape(b, t, h * d)

def chunk_gated_linear_attn(q, k, v, g):
    bsz, nh, t, dk = q.shape
    dv = v.shape[-1]
    n_chunks = t // CHUNK

    def to_chunks(a):
        return a.reshape(bsz, nh, n_chunks, CHUNK, a.shape[-1]).transpose(2, 0, 1, 3, 4)

    causal = jnp.tril(jnp.ones((CHUNK, CHUNK), dtype=bool))[:, :, None]

    def step(state, inp):
        q_c, k_c, v_c, g_c = inp
        b_cum = jnp.cumsum(g_c, axis=2)
        diff = b_cum[:, :, :, None, :] - b_cum[:, :, None, :, :]
        decay = jnp.exp(jnp.where(causal, diff, -jnp.inf))
        scores = jnp.einsum('bhtd,bhsd,bhtsd->bhts', q_c, k_c, decay)
        o_c = (jnp.einsum('bhts,bhsv->bhtv', scores, v_c)
               + jnp.einsum('bhtd,bhdv->bhtv', q_c * jnp.exp(b_cum), state))
        b_last = b_cum[:, :, -1:, :]
        state = (jnp.exp(b_last[:, :, 0, :, None]) * state
                 + jnp.einsum('bhsd,bhsv->bhdv', k_c * jnp.exp(b_last - b_cum), v_c))
        return state, o_c

    s0 = jnp.zeros((bsz, nh, dk, dv), dtype=v.dtype)
    _, o = lax.scan(step, s0, (to_chunks(q), to_chunks(k), to_chunks(v), to_chunks(g)))
    return o.transpose(1, 2, 0, 3, 4).reshape(bsz, nh, t, dv)

def stick_breaking_attn(q, k, v):
    bsz, nh, t, dh = q.shape
    scale = dh ** -0.5
    outs = []
    for i in range(t // SB_BLOCK):
        n_keys = (i + 1) * SB_BLOCK
        q_blk = q[:, :, i * SB_BLOCK:n_keys]
        k_blk = k[:, :, :n_keys]
        v_blk = v[:, :, :n_keys]
        z = jnp.einsum('bhtd,bhsd->bhts', q_blk, k_blk).astype(jnp.float32) * scale
        t_pos = i * SB_BLOCK + jnp.arange(SB_BLOCK)[:, None]
        s_pos = jnp.arange(n_keys)[None, :]
        strict = s_pos < t_pos
        log_beta = jax.nn.log_sigmoid(z)
        log_1m_beta = jnp.where(strict, jax.nn.log_sigmoid(-z), 0.0)
        between = lax.cumsum(log_1m_beta, axis=3, reverse=True) - log_1m_beta
        weights = jnp.where(strict, jnp.exp(log_beta + between), 0.0)
        outs.append(jnp.einsum('bhts,bhsv->bhtv', weights.astype(v.dtype), v_blk))
    return jnp.concatenate(outs, axis=2)

def split_columns(p):
    idx = []
    acc = 0
    for w in IN_WIDTHS[:-1]:
        acc += w
        idx.append(acc)
    return jnp.split(p, idx, axis=-1)

def first_inputs(seed: int = 0) -> dict:
    key = jax.random.key(seed)
    ks = jax.random.split(key, 12)
    f32 = jnp.float32
    x = jax.random.normal(ks[0], (BATCH, SEQ, D_MODEL), f32)
    c = jax.random.normal(ks[1], (BATCH, D_MODEL), f32)
    w_ada = jax.random.normal(ks[2], (DEPTH, D_MODEL, 3 * D_MODEL), f32) * (0.5 * D_MODEL ** -0.5)
    b_ada = 0.02 * jax.random.normal(ks[3], (DEPTH, 3 * D_MODEL), f32)
    w_in = jax.random.normal(ks[4], (DEPTH, D_MODEL, D_IN), f32) * D_MODEL ** -0.5
    w_gla_gate2 = jax.random.normal(ks[5], (DEPTH, GLA_GATE_RANK, GLA_QK_W), f32) * GLA_GATE_RANK ** -0.5
    b_gla_gate = 0.1 * jax.random.normal(ks[6], (DEPTH, GLA_QK_W), f32)
    gla_norm_w = 1.0 + 0.1 * jax.random.normal(ks[7], (DEPTH, GLA_DV), f32)
    hgrn_lb_logits = jax.random.normal(ks[8], (DEPTH, HGRN_QK_W), f32)
    hgrn_norm_w = 1.0 + 0.1 * jax.random.normal(ks[9], (DEPTH, HGRN_DV), f32)
    w_out = jax.random.normal(ks[10], (DEPTH, D_MIX, D_MODEL), f32) * D_MIX ** -0.5
    final_norm_w = 1.0 + 0.1 * jax.random.normal(ks[11], (D_MODEL,), f32)
    return {'x': x, 'c': c, 'w_ada': w_ada, 'b_ada': b_ada, 'w_in': w_in,
            'w_gla_gate2': w_gla_gate2, 'b_gla_gate': b_gla_gate, 'gla_norm_w': gla_norm_w,
            'hgrn_lb_logits': hgrn_lb_logits, 'hgrn_norm_w': hgrn_norm_w,
            'w_out': w_out, 'final_norm_w': final_norm_w}

def first_block(x, c, w_ada, b_ada, w_in, w_gla_gate2, b_gla_gate, gla_norm_w,
              hgrn_lb_logits, hgrn_norm_w, w_out, final_norm_w):
    c_act = jax.nn.silu(c)
    probs = jax.nn.softmax(hgrn_lb_logits.astype(jnp.float32), axis=0)
    cum = jnp.cumsum(probs, axis=0)
    lower_bounds = (cum - cum[0:1]).astype(x.dtype)

    for l in range(DEPTH):
        ada = c_act @ w_ada[l] + b_ada[l]
        shift, scale, gate = jnp.split(ada, 3, axis=-1)
        h = rms_norm(x) * (1.0 + scale[:, None, :]) + shift[:, None, :]
        p = h @ w_in[l]
        (qa, ka, va, lra, ga,
         qb, fb, ib, gb,
         qc, kc, vc, gc) = split_columns(p)

        log_alpha = jax.nn.log_sigmoid(lra @ w_gla_gate2[l] + b_gla_gate[l]) / GLA_GATE_TAU
        o_a = chunk_gated_linear_attn(split_heads(qa, GLA_HEADS) * GLA_DK ** -0.5,
                                      split_heads(ka, GLA_HEADS),
                                      split_heads(va, GLA_HEADS),
                                      split_heads(log_alpha, GLA_HEADS))
        o_a = merge_heads(rms_norm(o_a) * gla_norm_w[l]) * jax.nn.silu(ga)

        lb = lower_bounds[l]
        log_f = jnp.logaddexp(jnp.log(lb), jnp.log1p(-lb) + jax.nn.log_sigmoid(fb))
        k_b = (1.0 - lb) * jax.nn.sigmoid(-fb)
        o_b = chunk_gated_linear_attn(split_heads(jax.nn.silu(qb), HGRN_HEADS),
                                      split_heads(k_b, HGRN_HEADS),
                                      split_heads(ib, HGRN_HEADS),
                                      split_heads(log_f, HGRN_HEADS))
        o_b = merge_heads(rms_norm(o_b) * hgrn_norm_w[l]) * jax.nn.silu(gb)

        o_c = stick_breaking_attn(split_heads(qc, SB_HEADS),
                                  split_heads(kc, SB_HEADS),
                                  split_heads(vc, SB_HEADS))
        o_c = merge_heads(o_c) * jax.nn.silu(gc)

        y = jnp.concatenate([o_a, o_b, o_c], axis=-1) @ w_out[l]
        x = x + gate[:, None, :] * y

    return rms_norm(x) * final_norm_w


ATT_HEADS = 8
ATT_KV_HEADS = 2
ATT_HEAD_DIM = 64
ATT_GROUP = ATT_HEADS // ATT_KV_HEADS
WINDOW = 128
BLOCK = 128
ML_HEADS = 4
ML_HEAD_DIM = 128
ML_CHUNK = 64
CONV_WIDTH = 4
MEM_LEN = 256
X_HEADS = 4
X_HEAD_DIM = 128
N_GROUPS = 4
EXPERTS_PER_GROUP = 8
N_EXPERTS = N_GROUPS * EXPERTS_PER_GROUP
TOP_K = 2
D_EXPERT = 512
MOE_BLOCK = 128

ATT_Q = ATT_HEADS * ATT_HEAD_DIM
ATT_KV = ATT_KV_HEADS * ATT_HEAD_DIM
ML_W = ML_HEADS * ML_HEAD_DIM
MIX_WIDTH = ATT_Q + ML_W
IN_SPLITS = [ATT_Q, ATT_KV, ATT_KV, 2 * ML_W, ML_W, ML_W, 2 * ML_HEADS]
IN_COLS = sum(IN_SPLITS)
IN_OFFSETS = [int(v) for v in np.cumsum(IN_SPLITS)[:-1]]


def rms_norm_2(x, g):
    xf = x.astype(jnp.float32)
    y = xf * lax.rsqrt(jnp.mean(xf * xf, axis=-1, keepdims=True) + EPS)
    return (y * g.astype(jnp.float32)).astype(x.dtype)

def alibi_slopes(n):
    return jnp.exp2(-8.0 * jnp.arange(1, n + 1, dtype=jnp.float32) / n)

def causal_depthwise_conv(x, w, b):
    c = x.shape[-1]
    y = lax.conv_general_dilated(x, w[:, None, :], window_strides=(1,),
                                 padding=[(CONV_WIDTH - 1, 0)],
                                 dimension_numbers=('NWC', 'WIO', 'NWC'),
                                 feature_group_count=c)
    return y + b

def sliding_window_gqa(q, k, v, sinks):
    bsz, s = q.shape[0], q.shape[1]
    nb = s // BLOCK
    qb = q.reshape(bsz, nb, BLOCK, ATT_KV_HEADS, ATT_GROUP, ATT_HEAD_DIM)

    def with_prev(t):
        t = t.reshape(bsz, nb, BLOCK, ATT_KV_HEADS, ATT_HEAD_DIM)
        prev = jnp.pad(t[:, :-1], ((0, 0), (1, 0), (0, 0), (0, 0), (0, 0)))
        return jnp.concatenate([prev, t], axis=2)

    kk, vv = with_prev(k), with_prev(v)
    scores = jnp.einsum('bnqkgd,bnskd->bkgnqs', qb, kk).astype(jnp.float32)
    scores = scores * (1.0 / math.sqrt(ATT_HEAD_DIM))
    dist = (jnp.arange(BLOCK)[:, None] + BLOCK) - jnp.arange(2 * BLOCK)[None, :]
    in_band = (dist >= 0) & (dist < WINDOW)
    pad_key = (jnp.arange(nb)[:, None, None] == 0) & (jnp.arange(2 * BLOCK)[None, None, :] < BLOCK)
    valid = in_band[None] & ~pad_key
    slopes = alibi_slopes(ATT_HEADS).reshape(ATT_KV_HEADS, ATT_GROUP)[:, :, None, None, None]
    logits = scores - slopes * dist.astype(jnp.float32)
    logits = jnp.where(valid, logits, -jnp.inf)
    sink = sinks.astype(jnp.float32).reshape(ATT_KV_HEADS, ATT_GROUP)[:, :, None, None, None]
    mx = jnp.maximum(logits.max(axis=-1, keepdims=True), sink)
    e = jnp.exp(logits - mx)
    p = e / (e.sum(axis=-1, keepdims=True) + jnp.exp(sink - mx))
    out = jnp.einsum('bkgnqs,bnskd->bnqkgd', p.astype(v.dtype), vv)
    return out.reshape(bsz, s, ATT_Q)

def mlstm_chunk_step(carry, inp):
    c_st, n_st, m_st = carry
    q, k, v, ig, lf = inp
    L = q.shape[2]
    b = jnp.cumsum(lf, axis=-1)
    causal = jnp.tril(jnp.ones((L, L), dtype=bool))
    log_d = jnp.where(causal, b[..., :, None] - b[..., None, :] + ig[..., None, :], -jnp.inf)
    m_inter = b + m_st[..., None]
    m_t = jnp.maximum(m_inter, log_d.max(axis=-1))
    s = jnp.einsum('bhtd,bhsd->bhts', q, k) * jnp.exp(log_d - m_t[..., None])
    a_inter = jnp.exp(m_inter - m_t)
    num = jnp.einsum('bhts,bhsd->bhtd', s, v) + a_inter[..., None] * jnp.einsum('bhtk,bhkv->bhtv', q, c_st)
    den = s.sum(axis=-1) + a_inter * jnp.einsum('bhtk,bhk->bht', q, n_st)
    h = num / jnp.maximum(jnp.abs(den), jnp.exp(-m_t))[..., None]
    b_last = b[..., -1]
    log_w = b_last[..., None] - b + ig
    m_new = jnp.maximum(b_last + m_st, log_w.max(axis=-1))
    w = jnp.exp(log_w - m_new[..., None])
    decay = jnp.exp(b_last + m_st - m_new)
    c_new = decay[..., None, None] * c_st + jnp.einsum('bhsk,bhsv->bhkv', k * w[..., None], v)
    n_new = decay[..., None] * n_st + jnp.einsum('bhs,bhsk->bhk', w, k)
    return (c_new, n_new, m_new), h

def mlstm(q, k, v, i_pre, f_pre):
    bsz, s, nh, dh = q.shape
    nc = s // ML_CHUNK
    f32 = jnp.float32
    def chunks(t):
        return t.astype(f32).reshape(bsz, nc, ML_CHUNK, nh, dh).transpose(1, 0, 3, 2, 4)
    def gchunks(t):
        return t.reshape(bsz, nc, ML_CHUNK, nh).transpose(1, 0, 3, 2)
    qc = chunks(q)
    kc = chunks(k) * (1.0 / math.sqrt(dh))
    vc = chunks(v)
    igc = gchunks(i_pre.astype(f32))
    lfc = gchunks(jax.nn.log_sigmoid(f_pre.astype(f32)))
    init = (jnp.zeros((bsz, nh, dh, dh), f32), jnp.zeros((bsz, nh, dh), f32), jnp.zeros((bsz, nh), f32))
    _, hs = lax.scan(mlstm_chunk_step, init, (qc, kc, vc, igc, lfc))
    return hs.transpose(1, 0, 3, 2, 4).reshape(bsz, s, nh, dh)

def memory_cross_attention(xn, memn, w_cq, w_ckv, w_co):
    bsz, s, _ = xn.shape
    q = (xn @ w_cq).reshape(bsz, s, X_HEADS, X_HEAD_DIM)
    kv = (memn @ w_ckv).reshape(bsz, memn.shape[1], 2, X_HEADS, X_HEAD_DIM)
    k, v = kv[:, :, 0], kv[:, :, 1]
    sc = jnp.einsum('bshd,bmhd->bhsm', q, k).astype(jnp.float32) * (1.0 / math.sqrt(X_HEAD_DIM))
    p = jax.nn.softmax(sc, axis=-1)
    o = jnp.einsum('bhsm,bmhd->bshd', p.astype(v.dtype), v).reshape(bsz, s, X_HEADS * X_HEAD_DIM)
    return o @ w_co

def hierarchical_moe(xn, w_rg, b_rg, w_re, b_re, w_g, w_u, w_d):
    bsz, s, d = xn.shape
    t = bsz * s
    xt = xn.reshape(t, d)
    g_logits = (xt @ w_rg).astype(jnp.float32) + b_rg.astype(jnp.float32)
    g_prob = jax.nn.softmax(g_logits, axis=-1)
    g_sel = jnp.argmax(g_logits, axis=-1)
    g_w = jnp.take_along_axis(g_prob, g_sel[:, None], axis=-1)
    e_logits = ((xt @ w_re).astype(jnp.float32) + b_re.astype(jnp.float32)).reshape(t, N_GROUPS, EXPERTS_PER_GROUP)
    e_in = jnp.take_along_axis(e_logits, g_sel[:, None, None], axis=1)[:, 0]
    top_v, top_i = lax.top_k(e_in, TOP_K)
    top_p = jax.nn.softmax(top_v, axis=-1) * g_w
    expert_idx = (g_sel[:, None] * EXPERTS_PER_GROUP + top_i).reshape(-1)
    gates = top_p.reshape(-1)
    n_assign = t * TOP_K
    token_idx = jnp.arange(n_assign) // TOP_K
    order = jnp.argsort(expert_idx)
    sorted_e = expert_idx[order]
    counts = jnp.bincount(expert_idx, length=N_EXPERTS)
    padded = (counts + MOE_BLOCK - 1) // MOE_BLOCK * MOE_BLOCK
    pad_end = jnp.cumsum(padded)
    pad_start = pad_end - padded
    start = jnp.cumsum(counts) - counts
    dest = pad_start[sorted_e] + (jnp.arange(n_assign) - start[sorted_e])
    n_blocks = -(-n_assign // MOE_BLOCK) + N_EXPERTS
    x_pad = jnp.zeros((n_blocks * MOE_BLOCK, d), xt.dtype).at[dest].set(xt[token_idx[order]])
    block_e = jnp.minimum(jnp.searchsorted(pad_end, jnp.arange(n_blocks) * MOE_BLOCK, side='right'), N_EXPERTS - 1)

    def expert_block(args):
        xb, e = args
        hb = jax.nn.silu(xb @ w_g[e]) * (xb @ w_u[e])
        return hb @ w_d[e]

    y_pad = lax.map(expert_block, (x_pad.reshape(n_blocks, MOE_BLOCK, d), block_e)).reshape(-1, d)
    y = y_pad[dest] * gates[order][:, None].astype(y_pad.dtype)
    out = jnp.zeros((t, d), xt.dtype).at[token_idx[order]].add(y)
    return out.reshape(bsz, s, d)

def second_inputs(seed: int = 0) -> dict:
    key = jax.random.key(seed)
    ks = iter(jax.random.split(key, 40))
    f32 = jnp.float32

    def nrm(shape, scale):
        return jax.random.normal(next(ks), shape, f32) * scale

    def gain(shape):
        return 1.0 + nrm(shape, 0.02)

    L = DEPTH
    x = nrm((BATCH, SEQ, D_MODEL), 1.0)
    mem = nrm((BATCH, MEM_LEN, D_MODEL), 1.0)
    b_i = nrm((L, ML_HEADS), 0.1)
    b_f = jnp.linspace(3.0, 6.0, ML_HEADS, dtype=f32)[None, :] + nrm((L, ML_HEADS), 0.01)
    return {
        'x': x,
        'mem': mem,
        'norm_mix': gain((L, D_MODEL)),
        'w_in': nrm((L, D_MODEL, IN_COLS), D_MODEL ** -0.5),
        'b_gates': jnp.concatenate([b_i, b_f], axis=-1),
        'conv_w': nrm((L, CONV_WIDTH, 2 * ML_W), CONV_WIDTH ** -0.5),
        'conv_b': nrm((L, 2 * ML_W), 0.01),
        'att_sinks': nrm((L, ATT_HEADS), 0.5),
        'norm_att_out': gain((L, ATT_Q)),
        'norm_ml_out': gain((L, ML_W)),
        'w_out': nrm((L, MIX_WIDTH, D_MODEL), MIX_WIDTH ** -0.5),
        'norm_cross': gain((L, D_MODEL)),
        'norm_mem': gain((L, D_MODEL)),
        'w_cq': nrm((L, D_MODEL, X_HEADS * X_HEAD_DIM), D_MODEL ** -0.5),
        'w_ckv': nrm((L, D_MODEL, 2 * X_HEADS * X_HEAD_DIM), D_MODEL ** -0.5),
        'w_co': nrm((L, X_HEADS * X_HEAD_DIM, D_MODEL), (X_HEADS * X_HEAD_DIM) ** -0.5),
        'norm_ffn': gain((L, D_MODEL)),
        'w_router_group': nrm((L, D_MODEL, N_GROUPS), D_MODEL ** -0.5),
        'b_router_group': nrm((L, N_GROUPS), 0.01),
        'w_router_expert': nrm((L, D_MODEL, N_EXPERTS), D_MODEL ** -0.5),
        'b_router_expert': nrm((L, N_EXPERTS), 0.01),
        'w_e_gate': nrm((L, N_EXPERTS, D_MODEL, D_EXPERT), D_MODEL ** -0.5),
        'w_e_up': nrm((L, N_EXPERTS, D_MODEL, D_EXPERT), D_MODEL ** -0.5),
        'w_e_down': nrm((L, N_EXPERTS, D_EXPERT, D_MODEL), D_EXPERT ** -0.5),
        'norm_final': gain((D_MODEL,)),
    }

def second_block(x, mem, norm_mix, w_in, b_gates, conv_w, conv_b, att_sinks, norm_att_out,
              norm_ml_out, w_out, norm_cross, norm_mem, w_cq, w_ckv, w_co, norm_ffn,
              w_router_group, b_router_group, w_router_expert, b_router_expert,
              w_e_gate, w_e_up, w_e_down, norm_final):
    bsz, s, _ = x.shape
    for l in range(DEPTH):
        h = rms_norm_2(x, norm_mix[l])
        proj = h @ w_in[l]
        q_a, k_a, v_a, qk_m, v_m, o_m, g_m = jnp.split(proj, IN_OFFSETS, axis=-1)
        att = sliding_window_gqa(q_a.reshape(bsz, s, ATT_HEADS, ATT_HEAD_DIM),
                                 k_a.reshape(bsz, s, ATT_KV_HEADS, ATT_HEAD_DIM),
                                 v_a.reshape(bsz, s, ATT_KV_HEADS, ATT_HEAD_DIM),
                                 att_sinks[l])
        att = rms_norm_2(att, norm_att_out[l])
        qk_m = jax.nn.silu(causal_depthwise_conv(qk_m, conv_w[l], conv_b[l]))
        q_m, k_m = jnp.split(qk_m, 2, axis=-1)
        g_m = g_m + b_gates[l]
        i_pre, f_pre = g_m[..., :ML_HEADS], g_m[..., ML_HEADS:]
        hm = mlstm(q_m.reshape(bsz, s, ML_HEADS, ML_HEAD_DIM),
                   k_m.reshape(bsz, s, ML_HEADS, ML_HEAD_DIM),
                   v_m.reshape(bsz, s, ML_HEADS, ML_HEAD_DIM), i_pre, f_pre)
        hm = jax.nn.sigmoid(o_m.astype(jnp.float32)).reshape(bsz, s, ML_HEADS, ML_HEAD_DIM) * hm
        hm = rms_norm_2(hm.astype(x.dtype), norm_ml_out[l].reshape(ML_HEADS, ML_HEAD_DIM)).reshape(bsz, s, ML_W)
        x = x + jnp.concatenate([att, hm], axis=-1) @ w_out[l]
        x = x + memory_cross_attention(rms_norm_2(x, norm_cross[l]), rms_norm_2(mem, norm_mem[l]),
                                       w_cq[l], w_ckv[l], w_co[l])
        x = x + hierarchical_moe(rms_norm_2(x, norm_ffn[l]), w_router_group[l], b_router_group[l],
                                 w_router_expert[l], b_router_expert[l],
                                 w_e_gate[l], w_e_up[l], w_e_down[l])
    return rms_norm_2(x, norm_final)


def setup_inputs(seed=0):
    out = dict(first_inputs(seed))
    for name, value in second_inputs(seed + 1).items():
        if name != "x":
            out[name + "_2"] = value
    return out


def reference(
    x, c, w_ada, b_ada, w_in, w_gla_gate2, b_gla_gate, gla_norm_w, hgrn_lb_logits, hgrn_norm_w,
    w_out, final_norm_w, mem_2, norm_mix_2, w_in_2, b_gates_2, conv_w_2, conv_b_2, att_sinks_2,
    norm_att_out_2, norm_ml_out_2, w_out_2, norm_cross_2, norm_mem_2, w_cq_2, w_ckv_2, w_co_2,
    norm_ffn_2, w_router_group_2, b_router_group_2, w_router_expert_2, b_router_expert_2,
    w_e_gate_2, w_e_up_2, w_e_down_2, norm_final_2,
):
    x = first_block(
        x, c, w_ada, b_ada, w_in, w_gla_gate2, b_gla_gate, gla_norm_w, hgrn_lb_logits,
        hgrn_norm_w, w_out, final_norm_w,
    )
    return second_block(
        x, mem_2, norm_mix_2, w_in_2, b_gates_2, conv_w_2, conv_b_2, att_sinks_2,
        norm_att_out_2, norm_ml_out_2, w_out_2, norm_cross_2, norm_mem_2, w_cq_2, w_ckv_2,
        w_co_2, norm_ffn_2, w_router_group_2, b_router_group_2, w_router_expert_2,
        b_router_expert_2, w_e_gate_2, w_e_up_2, w_e_down_2, norm_final_2,
    )


_drawn_inputs = setup_inputs


def setup_inputs(seed=0):
    import zlib

    import numpy as np

    out = dict(_drawn_inputs(seed))
    spreads = {}
    factors = {'b_gla_gate': 3.055,
     'conv_b_2': 7.19,
     'norm_att_out_2': 3.36,
     'norm_ml_out_2': 3.345,
     'norm_cross_2': 8.0,
     'norm_mem_2': 8.0,
     'b_router_group_2': 30.904,
     'b_router_expert_2': 40.912,
     'norm_final_2': 7.913,
     'norm_ffn_2': 8.0}
    for name, (base, spread) in spreads.items():
        noise = np.random.default_rng([zlib.crc32(name.encode()), seed]).standard_normal(out[name].shape)
        drawn = base * np.exp(spread * noise) if base else spread * noise
        out[name] = __import__('jax').numpy.asarray(drawn.astype(out[name].dtype))
    for name, factor in factors.items():
        out[name] = (out[name] * factor).astype(out[name].dtype)
    return out
```

```python
from contextlib import ExitStack

import numpy as np

import concourse.bass as bass
from concourse import mybir

F32 = mybir.dt.float32
U32 = mybir.dt.uint32
I32 = mybir.dt.int32
ALU = mybir.AluOpType
ACT = mybir.ActivationFunctionType
AX_X = mybir.AxisListType.X

P = 128
T = 1024
D = 1024
NT = T // P
NK = D // P
HALF = 512
EPS = 1e-6

GLA_HEADS, GLA_DV, HGRN_HEADS, HGRN_DV, SB_HEADS, DK = 4, 128, 4, 64, 4, 64
RANK = 16
TAU = 16.0
LEVELS = 7

ATT_HEADS, KV_HEADS, ML_HEADS, ML_D, TAPS = 8, 2, 4, 128, 4
VA = ML_D + 1
MEM = 256
GROUPS, PER_GROUP = 4, 8
EXPERTS = GROUPS * PER_GROUP
DE = 512
SPARE = T * 2 // P - 1
BLOCKS = EXPERTS + SPARE
SLOTS = BLOCKS * P
BIG = 1e30
PHASES_BEFORE_ROUTING = 10

CONST = {}
_at = 0
for _name, _n in (("ident", P), ("negtri", P), ("negones", P), ("ones", P), ("strict", P), ("causal", P),
                  ("dist", 2 * P), ("sel", ML_HEADS * P), ("iota32", EXPERTS), ("token", NT)):
    CONST[_name] = (_at, _n)
    _at += _n
CONSTS = _at


def constants():
    c = np.zeros((P, CONSTS), np.float32)
    r, q = np.arange(P)[:, None], np.arange(P)[None, :]

    def put(name, value):
        at, n = CONST[name]
        c[:, at:at + n] = value

    put("ident", r == q)
    put("negtri", -1.0 * (r >= q))
    put("negones", -1.0)
    put("ones", 1.0)
    put("strict", r < q)
    put("causal", r <= q)
    dist = r + P - np.arange(2 * P)[None, :]
    put("dist", np.where((dist >= 0) & (dist < P), -dist, -BIG))
    sel = np.zeros((P, ML_HEADS, P), np.float32)
    for h in range(ML_HEADS):
        sel[h, h] = 1.0
    put("sel", sel.reshape(P, -1))
    put("iota32", np.arange(EXPERTS)[None, :])
    put("token", r + P * np.arange(NT)[None, :])
    masks = np.zeros((P, LEVELS + 1, P), np.uint32)
    for lvl in range(LEVELS):
        h = P // 2 >> lvl
        masks[:, lvl] = (r // (2 * h) == q // (2 * h)) & (r // h % 2 == 0) & (q // h % 2 == 1)
    masks[:, LEVELS] = r == q
    return c, masks.reshape(P, -1)


class Line:

    def __init__(self, eng, own):
        self.eng, self.own, self.count = eng, own, {}

    def __call__(self, ins, sem=None):
        sem = self.own if sem is None else sem
        self.count[sem.name] = self.count.get(sem.name, 0) + 1
        ins.then_inc(sem, 1)
        self.eng.wait_ge(sem, self.count[sem.name])


class Word:

    def __init__(self, sem):
        self.sem, self.told, self.heard = sem, 0, 0

    def tell(self, eng):
        eng.sem_inc(self.sem, 1)
        self.told += 1

    def hear(self, eng):
        self.heard += 1
        eng.wait_ge(self.sem, self.heard)


class Ring:

    def __init__(self, banks, full, free):
        self.banks, self.full, self.free = banks, full, free
        self.filled = self.taken = 0

    def open(self, pe):
        if self.filled >= len(self.banks):
            pe.wait_ge(self.free, self.filled - len(self.banks) + 1)
        return self.banks[self.filled % len(self.banks)]

    def close(self, ins):
        ins.then_inc(self.full, 1)
        self.filled += 1

    def take(self, eng):
        self.taken += 1
        eng.wait_ge(self.full, self.taken)
        return self.banks[(self.taken - 1) % len(self.banks)]


def program(nc, A, out):
    with ExitStack() as ctx:
        def sb(name, n, dt=F32):
            return ctx.enter_context(nc.sbuf_tensor(name, [P, n], dt))[:, :]

        def sem(name):
            return ctx.enter_context(nc.semaphore(name))

        def cut(ap, n):
            return ap.rearrange("p (a b) -> p a b", a=n)

        cst = sb("cst", CONSTS)
        masks = sb("masks", (LEVELS + 1) * P, U32)
        small = sb("small", 1024)
        gate_row = sb("gate_row", D)
        slots = sb("slots", 3 * NK * HALF)
        HT = cut(sb("HT", NK * T), NK)
        O = cut(sb("O", NT * D), NT)
        WORK = 19000
        work = sb("work", WORK)

        def scratch(name, shape, dt=F32):
            return nc.dram_tensor(name, shape, dt, kind="Internal").ap()

        def const(name, rows=P):
            at, n = CONST[name]
            return cst[0:rows, at:at + n]

        small_at = [0]

        def col(n):
            at = small_at[0]
            small_at[0] += n
            assert small_at[0] <= 1024
            return small[:, at:at + n]

        class Area:
            def __init__(self):
                self.at = 0

            def __call__(self, n):
                self.at += n
                assert self.at <= WORK, self.at
                return work[:, self.at - n:self.at]

        ccol, cact = col(NK), col(NK)
        bcol, mod = col(16), col(16)
        bgate = col(2)
        ss, rstd = col(64), col(64)
        one, zero = col(1), col(1)
        two_heads = col(2)
        decay = col(NT)
        gla_w, hgrn_w = col(GLA_DV), col(HGRN_DV)
        normcols = {n: col(NK) for n in ("norm_mix_2", "norm_cross_2", "norm_mem_2", "norm_ffn_2")}

        sinks, mx, es, rden = col(ATT_HEADS), col(16), col(16), col(16)
        b_if = col(2)
        conv_b, conv_w = col(NK), col(NK * TAPS)
        acm = col(NT * 3 * ML_HEADS)
        expm, wcol, dcol, den = col(NT * ML_HEADS), col(NT), col(NT), col(NT)

        banks = [ctx.enter_context(nc.psum_tensor(f"bank{i}", [P, HALF], F32))[:, :] for i in range(8)]
        ringA = Ring(banks[0:4], sem("act_banks_full"), sem("act_banks_free"))
        ringV = Ring(banks[4:8], sem("dve_banks_full"), sem("dve_banks_free"))

        act_own, dve_own, pool_own = sem("act_own"), sem("dve_own"), sem("pool_own")
        names = ("act", "dve", "pool", "pe")
        words = {(a, b): Word(sem(f"{a}_told_{b}")) for a in names for b in names if a != b and a != "pe"}
        phase = sem("phase_over")
        loaded = sem("small_loaded")
        dma_in = [sem(f"rows_loaded{i}") for i in range(4)]
        dma_out = sem("rows_stored")
        row_in = sem("weight_row_loaded")
        slot_full = [sem(f"slot_full{i}") for i in range(3)]

        chunks, chunk_of, chunk_over = [], {}, {}

        def add_chunk(name, *parts):
            chunk_of[name] = len(chunks)
            chunks.append(parts)

        w_ada, w_in, w_out = (A[n].rearrange("a (k p) n -> p (a k) n", p=P) for n in ("w_ada", "w_in", "w_out"))
        w_in2, w_out2 = (A[n].rearrange("a (k p) n -> p (a k) n", p=P) for n in ("w_in_2", "w_out_2"))
        for n in range(6):
            add_chunk(f"ada{n}", (w_ada, 512 * n, 512 * n + 512))
        add_chunk("a_qk", (w_in, 0, 512))
        add_chunk("a_v", (w_in, 512, 1024))
        add_chunk("a_rank", (w_in, 1024, 1040))
        add_chunk("b_qf", (w_in, 1552, 2064))
        add_chunk("b_v", (w_in, 2064, 2320))
        add_chunk("c_qk", (w_in, 2576, 3088))
        add_chunk("c_v", (w_in, 3088, 3344))
        add_chunk("a_gate", (w_in, 1040, 1552))
        add_chunk("bc_gate", (w_in, 2320, 2576), (w_in, 3344, 3600))
        add_chunk("out0", (w_out, 0, 512))
        add_chunk("out1", (w_out, 512, 1024))
        for_heads = [h // 2 + 4 * (h % 2) for h in range(ATT_HEADS)]
        add_chunk("att_q", *[(w_in2, 64 * h, 64 * h + 64) for h in for_heads])
        add_chunk("att_kv", (w_in2, 512, 768))
        add_chunk("ml_q", (w_in2, 768, 1280))
        add_chunk("ml_k", (w_in2, 1280, 1792))
        add_chunk("ml_v", (w_in2, 1792, 2304))
        add_chunk("ml_if", (w_in2, 2816, 2824))
        add_chunk("ml_gate", (w_in2, 2304, 2816))
        add_chunk("out2_0", (w_out2, 0, 512))
        add_chunk("out2_1", (w_out2, 512, 1024))
        w_cq, w_ckv, w_co = (A[n].rearrange("a (k p) n -> p (a k) n", p=P) for n in ("w_cq_2", "w_ckv_2", "w_co_2"))
        add_chunk("cross_q", (w_cq, 0, 512))
        add_chunk("cross_k", (w_ckv, 0, 512))
        add_chunk("cross_v", (w_ckv, 512, 1024))
        add_chunk("cross_out", (w_co, 0, 1024))
        w_rg, w_re = (A[n].rearrange("a (k p) n -> p (a k) n", p=P) for n in ("w_router_group_2", "w_router_expert_2"))
        add_chunk("router", (w_rg, 0, GROUPS), (w_re, 0, EXPERTS))

        def slot(i):
            return cut(slots[:, i * NK * HALF:(i + 1) * NK * HALF], NK)

        def fm_fills(tiles):
            return [(m, half, ringA if half == 0 else ringV) for m in range(tiles) for half in range(2)]

        def tm_fills():
            return [(i, ringA if i % 2 == 0 else ringV) for i in range(NT)]

        def turn_fills():
            return [(half, f, ringA if f % 2 == 0 else ringV) for half in range(2) for f in range(NK)]

        LIN = {"a": (GLA_DV, 0), "b": (HGRN_DV, GLA_HEADS * GLA_DV)}
        SB0 = GLA_HEADS * GLA_DV + HGRN_HEADS * HGRN_DV

        def lin_area():
            ar = Area()
            Q, K, G = cut(ar(2 * T), 2), cut(ar(2 * T), 2), cut(ar(2 * T), 2)
            V = cut(ar(NT * 512), NT)
            E = [cut(ar(T), NT), cut(ar(T), NT), O[:, :, SB0:SB0 + P]]
            Qe, Ke = [ar(T) for _ in range(2)], [ar(T) for _ in range(2)]
            S = cut(ar(2 * T), 2 * NT)
            return Q, K, G, V, E, Qe, Ke, S

        def level(x, n):
            return x.rearrange("p j (a n) -> p j a n", n=n)

        def sb_area():
            ar = Area()
            Q, K = cut(ar(2 * T), 2), cut(ar(2 * T), 2)
            V = cut(ar(NT * 256), NT)
            Z, L = ([cut(ar(4 * n * HALF), 4 * n) for n in (1, 2)] for _ in range(2))
            R = cut(masks.bitcast(F32), 2)
            return Q, K, V, Z, L, R

        SB_STEPS = [(h, c) for h in range(SB_HEADS) for c in range(2)]
        stick_weights = Word(sem("stick_weights_ready"))
        stick_sums_used = []

        def sb_order():
            for n in range(len(SB_STEPS) + 1):
                if n < len(SB_STEPS):
                    yield (*SB_STEPS[n], "logits")
                if n:
                    yield (*SB_STEPS[n - 1], "weights")

        def sb_blocks(c):
            n = 4 * c + 4
            first = lambda j: max(0, (j - 4 * c) * P)
            return [(n - 1 - j, j, first(j), first(j + 1)) for j in reversed(range(n))]

        def att_area():
            ar = Area()
            return (cut(ar(4 * T), 4), ar(T), cut(ar(NT * P), NT), [cut(ar(ATT_HEADS * 2 * P), ATT_HEADS) for _ in range(2)],
                    cut(ar(2 * ATT_HEADS * P), 2 * ATT_HEADS))

        def att_range(n):
            return P if n == 0 else 0

        def ml_area():
            ar = Area()
            QK = cut(ar(2 * ML_HEADS * T), 2 * ML_HEADS)
            VM = ar(NT * ML_HEADS * VA).rearrange("p (i h v) -> p i h v", i=NT, h=ML_HEADS)
            NMB, DM, QR, KW = ar(T), ar(T), ar(T), ar(T)
            C, HB = cut(ar(NT * VA), NT), cut(ar(NT * VA), NT)
            return QK, VM, NMB, DM, QR, KW, C, HB

        def cross_area():
            ar = Area()
            CQ = cut(ar(4 * T), 4)
            M2 = cut(ar(2 * D), 2)
            MT, CK = cut(ar(NK * MEM), NK), cut(ar(4 * MEM), 4)
            CV = cut(ar(2 * HALF), 2)
            S = [cut(ar(4 * MEM), 4) for _ in range(2)]
            PT = cut(ar(8 * P), 8)
            OT = cut(ar(4 * T), 4)
            return CQ, M2, MT, CK, CV, S, PT, OT

        TAIL = 3 * NK * HALF
        O_flat, HT_flat = O.rearrange("p i d -> p (i d)"), HT.rearrange("p k t -> p (k t)")

        def expert_weights(x):
            at = slots if x == 0 else work
            n = NK * HALF
            return cut(at[:, 0:n], NK), cut(at[:, n:2 * n], NK), cut(at[:, 2 * n:3 * n], DE // P)

        XG = [O_flat[:, 0:D], O_flat[:, D:2 * D]]
        XT = [cut(O_flat[:, 2 * D:3 * D], NK), cut(O_flat[:, 3 * D:4 * D], NK)]
        YO = [O_flat[:, 4 * D:5 * D], O_flat[:, 5 * D:6 * D]]
        SILU, HID = O_flat[:, 6 * D:6 * D + HALF], O_flat[:, 6 * D + HALF:7 * D]
        gates2 = col(2 * NT)
        lg_bias = col(GROUPS + EXPERTS)
        slot_id = ctx.enter_context(nc.sbuf_tensor("slot_id", [P, 2 * NT], U32))
        token_list = ctx.enter_context(nc.sbuf_tensor("token_list", [P, BLOCKS], U32))
        spare_map = ctx.enter_context(nc.sbuf_tensor("spare_map", [P, SPARE + 1], I32))
        index = [ctx.enter_context(nc.sbuf_tensor(f"index{x}", [P, 1], U32)) for x in range(3)]
        tail = work[:, TAIL:WORK]
        at_tail = [0]

        def temp(n):
            at_tail[0] += n
            assert at_tail[0] <= WORK - TAIL
            return tail[:, at_tail[0] - n:at_tail[0]]

        LG, OH1, OH2, EM, TMP, A2, AC, SM = (cut(temp(NT * n), NT) for n in
                                             (GROUPS + EXPERTS, EXPERTS, EXPERTS, EXPERTS, EXPERTS, EXPERTS, EXPERTS, EXPERTS))
        OHG, GT = cut(temp(NT * GROUPS), NT), cut(temp(NT * GROUPS), NT)
        AC9, CN, SPN, INC, KE = temp(EXPERTS), temp(EXPERTS), temp(EXPERTS), temp(EXPERTS), temp(EXPERTS)
        SPM = cut(temp(SPARE * EXPERTS), SPARE)
        R1, R2, R3, R4 = temp(NT), temp(NT), temp(NT), temp(NT)
        TOKF = temp(P)
        ZT = temp(P)
        tok_dram = scratch("token_of_slot", [SLOTS, 1])
        x3_dram, xn_dram = scratch("x3", [NT, P, D]), scratch("xn", [T, D])
        y_dram = scratch("y_of_slot", [BLOCKS, P, D])
        rows_gathered = [sem(f"rows_gathered{x}") for x in range(2)]
        weights_in = [[sem(f"expert_{n}_in{x}") for n in ("gate", "up", "down")] for x in range(2)]
        y_stored = [sem(f"y_stored{x}") for x in range(2)]
        (tokens_turned, tokens_ready, gate_full, up_full, silu_ready, hidden_ready, down0_full, down1_full,
         y0_out, y1_out, index_ready) = (sem(n) for n in (
             "tokens_turned", "tokens_ready", "gate_full", "up_full", "silu_ready", "hidden_ready", "down0_full",
             "down1_full", "y0_out", "y1_out", "index_ready"))
        (sp_rows, sp_weights, sp_turned, sp_ready, sp_gate, sp_up, sp_silu, sp_hidden, sp_down0, sp_down1, sp_y0, sp_y1,
         sp_stored, sp_over, sp_index, sp_passed) = (sem("spare_" + n) for n in (
             "rows", "weights", "turned", "ready", "gate_full", "up_full", "silu", "hidden", "down0", "down1", "y0", "y1",
             "stored", "over", "index", "passed"))
        pool_passed, spare_cleared = sem("pool_passed"), sem("spare_cleared")
        moe_over, final_ready = sem("moe_over"), sem("final_ready")
        scattered, tok_in = sem("tokens_scattered"), sem("token_list_in")
        combined = [sem(f"combine_rows{i}") for i in range(NT)]
        out_sem = [sem(f"out_stored{i}") for i in range(4)]
        YG = [work[:, i * D:(i + 1) * D] for i in range(16)]
        spare_count = lambda eng: eng.value_load(spare_map[0:1, SPARE:SPARE + 1], min_val=0, max_val=SPARE)
        FINAL_ROW = slots[:, 0:D]

        block = ctx.enter_context(nc.Block())

        @block.tensor
        def _(pe):
            loads = [0] * 3
            phases = [0]

            def hear(who):
                words[who, "pe"].hear(pe)

            def weights(name):
                n = chunk_of[name]
                pe.wait_ge(slot_full[n % 3], 16 * sum(len(chunks[m]) for m in range(n % 3, n + 1, 3)))
                return slot(n % 3)

            def used(name):
                chunk_over[name] = (ringA.filled, ringV.filled)

            def emptied():
                pe.wait_ge(ringA.free, ringA.filled)
                if ringV.filled:
                    pe.wait_ge(ringV.free, ringV.filled)

            def next_phase():
                emptied()
                phases[0] += 1
                pe.sem_inc(phase, 1)
                pe.wait_ge(phase, 4 * phases[0])

            def chain(bank, pairs):
                for n, (lhsT, rhs) in enumerate(pairs):
                    ins = pe.matmul(bank, lhsT, rhs, start=(n == 0), stop=(n == len(pairs) - 1))
                return ins

            def product_fm(name, cols, fills, at=0):
                w = weights(name)
                for m, half, ring in fills:
                    n = min(P, cols - m * P)
                    bank = ring.open(pe)[0:n, :]
                    ring.close(chain(bank, [(w[:, k, at + m * P:at + m * P + n], HT[:, k, half * HALF:(half + 1) * HALF])
                                            for k in range(NK)]))
                used(name)

            def product_tm(name, cols, fills, x=None, at=0):
                w = weights(name)
                x = HT if x is None else x
                for i, ring in fills:
                    bank = ring.open(pe)[:, 0:cols]
                    ring.close(chain(bank, [(x[:, k, i * P:(i + 1) * P], w[:, k, at:at + cols]) for k in range(NK)]))
                used(name)

            def turn(heard):
                ident = const("ident")
                for half, f, ring in turn_fills():
                    if heard and f == 0:
                        hear("dve")
                    bank = ring.open(pe)
                    for q in range(4):
                        ins = pe.transpose(bank[:, q * P:(q + 1) * P], O[:, 4 * half + q, f * P:(f + 1) * P], ident)
                    ring.close(ins)

            hear("dve")
            for n in range(4):
                w = weights(f"ada{n}")
                bank = ringV.open(pe)
                for m in range(4):
                    ins = chain(bank[:, m:m + 1], [(w[:, k, m * P:(m + 1) * P], cact[:, k:k + 1]) for k in range(NK)])
                ringV.close(ins)
                used(f"ada{n}")
            crep = cut(work[:, 0:NK * P], NK)
            for n in range(2):
                w = weights(f"ada{4 + n}")
                ringV.close(chain(ringV.open(pe), [(crep[:, k, :], w[:, k, :]) for k in range(NK)]))
                used(f"ada{4 + n}")
            turn(True)
            next_phase()

            def linear(name):
                dv, o0 = LIN[name]
                Q, K, G, V, E, Qe, Ke, S = lin_area()
                for pair in range(2):
                    hear("pool")
                    bank = ringV.open(pe)
                    for j in range(NT):
                        ins = pe.matmul(bank[:, 2 * j:2 * j + 2], Ke[1][:, j * P:(j + 1) * P], two_heads,
                                        start=True, stop=True)
                    ringV.close(ins)
                    for lvl in range(LEVELS):
                        hear("dve")
                        hear("pool")
                        q, k = Qe[lvl % 2], Ke[lvl % 2]
                        for j0 in range(0, NT, 4):
                            bank = ringV.open(pe)
                            for j in range(j0, j0 + 4):
                                ins = pe.matmul(bank[:, (j - j0) * P:(j - j0 + 1) * P], k[:, j * P:(j + 1) * P],
                                                q[:, j * P:(j + 1) * P], start=True, stop=True)
                            ringV.close(ins)
                    hear("pool")
                    for half in range(2):
                        bank = ringA.open(pe)
                        for j in range(4):
                            t = slice(half * HALF + j * P, half * HALF + (j + 1) * P)
                            ins = pe.transpose(bank[:, j * P:(j + 1) * P], Ke[0][:, t], const("ident"))
                        ringA.close(ins)
                    pe.wait_ge(ringA.free, ringA.filled)
                    KT, St = cut(Qe[1], NT), cut(Ke[1][:, 0:NT * dv], NT)
                    per = HALF // dv
                    for j0 in range(0, NT - 1, per):
                        bank = ringV.open(pe)
                        for j in range(j0, min(j0 + per, NT - 1)):
                            for hh in range(2):
                                v = V[:, j, (2 * pair + hh) * dv:(2 * pair + hh + 1) * dv]
                                ins = pe.matmul(bank[64 * hh:64 * hh + 64, (j - j0) * dv:(j - j0 + 1) * dv],
                                                KT[:, j, 64 * hh:64 * hh + 64], v, start=True, stop=True)
                        ringV.close(ins)
                    hear("dve")
                    for hh in range(2):
                        d = slice(64 * hh, 64 * hh + 64)
                        for j0 in range(0, NT, per):
                            bank = ringA.open(pe)
                            for j in range(j0, j0 + per):
                                to, t = bank[:, (j - j0) * dv:(j - j0 + 1) * dv], slice(j * P, (j + 1) * P)
                                v = V[:, j, (2 * pair + hh) * dv:(2 * pair + hh + 1) * dv]
                                ins = pe.matmul(to, S[:, 2 * j + hh, :], v, start=True, stop=(j == 0))
                                if j:
                                    ins = pe.matmul(to, Qe[0][d, t], St[d, j, :], start=False, stop=True)
                            ringA.close(ins)

            product_fm("a_qk", 512, fm_fills(4))
            product_tm("a_v", 512, tm_fills())
            product_fm("a_rank", RANK, fm_fills(1))
            emptied()
            Q, K, G, V, E, Qe, Ke, S = lin_area()
            for m in range(2):
                for half in range(2):
                    ringV.close(pe.matmul(ringV.open(pe), Ke[0][0:RANK, m * P:(m + 1) * P],
                                          Ke[1][0:RANK, half * HALF:(half + 1) * HALF], start=True, stop=True))
            emptied()
            linear("a")
            next_phase()
            product_fm("b_qf", 512, fm_fills(4))
            product_tm("b_v", 256, tm_fills())
            emptied()
            linear("b")
            next_phase()

            product_fm("c_qk", 512, fm_fills(4))
            product_tm("c_v", 256, tm_fills())
            emptied()
            Q, K, V, Z, L, R = sb_area()
            for h, c, part in sb_order():
                pair, d, z, l = h // 2, slice(64 * (h % 2), 64 * (h % 2) + 64), Z[c], L[c]
                if part == "logits":
                    for at, j, t0, above in sb_blocks(c):
                        bank = ringA.open(pe)
                        ringA.close(pe.matmul(bank[:, t0:HALF], K[d, pair, j * P:(j + 1) * P],
                                              Q[d, pair, c * HALF + t0:(c + 1) * HALF], start=True, stop=True))
                    continue
                for at, j, t0, above in sb_blocks(c):
                    hear("dve")
                    bank = ringV.open(pe)
                    ins = pe.matmul(bank[:, t0:HALF], const("negtri"), l[:, at, t0:HALF], start=True, stop=(at == 0))
                    if at:
                        hear("pool")
                        ins = pe.matmul(bank[:, above:HALF], const("negones"), R[:, len(stick_sums_used) % 2, above:HALF],
                                        start=False, stop=True)
                    ringV.close(ins)
                    if at:
                        stick_sums_used.append(ringV.filled)
                stick_weights.hear(pe)
                bank = ringA.open(pe)
                for tb in range(4):
                    n = 4 * c + 4
                    ins = chain(bank[:, tb * 64:tb * 64 + 64],
                                [(z[:, n - 1 - j, tb * P:(tb + 1) * P], V[:, j, h * 64:h * 64 + 64])
                                 for j in range(4 * c + tb + 1)])
                ringA.close(ins)
            next_phase()

            product_tm("a_gate", 512, [(i, ringA) for i in range(NT)])
            product_tm("bc_gate", 512, [(i, ringA) for i in range(NT)])
            hear("dve")
            emptied()
            turn(False)
            emptied()
            product_tm("out0", 512, [(i, ringV) for i in range(NT)])
            product_tm("out1", 512, [(i, ringV) for i in range(NT)])
            next_phase()

            turn(True)
            emptied()
            product_fm("att_q", 512, fm_fills(4))
            product_fm("att_kv", P, fm_fills(1))
            product_tm("att_kv", P, tm_fills(), at=P)
            emptied()
            QA, KA, VT, S, PT = att_area()
            for n in range(NT + 1):
                if n < NT:
                    o = att_range(n)
                    for kv in range(KV_HEADS):
                        d = slice(64 * kv, 64 * kv + 64)
                        for mm in range(2):
                            bank = ringV.open(pe)
                            for x in range(2):
                                ins = pe.matmul(bank[:, 256 * x + o:256 * x + 256], QA[d, 2 * mm + x, n * P:(n + 1) * P],
                                                KA[d, (n - 1) * P + o:(n + 1) * P], start=True, stop=True)
                            ringV.close(ins)
                if n:
                    b, o = n - 1, att_range(n - 1)
                    hear("dve")
                    turns = [(h, kb) for h in range(ATT_HEADS) for kb in range(o // P, 2)]
                    for at in range(0, len(turns), 4):
                        bank = ringA.open(pe)
                        for x, (h, kb) in enumerate(turns[at:at + 4]):
                            ins = pe.transpose(bank[:, x * P:(x + 1) * P], S[b % 2][:, h, kb * P:(kb + 1) * P],
                                               const("ident"))
                        ringA.close(ins)
                    pe.wait_ge(ringA.free, ringA.filled)
                    bank = ringV.open(pe)
                    for h in range(ATT_HEADS):
                        kv = h // 4
                        ins = chain(bank[:, h * 64:h * 64 + 64],
                                    [(PT[:, turns.index((h, kb)), :], VT[:, b - 1 + kb, kv * 64:kv * 64 + 64])
                                     for kb in range(o // P, 2)])
                    ringV.close(ins)
            next_phase()

            product_fm("ml_q", 512, [(m, half, ringV) for m in range(4) for half in range(2)])
            product_fm("ml_k", 512, [(m, half, ringV) for m in range(4) for half in range(2)])
            product_tm("ml_v", 512, [(i, ringA) for i in range(NT)])
            w = weights("ml_if")
            for x in range(2):
                for half in range(2):
                    ringV.close(chain(ringV.open(pe)[0:ML_HEADS, :],
                                      [(w[:, k, 4 * x:4 * x + 4], HT[:, k, half * HALF:(half + 1) * HALF]) for k in range(NK)]))
            used("ml_if")
            QK, VM, NMB, DM, QR, KW, C, HB = ml_area()
            MROW = gate_row
            hear("dve")
            bank = ringV.open(pe)
            for i in range(NT):
                for x, row in enumerate((KW, HB.rearrange("p a b -> p (a b)"), MROW)):
                    at = (3 * i + x) * ML_HEADS
                    ins = pe.transpose(bank[:, at:at + ML_HEADS], row[0:ML_HEADS, i * P:(i + 1) * P],
                                       const("ident", ML_HEADS)[:, 0:ML_HEADS])
            ringV.close(ins)
            emptied()
            for h in range(ML_HEADS):
                for half in range(2):
                    ringA.close(pe.matmul(ringA.open(pe), const("sel", ML_HEADS)[:, h * P:(h + 1) * P],
                                          MROW[0:ML_HEADS, half * HALF:(half + 1) * HALF], start=True, stop=True))
                for half in range(2):
                    bank = ringV.open(pe)
                    for j in range(4):
                        t = slice(half * HALF + j * P, half * HALF + (j + 1) * P)
                        ins = pe.matmul(bank[:, j * P:(j + 1) * P], QK[:, 4 + h, t], QK[:, h, t], start=True, stop=True)
                    ringV.close(ins)
                for half in range(2):
                    bank = ringV.open(pe)
                    for j in range(4):
                        t = slice(half * HALF + j * P, half * HALF + (j + 1) * P)
                        ins = pe.transpose(bank[:, j * P:(j + 1) * P], QK[:, 4 + h, t], const("ident"))
                    ringV.close(ins)
                pe.wait_ge(ringV.free, ringV.filled)
                for j in range(0, NT - 1, 2):
                    bank = ringV.open(pe)
                    for x in range(min(2, NT - 1 - j)):
                        ins = pe.matmul(bank[:, x * VA:(x + 1) * VA], cut(KW, NT)[:, j + x, :], VM[:, j + x, h, :],
                                        start=True, stop=True)
                    ringV.close(ins)
                hear("dve")
                for j in range(0, NT, 2):
                    bank = ringA.open(pe)
                    for x in range(2):
                        to = bank[:, x * VA:(x + 1) * VA]
                        t = slice((j + x) * P, (j + x + 1) * P)
                        ins = pe.matmul(to, DM[:, t], VM[:, j + x, h, :], start=True, stop=(j + x == 0))
                        if j + x:
                            ins = pe.matmul(to, QR[:, t], C[:, j + x, :], start=False, stop=True)
                    ringA.close(ins)
            next_phase()

            product_tm("ml_gate", 512, [(i, ringA) for i in range(NT)])
            hear("dve")
            emptied()
            turn(False)
            emptied()
            product_tm("out2_0", 512, [(i, ringV) for i in range(NT)])
            product_tm("out2_1", 512, [(i, ringV) for i in range(NT)])
            next_phase()

            CQ, M2, MT, CK, CV, S, PT, OT = cross_area()
            turn(True)
            hear("dve")
            for f in range(NK):
                bank = ringV.open(pe)
                for q in range(2):
                    ins = pe.transpose(bank[:, q * P:(q + 1) * P], M2[:, q, f * P:(f + 1) * P], const("ident"))
                ringV.close(ins)
            emptied()
            product_fm("cross_q", 512, fm_fills(4))
            w = weights("cross_k")
            for m in range(4):
                ringA.close(chain(ringA.open(pe)[:, 0:MEM], [(w[:, k, m * P:(m + 1) * P], MT[:, k, :]) for k in range(NK)]))
            used("cross_k")
            product_tm("cross_v", 512, [(i, ringA) for i in range(2)], x=MT)
            emptied()
            for n in range(NT + 1):
                if n < NT:
                    for x in range(2):
                        bank = ringV.open(pe)
                        for y in range(2):
                            h = 2 * x + y
                            ins = pe.matmul(bank[:, y * MEM:(y + 1) * MEM], CQ[:, h, n * P:(n + 1) * P], CK[:, h, :],
                                            start=True, stop=True)
                        ringV.close(ins)
                if n:
                    b = n - 1
                    hear("dve")
                    for x in range(2):
                        bank = ringA.open(pe)
                        for y in range(4):
                            h, m = 2 * x + y // 2, y % 2
                            ins = pe.transpose(bank[:, y * P:(y + 1) * P], S[b % 2][:, h, m * P:(m + 1) * P],
                                               const("ident"))
                        ringA.close(ins)
                    pe.wait_ge(ringA.free, ringA.filled)
                    bank = ringA.open(pe)
                    for h in range(4):
                        ins = chain(bank[:, h * P:(h + 1) * P],
                                    [(CV[:, m, h * P:(h + 1) * P], PT[:, 2 * h + m, :]) for m in range(2)])
                    ringA.close(ins)
            next_phase()
            n = chunk_of["cross_out"] % 3
            weights("cross_out")
            w = cut(slots[:, n * NK * HALF:(n + 1) * NK * HALF], 4)
            for half in range(2):
                for i in range(NT):
                    ringV.close(chain(ringV.open(pe), [(OT[:, k, i * P:(i + 1) * P], w[:, k, half * HALF:(half + 1) * HALF])
                                                       for k in range(4)]))
            used("cross_out")
            next_phase()

            turn(True)
            emptied()
            w = weights("router")
            bank = ringV.open(pe)
            for i in range(NT):
                n = GROUPS + EXPERTS
                ins = chain(bank[:, i * n:(i + 1) * n], [(HT[:, k, i * P:(i + 1) * P], w[:, k, 0:n]) for k in range(NK)])
            ringV.close(ins)
            used("router")
            hear("dve")
            bank = ringV.open(pe)
            for i in range(NT):
                to = bank[:, i * EXPERTS:(i + 1) * EXPERTS]
                ins = pe.matmul(to, const("strict"), A2[:, i, :], start=True, stop=(i == 0))
                if i:
                    ins = pe.matmul(to, const("ones"), AC[:, i, :], start=False, stop=True)
            ins = pe.matmul(bank[:, NT * EXPERTS:(NT + 1) * EXPERTS], const("ones"), AC9, start=True, stop=True)
            ringV.close(ins)
            hear("pool")
            ringV.close(pe.transpose(ringV.open(pe)[:, 0:BLOCKS], TOKF[0:BLOCKS, :], const("ident", BLOCKS)[:, 0:BLOCKS]))
            next_phase()

            A0, A1, V0, V1, V2, V3 = banks[0], banks[1], banks[4], banks[5], banks[6], banks[7]

            def turn_block(x, last):
                for half, bank in ((0, V1), (1, V2)):
                    for q in range(4):
                        f = 4 * half + q
                        ins = pe.transpose(bank[:, q * P:(q + 1) * P], XG[x][:, f * P:(f + 1) * P], const("ident"))
                ins.then_inc(last, 1)

            def hidden_products(w, bank, x, last):
                for f in range(DE // P):
                    ins = chain(bank[:, f * P:(f + 1) * P], [(w[:, k, f * P:(f + 1) * P], XT[x][:, k, :]) for k in range(NK)])
                ins.then_inc(last, 1)

            def down_products(w, last0, last1):
                for half, bank, last in ((0, A1, last0), (1, V3, last1)):
                    chain(bank, [(HID[:, f * P:(f + 1) * P], w[:, f, half * HALF:(half + 1) * HALF])
                                 for f in range(DE // P)]).then_inc(last, 1)

            pe.wait_ge(rows_gathered[0], 16)
            turn_block(0, tokens_turned)
            with pe.Fori(0, EXPERTS // 2) as it:
                for x in range(2):
                    wg, wu, wd = expert_weights(x)
                    pe.wait_ge(tokens_ready, it * 4 + 2 * (x + 1))
                    pe.wait_ge(weights_in[x][0], it * 16 + 16)
                    hidden_products(wg, A0, x, gate_full)
                    pe.wait_ge(weights_in[x][1], it * 16 + 16)
                    hidden_products(wu, V0, x, up_full)
                    pe.wait_ge(rows_gathered[1 - x], it * 16 + 16 * (x + 1))
                    turn_block(1 - x, tokens_turned)
                    pe.wait_ge(hidden_ready, it * 2 + x + 1)
                    pe.wait_ge(weights_in[x][2], it * 16 + 16)
                    pe.wait_ge(y0_out, it * 2 + x + 1)
                    pe.wait_ge(y1_out, it * 2 + x + 1)
                    down_products(wd, down0_full, down1_full)
            spare = spare_count(pe)
            with pe.If(spare > 0):
                with pe.Fori(0, spare) as s:
                    wg, wu, wd = expert_weights(0)
                    pe.wait_ge(sp_rows, s * 16 + 16)
                    turn_block(0, sp_turned)
                    pe.wait_ge(sp_ready, s * 2 + 2)
                    pe.wait_ge(sp_weights, s * 48 + 48)
                    hidden_products(wg, A0, 0, sp_gate)
                    hidden_products(wu, V0, 0, sp_up)
                    pe.wait_ge(sp_hidden, s + 1)
                    down_products(wd, sp_down0, sp_down1)
            pe.nop()

        @block.scalar
        def _(act):
            line = Line(act, act_own)
            phases = [0]

            def tell(who):
                words["act", who].tell(act)

            def hear(who):
                words[who, "act"].hear(act)

            def empty(fn):
                bank = ringA.take(act)
                line(fn(bank), ringA.free)

            def func(o, i, f, bias=0.0, scale=1.0, **more):
                return act.activation(o, i, f, bias=bias, scale=scale, **more)

            def do(*args, **more):
                line(func(*args, **more))

            def next_phase():
                phases[0] += 1
                act.sem_inc(phase, 1)
                act.wait_ge(phase, 4 * phases[0])

            def log_sigmoid_part(x, tmp):
                act.preload_act_table_set("natural_log_exp_and_others")
                do(tmp, x, ACT.Abs)
                do(tmp, tmp, ACT.Exp, scale=-1.0)
                do(tmp, tmp, ACT.Ln, bias=1.0)

            def squares(half, junk, scale=None):
                for i in range(4 * half, 4 * half + 4):
                    if i % 2 == 0 and scale is not None:
                        act.wait_ge(dma_in[i // 2], scale)
                    do(junk, O[:, i, :], ACT.Square, accum_out=ss[:, i:i + 1])
                tell("dve")
                hear("dve")
                do(rstd[:, 4 * half:4 * half + 4], rstd[:, 4 * half:4 * half + 4], ACT.Sqrt)
                tell("dve")

            def turned(scale=None, bias=None):
                for half, f, ring in turn_fills():
                    if ring is ringA:
                        to = HT[:, f, half * HALF:(half + 1) * HALF]
                        if scale is None:
                            empty(lambda b: func(to, b, ACT.Copy))
                        else:
                            empty(lambda b: func(to, b, ACT.Identity, scale=scale[:, f:f + 1],
                                                 bias=0.0 if bias is None else bias[:, f:f + 1]))

            with nc.allow_non_contiguous_dma(reason="columns of small weights"):
                k_cols = lambda n: A[n].rearrange("a (k p) -> p (a k)", p=P)
                small_loads = [
                    (ccol, k_cols("c")),
                    (bcol, A["b_ada"][:, 0:2 * D].rearrange("a (k p) -> p (a k)", p=P)),
                    (gate_row, A["b_ada"][:, 2 * D:3 * D].partition_broadcast(P)),
                    (bgate, k_cols("b_gla_gate")),
                    (gla_w, A["gla_norm_w"].partition_broadcast(P)),
                    (hgrn_w, A["hgrn_norm_w"].partition_broadcast(P)),
                    (cst, A["consts"]),
                    (masks, A["masks"]),
                    (sinks, A["att_sinks_2"].partition_broadcast(P)),
                    (b_if[0:ML_HEADS, :], A["b_gates_2"].rearrange("a (c p) -> p (a c)", p=ML_HEADS)),
                    (conv_b, k_cols("conv_b_2")),
                    (lg_bias[:, 0:GROUPS], A["b_router_group_2"].partition_broadcast(P)),
                    (lg_bias[:, GROUPS:], A["b_router_expert_2"].partition_broadcast(P)),
                    (conv_w, A["conv_w_2"].rearrange("a t (k p) -> p (a t k)", p=P)),
                ] + [(normcols[n], k_cols(n)) for n in normcols]
                for to, of in small_loads:
                    act.dma_start(to, of).then_inc(loaded, 16)
            act.wait_ge(loaded, 16 * len(small_loads))
            do(cact, ccol, ACT.Silu)
            tell("dve")
            junk = work[:, 1024:2048]
            hear("dve")
            squares(0, junk, 16)
            squares(1, junk, 16)
            hear("dve")
            turned(mod[:, 8:16], mod[:, 0:8])
            next_phase()

            def linear(name):
                dv, o0 = LIN[name]
                Q, K, G, V, E, Qe, Ke, S = lin_area()
                for pair in range(2):
                    B = G[:, pair]
                    for lvl in range(LEVELS):
                        hear("pool")
                        do(E[lvl % 3], E[lvl % 3], ACT.Abs)
                        do(E[lvl % 3], E[lvl % 3], ACT.Exp, scale=-1.0)
                        tell("dve")
                        tell("pool")
                    hear("pool")
                    do(E[0], E[0], ACT.Exp)
                    do(E[1], cut(B, NT), ACT.Exp)
                    do(decay, cut(B, NT)[:, :, P - 1], ACT.Exp)
                    tell("dve")
                    tell("pool")
                    for half in range(2):
                        if half == 0:
                            hear("dve")
                        to = Qe[1][:, half * HALF:(half + 1) * HALF]
                        empty(lambda b: func(to, b, ACT.Copy))
                    per = HALF // dv
                    for hh in range(2):
                        for j0 in range(0, NT, per):
                            at = o0 + (2 * pair + hh) * dv
                            empty(lambda b: func(O[:, j0:j0 + per, at:at + dv], cut(b, per), ACT.Copy))
                    tell("dve")
                    tell("pool")

            Q, K, G, V, E, Qe, Ke, S = lin_area()
            for m, half, ring in fm_fills(4):
                if ring is ringA:
                    t = slice(half * HALF, (half + 1) * HALF)
                    if m < 2:
                        empty(lambda b: func(Q[:, m, t], b, ACT.Copy, scale=DK ** -0.5))
                    else:
                        empty(lambda b: func(K[:, m - 2, t], b, ACT.Copy))
            for i, ring in tm_fills():
                if ring is ringA:
                    empty(lambda b: func(V[:, i, :], b, ACT.Copy))
            act.dma_start(Ke[0][0:RANK, 0:2 * P], A["w_gla_gate2"].rearrange("a r n -> (a r) n")).then_inc(loaded, 16)
            act.wait_ge(loaded, 16 * (len(small_loads) + 1))
            empty(lambda b: func(Ke[1][0:RANK, 0:HALF], b[0:RANK, :], ACT.Copy))
            hear("dve")
            for pair in range(2):
                log_sigmoid_part(cut(G[:, pair], NT), E[pair])
            tell("dve")
            linear("a")
            next_phase()

            for m, half, ring in fm_fills(4):
                if ring is ringA:
                    t = slice(half * HALF, (half + 1) * HALF)
                    if m < 2:
                        empty(lambda b: func(Q[:, m, t], b, ACT.Silu))
                    else:
                        empty(lambda b: func(G[:, m - 2, t], b, ACT.Copy))
            for i, ring in tm_fills():
                if ring is ringA:
                    empty(lambda b: func(V[:, i, 0:256], b[:, 0:256], ACT.Copy))
            hear("dve")
            for m in range(2):
                do(Q[:, m, HALF:T], Q[:, m, HALF:T], ACT.Silu)
            for m in range(2):
                do(K[:, m], G[:, m], ACT.Sigmoid, scale=-1.0)
            for m in range(2):
                log_sigmoid_part(cut(G[:, m], NT), E[m])
            tell("dve")
            linear("b")
            next_phase()

            Q, K, V, Z, L, R = sb_area()
            for m, half, ring in fm_fills(4):
                if ring is ringA:
                    t = slice(half * HALF, (half + 1) * HALF)
                    to, s = (Q[:, m, t], DK ** -0.5) if m < 2 else (K[:, m - 2, t], 1.0)
                    empty(lambda b: func(to, b, ACT.Copy, scale=s))
            for i, ring in tm_fills():
                if ring is ringA:
                    empty(lambda b: func(V[:, i, :], b[:, 0:256], ACT.Copy))
            act.preload_act_table_set("natural_log_exp_and_others")
            for h, c, part in sb_order():
                blocks, z, l = sb_blocks(c), Z[c], L[c]
                if part == "logits":
                    for n in range(len(blocks) + 2):
                        if n < len(blocks):
                            at, _, t0, _ = blocks[n]
                            empty(lambda b: func(z[:, at, t0:HALF], b[:, t0:HALF], ACT.Copy))
                            tell("dve")
                        if n >= 2:
                            at, _, t0, _ = blocks[n - 2]
                            hear("dve")
                            do(l[:, at, t0:HALF], l[:, at, t0:HALF], ACT.Exp, scale=-1.0)
                            do(l[:, at, t0:HALF], l[:, at, t0:HALF], ACT.Ln, bias=1.0)
                            tell("dve")
                    continue
                for at, j, t0, above in blocks:
                    hear("dve")
                    do(z[:, at, t0:HALF], z[:, at, t0:HALF], ACT.Exp)
                    tell("dve")
                empty(lambda b: func(O[:, 4 * c:4 * c + 4, SB0 + h * 64:SB0 + h * 64 + 64],
                                     cut(b[:, 0:256], 4), ACT.Copy))
            next_phase()

            hear("dve")
            do(rstd[:, :], rstd[:, :], ACT.Sqrt)
            tell("dve")
            for n in range(2 * NT):
                if n >= 2:
                    hear("dve")
                g = work[:, (n % 2) * HALF:(n % 2 + 1) * HALF]
                empty(lambda b: func(g, b, ACT.Silu))
                tell("dve")
            turned()
            hear("dve")
            squares(0, work[:, 0:T])
            squares(1, work[:, 0:T])
            next_phase()

            squares(0, work[:, 0:T])
            squares(1, work[:, 0:T])
            turned(normcols["norm_mix_2"])
            QA, KA, VT, S, PT = att_area()
            for m, half, ring in fm_fills(4):
                if ring is ringA:
                    empty(lambda b: func(QA[:, m, half * HALF:(half + 1) * HALF], b, ACT.Copy, scale=DK ** -0.5))
            empty(lambda b: func(KA[:, 0:HALF], b, ACT.Copy))
            for i, ring in tm_fills():
                if ring is ringA:
                    empty(lambda b: func(VT[:, i, :], b[:, 0:P], ACT.Copy))
            for n in range(NT + 1):
                if n < NT:
                    o = att_range(n)
                    m = slice(8 * (n % 2), 8 * (n % 2) + 8)
                    hear("dve")
                    do(S[n % 2][:, :, o:2 * P], S[n % 2][:, :, o:2 * P], ACT.Exp)
                    do(es[:, m], es[:, m], ACT.Exp)
                    tell("dve")
                if n:
                    turns = (2 if n > 1 else 1) * ATT_HEADS
                    for at in range(0, turns, 4):
                        empty(lambda b: func(PT[:, at:at + 4, :], cut(b, 4), ACT.Copy))
            next_phase()

            QK, VM, NMB, DM, QR, KW, C, HB = ml_area()
            for i in range(NT):
                empty(lambda b: func(VM[:, i, :, 0:ML_D], cut(b, ML_HEADS), ACT.Copy))
            for m in range(2 * ML_HEADS):
                hear("dve")
                do(QK[:, m], QK[:, m], ACT.Silu)
                if m < ML_HEADS:
                    do(QK[:, m], QK[:, m], ACT.Copy, scale=ML_D ** -0.5)
            hear("dve")
            log_sigmoid_part(QR[0:ML_HEADS, :], DM[0:ML_HEADS, :])
            tell("dve")
            hear("dve")
            do(cut(expm, NT), acm.rearrange("p (i x h) -> p i x h", i=NT, x=3)[:, :, 1, :], ACT.Exp, scale=-1.0)
            for h in range(ML_HEADS):
                for half in range(2):
                    empty(lambda b: func(NMB[:, half * HALF:(half + 1) * HALF], b, ACT.Copy, scale=-1.0))
                tell("dve")
                hear("dve")
                do(DM, DM, ACT.Exp)
                do(wcol, wcol, ACT.Exp)
                do(dcol, dcol, ACT.Exp)
                do(QR[:, P:T], QR[:, P:T], ACT.Exp)
                tell("dve")
                for j in range(0, NT, 2):
                    empty(lambda b: func(HB[:, j:j + 2, :], cut(b[:, 0:2 * VA], 2), ACT.Copy))
                tell("dve")
                hear("dve")
            next_phase()

            for n in range(NT):
                if n >= 2:
                    hear("dve")
                g = work[:, (n % 2) * HALF:(n % 2 + 1) * HALF]
                empty(lambda b: func(g, b, ACT.Sigmoid))
                tell("dve")
            hear("dve")
            do(rstd[:, 0:5 * NT], rstd[:, 0:5 * NT], ACT.Sqrt)
            tell("dve")
            turned()
            next_phase()

            CQ, M2, MT, CK, CV, S, PT, OT = cross_area()
            squares(0, OT.rearrange("p a b -> p (a b)")[:, 0:D])
            squares(1, OT.rearrange("p a b -> p (a b)")[:, 0:D])
            turned(normcols["norm_cross_2"])
            act.wait_ge(row_in, 64)
            for i in range(2):
                do(OT[:, i, :], M2[:, i, :], ACT.Square, accum_out=ss[:, 8 + i:9 + i])
            tell("dve")
            hear("dve")
            do(rstd[:, 8:10], rstd[:, 8:10], ACT.Sqrt)
            tell("dve")
            for m, half, ring in fm_fills(4):
                if ring is ringA:
                    empty(lambda b: func(CQ[:, m, half * HALF:(half + 1) * HALF], b, ACT.Copy, scale=P ** -0.5))
            for m in range(4):
                empty(lambda b: func(CK[:, m, :], b[:, 0:MEM], ACT.Copy))
            for i in range(2):
                empty(lambda b: func(CV[:, i, :], b, ACT.Copy))
            for n in range(NT + 1):
                if n < NT:
                    hear("dve")
                    do(S[n % 2], S[n % 2], ACT.Exp)
                    tell("dve")
                if n:
                    for x in range(2):
                        empty(lambda b: func(PT[:, 4 * x:4 * x + 4, :], cut(b, 4), ACT.Copy))
                    empty(lambda b: func(OT[:, :, (n - 1) * P:n * P], cut(b, 4), ACT.Copy))
            next_phase()
            next_phase()

            squares(0, tail[:, 0:D])
            squares(1, tail[:, 0:D])
            turned(normcols["norm_ffn_2"])
            hear("dve")
            do(GT, GT, ACT.Exp)
            do(R3, R3, ACT.Exp)
            tell("dve")
            next_phase()

            A0, A1 = banks[0], banks[1]
            with act.Fori(0, EXPERTS // 2) as it:
                for x in range(2):
                    act.wait_ge(gate_full, it * 2 + x + 1)
                    func(SILU, A0, ACT.Silu).then_inc(silu_ready, 1)
                    act.wait_ge(down0_full, it * 2 + x + 1)
                    act.wait_ge(y_stored[x], it * 16 + 16)
                    func(YO[x][:, 0:HALF], A1, ACT.Copy).then_inc(y0_out, 1)
                    act.wait_ge(y0_out, it * 2 + x + 2)
                    act.wait_ge(y1_out, it * 2 + x + 2)
                    act.dma_start(y_dram[bass.ds(it * 2 + x, 1)].rearrange("a p d -> p (a d)"), YO[x])\
                        .then_inc(y_stored[x], 16)
            for x in range(2):
                act.wait_ge(y_stored[x], 16 * (EXPERTS // 2 + 1))
            spare = spare_count(act)
            act.sem_inc(sp_over, 1)
            with act.If(spare > 0):
                with act.Fori(0, spare) as s:
                    act.wait_ge(sp_gate, s + 1)
                    func(SILU, A0, ACT.Silu).then_inc(sp_silu, 1)
                    act.wait_ge(sp_down0, s + 1)
                    func(YO[0][:, 0:HALF], A1, ACT.Copy).then_inc(sp_y0, 1)
                    act.wait_ge(sp_y0, s + 1)
                    act.wait_ge(sp_y1, s + 1)
                    act.dma_start(y_dram[bass.ds(s + EXPERTS, 1)].rearrange("a p d -> p (a d)"), YO[0])\
                        .then_inc(sp_stored, 16)
                    act.wait_ge(sp_stored, s * 16 + 16)
                    act.sem_inc(sp_over, 1)
            act.sem_inc(moe_over, 1)
            for i in range(NT):
                hear("dve")
                do(YG[2 * i], O[:, i, :], ACT.Square, accum_out=ss[:, i:i + 1])
                tell("dve")
                hear("dve")
                do(rstd[:, i:i + 1], rstd[:, i:i + 1], ACT.Sqrt)
                tell("dve")

        @block.vector
        def _(dve):
            line = Line(dve, dve_own)
            phases = [0]

            def tell(who):
                words["dve", who].tell(dve)

            def hear(who):
                words[who, "dve"].hear(dve)

            def empty(fn):
                bank = ringV.take(dve)
                line(fn(bank), ringV.free)

            def copy(o, i):
                line(dve.tensor_copy(o, i))

            def tt(o, a, b, op):
                line(dve.tensor_tensor(o, a, b, op))

            def ts(o, a, s1, s2, op0, *op1):
                line(dve.tensor_scalar(o, a, s1, s2, op0, *op1))

            def stt(o, a, s, b, op0, op1):
                line(dve.scalar_tensor_tensor(out=o, in0=a, scalar=s, in1=b, op0=op0, op1=op1))

            def bcast(ap, shape):
                return ap.to_broadcast(shape)

            def next_phase():
                phases[0] += 1
                dve.sem_inc(phase, 1)
                dve.wait_ge(phase, 4 * phases[0])

            def inverse_root(half, scale=1.0 / D):
                hear("act")
                r = rstd[:, 4 * half:4 * half + 4]
                ts(r, ss[:, 4 * half:4 * half + 4], scale, EPS, ALU.mult, ALU.add)
                line(dve.reciprocal(r, r))
                tell("act")
                hear("act")

            def normed(told=True):
                for half in range(2):
                    inverse_root(half)
                    for i in range(4 * half, 4 * half + 4):
                        ts(O[:, i, :], O[:, i, :], rstd[:, i:i + 1], None, ALU.mult)
                    if told:
                        tell("pe")

            def turned(scale=None, bias=None):
                for half, f, ring in turn_fills():
                    if ring is ringV:
                        to = HT[:, f, half * HALF:(half + 1) * HALF]
                        if scale is None:
                            empty(lambda b: dve.tensor_copy(to, b))
                        elif bias is None:
                            empty(lambda b: dve.tensor_scalar(to, b, scale[:, f:f + 1], None, ALU.mult))
                        else:
                            empty(lambda b: dve.tensor_scalar(to, b, scale[:, f:f + 1], bias[:, f:f + 1],
                                                              ALU.mult, ALU.add))

            line(dve.memset(one, 1.0))
            line(dve.memset(zero, 0.0))
            line(dve.memset(two_heads, 0.0))
            for hh in range(2):
                line(dve.memset(two_heads[64 * hh:64 * hh + 64, hh:hh + 1], 1.0))
            line(dve.memset(ss[:, :], 0.0))
            line(dve.memset(rstd[:, :], 1.0))
            hear("act")
            crep = cut(work[:, 0:NK * P], NK)
            copy(crep, bcast(cact.unsqueeze(2), [P, NK, P]))
            tell("pe")
            tell("act")
            normed()
            for n in range(4):
                c = slice(4 * n, 4 * n + 4)
                empty(lambda b: dve.tensor_tensor(mod[:, c], b[:, 0:4], bcol[:, c], ALU.add))
            ts(mod[:, 8:16], mod[:, 8:16], 1.0, None, ALU.add)
            for n in range(2):
                g = gate_row[:, n * HALF:(n + 1) * HALF]
                empty(lambda b: dve.tensor_tensor(g, g, b, ALU.add))
            tell("act")
            turned(mod[:, 8:16], mod[:, 0:8])
            next_phase()

            def linear(name):
                dv, o0 = LIN[name]
                Q, K, G, V, E, Qe, Ke, S = lin_area()
                for pair in range(2):
                    B = G[:, pair]
                    for j in range(NT):
                        g = B[:, j * P:(j + 1) * P]
                        line(dve.tensor_tensor_scan(g, bcast(one, [P, P]), g, 0.0, ALU.mult, ALU.add))
                    tell("pool")
                    if pair:
                        hear("act")

                    def itself():
                        empty(lambda b: dve.tensor_tensor(S, bcast(const("ident").unsqueeze(1), [P, 2 * NT, P]),
                                                          bcast(b[:, 0:2 * NT].unsqueeze(2), [P, 2 * NT, P]), ALU.mult))

                    def scores(lvl):
                        n = P >> lvl
                        m = cut(cut(masks, LEVELS + 1)[:, lvl, :], P // n)[:, :, n // 2:n]
                        for half in range(2):
                            s = S[:, 8 * half:8 * half + 8, :].rearrange("p j (a n) -> p j a n", n=n)[:, :, :, n // 2:n]
                            empty(lambda b: dve.copy_predicated(
                                s, bcast(m.unsqueeze(1), [P, NT, P // n, n // 2]),
                                b.rearrange("p (j a h) -> p j a h", j=NT, h=n // 2)))

                    for x in range(2):
                        for hh in range(2):
                            other = Qe[x].rearrange("p (j c h) -> p j c h", j=NT, c=2)[64 * hh:64 * hh + 64, :, 1 - hh]
                            line(dve.memset(other, 0.0))
                    itself()
                    for lvl in range(LEVELS):
                        n = P >> lvl
                        hear("act")
                        for hh in range(2):
                            d = slice(64 * hh, 64 * hh + 64)
                            to = Qe[lvl % 2].rearrange("p (j c a h) -> p j c a h", j=NT, c=2, h=n // 2)[d, :, hh]
                            q, e = (level(x[d], n)[:, :, :, n // 2:n] for x in (cut(Q[:, pair], NT), E[lvl % 3]))
                            tt(to, q, e, ALU.mult)
                        tell("pe")
                        tell("pool")
                        if lvl >= 1:
                            scores(lvl - 1)
                    scores(LEVELS - 1)
                    tell("pool")
                    hear("act")
                    tt(cut(Qe[0], NT), cut(Q[:, pair], NT), E[1], ALU.mult)
                    tell("act")
                    St = cut(Ke[1][:, 0:NT * dv], NT)
                    line(dve.memset(St[:, 0, :], 0.0))
                    per = HALF // dv
                    for j0 in range(0, NT - 1, per):
                        bank = ringV.take(dve)
                        n = min(j0 + per, NT - 1)
                        for j in range(j0, n):
                            ins = dve.scalar_tensor_tensor(
                                out=St[:, j + 1, :], in0=St[:, j, :], scalar=decay[:, j:j + 1],
                                in1=bank[:, (j - j0) * dv:(j - j0 + 1) * dv], op0=ALU.mult, op1=ALU.add)
                            line(ins, ringV.free if j == n - 1 else None)
                    tell("pe")
                hear("act")

            def copies(fills, to):
                for *at, ring in fills:
                    if ring is ringV:
                        dst, n = to(*at)
                        empty(lambda b: dve.tensor_copy(dst, b[:, 0:n]))

            Q, K, G, V, E, Qe, Ke, S = lin_area()
            for m, half, ring in fm_fills(4):
                if ring is ringV:
                    t = slice(half * HALF, (half + 1) * HALF)
                    if m < 2:
                        empty(lambda b: dve.tensor_scalar(Q[:, m, t], b, DK ** -0.5, None, ALU.mult))
                    else:
                        empty(lambda b: dve.tensor_copy(K[:, m - 2, t], b))
            copies(tm_fills(), lambda i: (V[:, i, :], 512))
            empty(lambda b: dve.tensor_copy(Ke[1][0:RANK, HALF:T], b[0:RANK, :]))
            for m in range(2):
                for half in range(2):
                    t = slice(half * HALF, (half + 1) * HALF)
                    empty(lambda b: dve.tensor_scalar(G[:, m, t], b, bgate[:, m:m + 1], None, ALU.add))
            tell("act")
            hear("act")
            for m in range(2):
                g = cut(G[:, m], NT)
                stt(g, g, 0.0, E[m], ALU.min, ALU.subtract)
                ts(G[:, m], G[:, m], 1.0 / TAU, None, ALU.mult)
            linear("a")
            next_phase()

            for m, half, ring in fm_fills(4):
                if ring is ringV:
                    t = slice(half * HALF, (half + 1) * HALF)
                    to = Q[:, m, t] if m < 2 else G[:, m - 2, t]
                    empty(lambda b: dve.tensor_copy(to, b))
            copies(tm_fills(), lambda i: (V[:, i, 0:256], 256))
            tell("act")
            hear("act")
            for m in range(2):
                g = cut(G[:, m], NT)
                stt(g, g, 0.0, E[m], ALU.min, ALU.subtract)
            linear("b")
            next_phase()

            Q, K, V, Z, L, R = sb_area()
            for m, half, ring in fm_fills(4):
                if ring is ringV:
                    t = slice(half * HALF, (half + 1) * HALF)
                    to, s = (Q[:, m, t], DK ** -0.5) if m < 2 else (K[:, m - 2, t], 1.0)
                    empty(lambda b: dve.tensor_scalar(to, b, s, None, ALU.mult))
            copies(tm_fills(), lambda i: (V[:, i, :], 256))
            strict = const("strict")
            for h, c, part in sb_order():
                blocks, z, l = sb_blocks(c), Z[c], L[c]
                if part == "logits":
                    for n in range(len(blocks) + 2):
                        if n < len(blocks):
                            at, _, t0, _ = blocks[n]
                            hear("act")
                            stt(l[:, at, t0:HALF], z[:, at, t0:HALF], -1.0, z[:, at, t0:HALF], ALU.mult, ALU.max)
                            tell("act")
                        if n >= 2:
                            at, j, t0, _ = blocks[n - 2]
                            hear("act")
                            stt(l[:, at, t0:HALF], z[:, at, t0:HALF], 0.0, l[:, at, t0:HALF], ALU.max, ALU.add)
                            if j >= 4 * c:
                                tt(l[:, at, t0:t0 + P], l[:, at, t0:t0 + P], strict, ALU.mult)
                            tell("pe")
                            tell("pool")
                    continue
                for at, j, t0, above in blocks:
                    zb = z[:, at, t0:HALF]
                    empty(lambda b: dve.tensor_tensor(zb, zb, b[:, t0:HALF], ALU.add))
                    tell("act")
                for at, j, t0, above in blocks:
                    hear("act")
                    if j >= 4 * c:
                        tt(z[:, at, t0:t0 + P], z[:, at, t0:t0 + P], strict, ALU.mult)
                stick_weights.tell(dve)
            next_phase()

            ssh, rh = cut(ss, NT), cut(rstd, NT)
            sq = work[:, 2 * HALF:2 * HALF + SB0]
            NG = GLA_HEADS * GLA_DV
            for i in range(NT):
                o = O[:, i, 0:SB0]
                tt(sq, o, o, ALU.mult)
                line(dve.tensor_reduce(ssh[:, i, 0:4], cut(sq[:, 0:NG], 4), AX_X, ALU.add))
                line(dve.tensor_reduce(ssh[:, i, 4:8], cut(sq[:, NG:SB0], 4), AX_X, ALU.add))
            ts(rh[:, :, 0:4], ssh[:, :, 0:4], 1.0 / GLA_DV, EPS, ALU.mult, ALU.add)
            ts(rh[:, :, 4:8], ssh[:, :, 4:8], 1.0 / HGRN_DV, EPS, ALU.mult, ALU.add)
            line(dve.reciprocal(rstd[:, :], rstd[:, :]))
            tell("act")
            hear("act")
            for i in range(NT):
                for at, n, dv, w in ((0, 0, GLA_DV, gla_w), (NG, 4, HGRN_DV, hgrn_w)):
                    o = cut(O[:, i, at:at + 4 * dv], 4)
                    tt(o, o, bcast(rh[:, i, n:n + 4].unsqueeze(2), [P, 4, dv]), ALU.mult)
                    tt(o, o, bcast(w.unsqueeze(1), [P, 4, dv]), ALU.mult)
            for n in range(2 * NT):
                hear("act")
                o = O[:, n % NT, (n // NT) * HALF:(n // NT + 1) * HALF]
                tt(o, o, work[:, (n % 2) * HALF:(n % 2 + 1) * HALF], ALU.mult)
                if n < 2 * NT - 2:
                    tell("act")
            tell("pe")
            turned()
            X = cut(work[:, 2 * T:2 * T + NT * D], NT)
            for n in range(2):
                for i in range(NT):
                    if n == 0 and i % 2 == 0:
                        dve.wait_ge(dma_in[i // 2], 32)
                    c = slice(n * HALF, (n + 1) * HALF)
                    empty(lambda b: dve.tensor_tensor(O[:, i, c], b, gate_row[:, c], ALU.mult))
                    tt(O[:, i, c], O[:, i, c], X[:, i, c], ALU.add)
            tell("act")
            normed(False)
            dve.wait_ge(row_in, 16)
            for i in range(NT):
                tt(O[:, i, :], O[:, i, :], work[:, 10 * T:11 * T], ALU.mult)
            tell("pool")
            next_phase()

            normed()
            turned(normcols["norm_mix_2"])
            QA, KA, VT, S, PT = att_area()
            for m, half, ring in fm_fills(4):
                if ring is ringV:
                    empty(lambda b: dve.tensor_scalar(QA[:, m, half * HALF:(half + 1) * HALF], b, DK ** -0.5, None, ALU.mult))
            empty(lambda b: dve.tensor_copy(KA[:, HALF:T], b))
            copies(tm_fills(), lambda i: (VT[:, i, :], P))
            for n in range(NT + 1):
                if n < NT:
                    o, s = att_range(n), S[n % 2]
                    m = slice(8 * (n % 2), 8 * (n % 2) + 8)
                    for kv in range(KV_HEADS):
                        for mm in range(2):
                            bank = ringV.take(dve)
                            for x in range(2):
                                h = 4 * kv + 2 * mm + x
                                line(dve.scalar_tensor_tensor(
                                    out=s[:, h, o:2 * P], in0=const("dist")[:, o:2 * P],
                                    scalar=2.0 ** (-8.0 * (h + 1) / ATT_HEADS), in1=bank[:, 256 * x + o:256 * x + 256],
                                    op0=ALU.mult, op1=ALU.add), ringV.free if x else None)
                    line(dve.tensor_reduce(mx[:, m], s[:, :, o:2 * P], AX_X, ALU.max))
                    tt(mx[:, m], mx[:, m], sinks, ALU.max)
                    tt(es[:, m], sinks, mx[:, m], ALU.subtract)
                    tt(s[:, :, o:2 * P], s[:, :, o:2 * P], bcast(mx[:, m].unsqueeze(2), [P, ATT_HEADS, 2 * P - o]),
                       ALU.subtract)
                    tell("act")
                if n:
                    o, s = att_range(n - 1), S[(n - 1) % 2]
                    m = slice(8 * ((n - 1) % 2), 8 * ((n - 1) % 2) + 8)
                    hear("act")
                    tell("pe")
                    line(dve.tensor_reduce(rden[:, m], s[:, :, o:2 * P], AX_X, ALU.add))
                    tt(rden[:, m], rden[:, m], es[:, m], ALU.add)
                    line(dve.reciprocal(rden[:, m], rden[:, m]))
                    empty(lambda b: dve.tensor_tensor(cut(O[:, n - 1, 0:512], ATT_HEADS), cut(b, ATT_HEADS),
                                                      bcast(rden[:, m].unsqueeze(2), [P, ATT_HEADS, 64]), ALU.mult))
            next_phase()

            QK, VM, NMB, DM, QR, KW, C, HB = ml_area()
            raw = [work[:, 12320:12320 + T + 3], work[:, 13376:13376 + T + 3]]
            cw = cut(conv_w, TAPS)
            line(dve.memset(VM[:, :, :, ML_D:VA], 1.0))
            for m in range(2 * ML_HEADS):
                r = raw[m % 2]
                line(dve.memset(r[:, 0:TAPS - 1], 0.0))
                for half in range(2):
                    empty(lambda b: dve.tensor_copy(r[:, TAPS - 1 + half * HALF:TAPS - 1 + (half + 1) * HALF], b))
                ts(QK[:, m], r[:, TAPS - 1:TAPS - 1 + T], cw[:, TAPS - 1, m:m + 1], conv_b[:, m:m + 1], ALU.mult, ALU.add)
                for k in range(TAPS - 1):
                    stt(QK[:, m], r[:, k:k + T], cw[:, k, m:m + 1], QK[:, m], ALU.mult, ALU.add)
                tell("act")
            heads = slice(0, ML_HEADS)
            for row, x in ((KW, 0), (QR, 1)):
                for half in range(2):
                    empty(lambda b: dve.tensor_scalar(row[heads, half * HALF:(half + 1) * HALF], b[heads, :],
                                                      b_if[heads, x:x + 1], None, ALU.add))
            tell("act")
            hear("act")
            F, a, MROW, MT_ROW = QR[heads, :], KW[heads, :], gate_row[heads, :], HB.rearrange("p a b -> p (a b)")[heads, 0:T]
            stt(F, F, 0.0, DM[heads, :], ALU.min, ALU.subtract)
            line(dve.tensor_tensor_scan(F, bcast(one[heads, :], [ML_HEADS, T]), F, 0.0, ALU.mult, ALU.add))
            tt(a, a, F, ALU.subtract)
            line(dve.tensor_tensor_scan(MROW, a, bcast(zero[heads, :], [ML_HEADS, T]), 0.0, ALU.max, ALU.add))
            tt(MT_ROW, MROW, F, ALU.add)
            tell("pe")
            empty(lambda b: dve.tensor_copy(acm, b[:, 0:NT * 3 * ML_HEADS]))
            tell("act")
            acm4 = acm.rearrange("p (i x h) -> p i x h", i=NT, x=3)
            nmb, dm, qr, kw = cut(NMB, NT), cut(DM, NT), cut(QR, NT), cut(KW, NT)
            causal = const("causal")
            for h in range(ML_HEADS):
                hear("act")
                a_h = acm4[:, :, 0, h]
                tt(dm, nmb, bcast(a_h.unsqueeze(2), [P, NT, P]), ALU.add)
                ts(DM, DM, 0.0, None, ALU.min)
                tt(wcol, a_h, nmb[:, :, P - 1], ALU.add)
                line(dve.memset(dcol[:, 0:1], 0.0))
                tt(dcol[:, 1:NT], nmb[:, 1:NT, P - 1], nmb[:, 0:NT - 1, P - 1], ALU.subtract)
                tt(qr[:, 1:NT, :], nmb[:, 1:NT, :], bcast(nmb[:, 0:NT - 1, P - 1:P], [P, NT - 1, P]), ALU.subtract)
                tell("act")
                hear("act")
                tt(dm, dm, bcast(causal.unsqueeze(1), [P, NT, P]), ALU.mult)
                for half in range(2):
                    d = DM[:, half * HALF:(half + 1) * HALF]
                    empty(lambda b: dve.tensor_tensor(d, d, b, ALU.mult))
                tt(QR[:, P:T], QR[:, P:T], QK[:, h, P:T], ALU.mult)
                for half in range(2):
                    j = slice(4 * half, 4 * half + 4)
                    empty(lambda b: dve.tensor_tensor(kw[:, j, :], cut(b, 4), bcast(wcol[:, j].unsqueeze(2), [P, 4, P]),
                                                      ALU.mult))
                for j0 in range(0, NT - 1, 2):
                    bank = ringV.take(dve)
                    n = min(2, NT - 1 - j0)
                    for x in range(n):
                        j, u = j0 + x, bank[:, x * VA:(x + 1) * VA]
                        if j == 0:
                            line(dve.tensor_copy(C[:, 1, :], u))
                        else:
                            line(dve.scalar_tensor_tensor(out=C[:, j + 1, :], in0=C[:, j, :], scalar=dcol[:, j:j + 1],
                                                          in1=u, op0=ALU.mult, op1=ALU.add),
                                 ringV.free if x == n - 1 else None)
                tell("pe")
                hear("act")
                stt(den, HB[:, :, ML_D], -1.0, HB[:, :, ML_D], ALU.mult, ALU.max)
                tt(den, den, cut(expm, NT)[:, :, h], ALU.max)
                line(dve.reciprocal(den, den))
                tt(O[:, :, 512 + h * ML_D:512 + (h + 1) * ML_D], HB[:, :, 0:ML_D], bcast(den.unsqueeze(2), [P, NT, ML_D]),
                   ALU.mult)
                tell("act")
            next_phase()

            for n in range(NT):
                hear("act")
                o = O[:, n, 512:1024]
                tt(o, o, work[:, (n % 2) * HALF:(n % 2 + 1) * HALF], ALU.mult)
                if n < NT - 2:
                    tell("act")
            sq = work[:, T:2 * T]
            ss5, r5 = cut(ss[:, 0:5 * NT], NT), cut(rstd[:, 0:5 * NT], NT)
            for i in range(NT):
                tt(sq, O[:, i, :], O[:, i, :], ALU.mult)
                line(dve.tensor_reduce(ss5[:, i, 0:1], sq[:, 0:512], AX_X, ALU.add))
                line(dve.tensor_reduce(ss5[:, i, 1:5], cut(sq[:, 512:1024], 4), AX_X, ALU.add))
            ts(r5[:, :, 0:1], ss5[:, :, 0:1], 1.0 / 512, EPS, ALU.mult, ALU.add)
            ts(r5[:, :, 1:5], ss5[:, :, 1:5], 1.0 / ML_D, EPS, ALU.mult, ALU.add)
            line(dve.reciprocal(rstd[:, 0:5 * NT], rstd[:, 0:5 * NT]))
            tell("act")
            hear("act")
            dve.wait_ge(row_in, 48)
            rows = work[:, 10 * T:11 * T]
            for i in range(NT):
                stt(O[:, i, 0:512], O[:, i, 0:512], r5[:, i, 0:1], rows[:, 0:512], ALU.mult, ALU.mult)
                o = cut(O[:, i, 512:1024], 4)
                tt(o, o, bcast(r5[:, i, 1:5].unsqueeze(2), [P, 4, ML_D]), ALU.mult)
                tt(O[:, i, 512:1024], O[:, i, 512:1024], rows[:, 512:1024], ALU.mult)
            tell("pe")
            turned()

            def residual(X, count):
                for n in range(2):
                    for i in range(NT):
                        if n == 0 and i % 2 == 0:
                            dve.wait_ge(dma_in[i // 2], count)
                        c = slice(n * HALF, (n + 1) * HALF)
                        empty(lambda b: dve.tensor_tensor(O[:, i, c], b, X[:, i, c], ALU.add))

            residual(X, 48)
            next_phase()

            CQ, M2, MT, CK, CV, S, PT, OT = cross_area()
            hear("pool")
            normed()
            turned(normcols["norm_cross_2"])
            hear("act")
            ts(rstd[:, 8:10], ss[:, 8:10], 1.0 / D, EPS, ALU.mult, ALU.add)
            line(dve.reciprocal(rstd[:, 8:10], rstd[:, 8:10]))
            tell("act")
            hear("act")
            for i in range(2):
                ts(M2[:, i, :], M2[:, i, :], rstd[:, 8 + i:9 + i], None, ALU.mult)
            tell("pe")
            for f in range(NK):
                empty(lambda b: dve.tensor_scalar(MT[:, f, :], b[:, 0:MEM], normcols["norm_mem_2"][:, f:f + 1], None,
                                                  ALU.mult))
            for m, half, ring in fm_fills(4):
                if ring is ringV:
                    empty(lambda b: dve.tensor_scalar(CQ[:, m, half * HALF:(half + 1) * HALF], b, P ** -0.5, None, ALU.mult))
            for n in range(NT + 1):
                if n < NT:
                    s = S[n % 2]
                    m = slice(4 * (n % 2), 4 * (n % 2) + 4)
                    for x in range(2):
                        empty(lambda b: dve.tensor_copy(s[:, 2 * x:2 * x + 2, :], cut(b, 2)))
                    line(dve.tensor_reduce(mx[:, m], s, AX_X, ALU.max))
                    tt(s, s, bcast(mx[:, m].unsqueeze(2), [P, 4, MEM]), ALU.subtract)
                    tell("act")
                if n:
                    s = S[(n - 1) % 2]
                    m = slice(4 * ((n - 1) % 2), 4 * ((n - 1) % 2) + 4)
                    hear("act")
                    line(dve.tensor_reduce(rden[:, m], s, AX_X, ALU.add))
                    line(dve.reciprocal(rden[:, m], rden[:, m]))
                    tt(s, s, bcast(rden[:, m].unsqueeze(2), [P, 4, MEM]), ALU.mult)
                    tell("pe")
            next_phase()
            residual(cut(work[:, 0:NT * D], NT), 64)
            next_phase()

            hear("pool")
            for half in range(2):
                inverse_root(half)
                for i in range(4 * half, 4 * half + 4):
                    ts(O[:, i, :], O[:, i, :], rstd[:, i:i + 1], None, ALU.mult)
                tell("pe")
            tell("pool")
            turned(normcols["norm_ffn_2"])
            n = GROUPS + EXPERTS
            empty(lambda b: dve.tensor_tensor(LG, cut(b[:, 0:NT * n], NT), bcast(lg_bias.unsqueeze(1), [P, NT, n]), ALU.add))
            iota = const("iota32")

            def reduce(to, of, op):
                line(dve.tensor_reduce(to, of, AX_X, op))

            def wide(ap, n):
                return bcast(ap.unsqueeze(2), [P, NT, n])

            def first_of(onehot, values, best, n):
                tt(onehot, values, wide(best, n), ALU.is_equal)
                stt(onehot, onehot, -1024.0, bcast(iota[:, 0:n].unsqueeze(1), [P, NT, n]), ALU.mult, ALU.add)
                reduce(R4, onehot, ALU.min)
                tt(onehot, onehot, wide(R4, n), ALU.is_equal)

            g, e = LG[:, :, 0:GROUPS], LG[:, :, GROUPS:]
            reduce(R1, g, ALU.max)
            first_of(OHG, g, R1, GROUPS)
            tt(GT, g, wide(R1, GROUPS), ALU.subtract)
            ts(cut(TMP.rearrange("p i e -> p (i e)")[:, 0:NT * GROUPS], NT), OHG, BIG, -BIG, ALU.mult, ALU.add)
            em, pen = EM.rearrange("p i e -> p (i e)"), TMP.rearrange("p i e -> p (i e)")[:, 0:NT * GROUPS]
            line(dve.tensor_copy(EM, e))
            tt(cut(em, NT * GROUPS), cut(em, NT * GROUPS), bcast(pen.unsqueeze(2), [P, NT * GROUPS, PER_GROUP]), ALU.add)
            reduce(R1, EM, ALU.max)
            first_of(OH1, EM, R1, EXPERTS)
            stt(EM, OH1, -3 * BIG, EM, ALU.mult, ALU.add)
            reduce(R2, EM, ALU.max)
            first_of(OH2, EM, R2, EXPERTS)
            tt(R3, R2, R1, ALU.subtract)
            tell("act")
            tt(A2, OH1, OH2, ALU.add)
            line(dve.memset(AC[:, 0, :], 0.0))
            for i in range(NT):
                tt(AC[:, i + 1, :] if i < NT - 1 else AC9, AC[:, i, :], A2[:, i, :], ALU.add)
            tell("pe")
            hear("act")
            reduce(R1, GT, ALU.add)
            ts(R2, R3, 1.0, None, ALU.add)
            tt(R1, R1, R2, ALU.mult)
            line(dve.reciprocal(gates2[:, 0:NT], R1))
            tt(gates2[:, NT:], gates2[:, 0:NT], R3, ALU.mult)
            bank = ringV.take(dve)
            line(dve.tensor_copy(TMP, cut(bank[:, 0:NT * EXPERTS], NT)))
            line(dve.tensor_copy(CN, bank[:, NT * EXPERTS:(NT + 1) * EXPERTS]), ringV.free)
            ts(SPN, CN, float(P), None, ALU.is_gt)
            for k in range(2, NT):
                stt(SPN, CN, float(k * P), SPN, ALU.is_gt, ALU.add)
            line(dve.tensor_tensor_scan(INC, bcast(one, [P, EXPERTS]), SPN, 0.0, ALU.mult, ALU.add))
            tt(KE, INC, SPN, ALU.subtract)
            tt(KE, KE, iota, ALU.subtract)
            ts(KE, KE, float(EXPERTS - 1), float(P), ALU.add, ALU.mult)
            ts(SM, TMP, float(P), None, ALU.is_ge)
            tt(SM, SM, bcast(KE.unsqueeze(1), [P, NT, EXPERTS]), ALU.mult)
            tt(SM, SM, TMP, ALU.add)
            stt(SM, bcast(iota.unsqueeze(1), [P, NT, EXPERTS]), float(P), SM, ALU.mult, ALU.add)
            for x, oh in ((0, OH1), (1, OH2)):
                tt(TMP, SM, oh, ALU.mult)
                reduce(R4, TMP, ALU.add)
                copy(slot_id[:, x * NT:(x + 1) * NT], R4)
            tell("pool")
            tt(SPM, bcast(INC.unsqueeze(1), [P, SPARE, EXPERTS]), bcast(iota[:, 0:SPARE].unsqueeze(2), [P, SPARE, EXPERTS]),
               ALU.is_le)
            reduce(CN[:, 0:SPARE], SPM, ALU.add)
            ts(CN[:, 0:SPARE], CN[:, 0:SPARE], float(EXPERTS - 1), None, ALU.min)
            copy(CN[:, SPARE:SPARE + 1], INC[:, EXPERTS - 1:EXPERTS])
            copy(spare_map[:, :], CN[:, 0:SPARE + 1])
            empty(lambda b: dve.tensor_copy(token_list[:, :], b[:, 0:BLOCKS]))
            for x in range(2):
                dve.sem_inc(y_stored[x], 16)
            dve.sem_inc(y0_out, 1)
            dve.sem_inc(y1_out, 1)
            next_phase()

            V0, V1, V2, V3 = banks[4:8]
            ffn = normcols["norm_ffn_2"]

            def block_ready(x, sem):
                for half, bank in ((0, V1), (1, V2)):
                    k = slice(4 * half, 4 * half + 4)
                    dve.tensor_tensor(XT[x][:, k, :], cut(bank, 4), bcast(ffn[:, k].unsqueeze(2), [P, 4, P]), ALU.mult)\
                        .then_inc(sem, 1)

            dve.wait_ge(tokens_turned, 1)
            block_ready(0, tokens_ready)
            with dve.Fori(0, EXPERTS // 2) as it:
                for x in range(2):
                    dve.wait_ge(up_full, it * 2 + x + 1)
                    dve.wait_ge(silu_ready, it * 2 + x + 1)
                    dve.tensor_tensor(HID, SILU, V0, ALU.mult).then_inc(hidden_ready, 1)
                    dve.wait_ge(tokens_turned, it * 2 + x + 2)
                    block_ready(1 - x, tokens_ready)
                    dve.wait_ge(down1_full, it * 2 + x + 1)
                    dve.wait_ge(y_stored[x], it * 16 + 16)
                    dve.tensor_copy(YO[x][:, HALF:D], V3).then_inc(y1_out, 1)
            spare = spare_count(dve)
            with dve.If(spare > 0):
                with dve.Fori(0, spare) as s:
                    dve.wait_ge(sp_turned, s + 1)
                    block_ready(0, sp_ready)
                    dve.wait_ge(sp_up, s + 1)
                    dve.wait_ge(sp_silu, s + 1)
                    dve.tensor_tensor(HID, SILU, V0, ALU.mult).then_inc(sp_hidden, 1)
                    dve.wait_ge(sp_down1, s + 1)
                    dve.tensor_copy(YO[0][:, HALF:D], V3).then_inc(sp_y1, 1)
            dve.wait_ge(moe_over, 1)
            for i in range(NT):
                if i % 2 == 0:
                    dve.wait_ge(dma_in[i // 2], 80)
                dve.wait_ge(combined[i], 32)
                for x in range(2):
                    stt(O[:, i, :], YG[2 * i + x], gates2[:, x * NT + i:x * NT + i + 1], O[:, i, :], ALU.mult, ALU.add)
                tell("act")
                hear("act")
                ts(rstd[:, i:i + 1], ss[:, i:i + 1], 1.0 / D, EPS, ALU.mult, ALU.add)
                line(dve.reciprocal(rstd[:, i:i + 1], rstd[:, i:i + 1]))
                tell("act")
                hear("act")
                if i == 0:
                    dve.wait_ge(row_in, 80)
                stt(O[:, i, :], O[:, i, :], rstd[:, i:i + 1], FINAL_ROW, ALU.mult, ALU.mult)
                dve.sem_inc(final_ready, 1)

        x1, x2 = scratch("x1", [NT, P, D]), scratch("x2", [NT, P, D])

        @block.gpsimd
        def _(pool):
            line = Line(pool, pool_own)
            phases = [0]
            stored = [0]

            def tell(who):
                words["pool", who].tell(pool)

            def hear(who):
                words[who, "pool"].hear(pool)

            def tt(o, a, b, op):
                line(pool.tensor_tensor(o, a, b, op))

            def next_phase():
                phases[0] += 1
                pool.sem_inc(phase, 1)
                pool.wait_ge(phase, 4 * phases[0])

            def bcast(ap, shape):
                return ap.to_broadcast(shape)

            def load_rows(to, of):
                for n in range(4):
                    pool.dma_start(to[:, 2 * n:2 * n + 2, :], of[2 * n:2 * n + 2].rearrange("i p d -> p i d"))\
                        .then_inc(dma_in[n], 16)

            def store_rows(to, of):
                pool.dma_start(to.rearrange("i p d -> p i d"), of).then_inc(dma_out, 16)
                stored[0] += 1
                pool.wait_ge(dma_out, 16 * stored[0])

            x_rows = A["x"][0].rearrange("(i p) d -> i p d", p=P)
            load_rows(O, x_rows)
            next_phase()

            def linear(name):
                Q, K, G, V, E, Qe, Ke, S = lin_area()
                for pair in range(2):
                    B = G[:, pair]
                    hear("dve")

                    def differ(lvl):
                        n = P >> lvl
                        b = level(cut(B, NT), n)
                        tt(level(E[lvl % 3], n), b, bcast(b[:, :, :, n // 2 - 1:n // 2], [P, NT, P // n, n]), ALU.subtract)
                        tell("act")

                    differ(0)
                    if pair:
                        hear("act")
                    tt(Ke[1], K[:, pair], Q[:, pair], ALU.mult)
                    tell("pe")
                    differ(1)
                    for lvl in range(LEVELS):
                        if lvl + 2 < LEVELS:
                            differ(lvl + 2)
                        hear("act")
                        hear("dve")
                        n = P >> lvl
                        h = n if lvl < 2 else n // 2
                        tt(level(cut(Ke[lvl % 2], NT), n)[:, :, :, 0:h], level(cut(K[:, pair], NT), n)[:, :, :, 0:h],
                           level(E[lvl % 3], n)[:, :, :, 0:h], ALU.mult)
                        tell("pe")
                    b = cut(B, NT)
                    tt(E[0], bcast(b[:, :, P - 1:P], [P, NT, P]), b, ALU.subtract)
                    tell("act")
                    hear("act")
                    hear("dve")
                    tt(cut(Ke[0], NT), cut(K[:, pair], NT), E[0], ALU.mult)
                    tell("pe")

            linear("a")
            words["act", "pool"].hear(pool)
            next_phase()
            linear("b")
            words["act", "pool"].hear(pool)
            next_phase()

            Q, K, V, Z, L, R = sb_area()
            sums = 0
            for h, c in SB_STEPS:
                l = L[c]
                for at, j, t0, above in sb_blocks(c):
                    if at:
                        if sums >= 2:
                            pool.wait_ge(ringV.full, stick_sums_used[sums - 2])
                        new = min(above + P, HALF) if j >= 4 * c - 1 else above
                        if new > above:
                            line(pool.tensor_copy(R[:, sums % 2, above:new], l[:, at - 1, above:new]))
                        if new < HALF:
                            tt(R[:, sums % 2, new:HALF], R[:, 1 - sums % 2, new:HALF], l[:, at - 1, new:HALF], ALU.add)
                        tell("pe")
                        sums += 1
                    hear("dve")
            next_phase()

            load_rows(cut(work[:, 2 * T:2 * T + NT * D], NT), x_rows)
            pool.dma_start(work[:, 10 * T:11 * T], A["final_norm_w"].rearrange("(a n) -> a n", a=1).partition_broadcast(P)).then_inc(row_in, 16)
            hear("dve")
            store_rows(x1, O)
            next_phase()

            zeros = masks.bitcast(F32)
            line(pool.memset(zeros, 0.0))
            pool.dma_start(y_dram[EXPERTS:BLOCKS].rearrange("b p d -> p b d"),
                           zeros.unsqueeze(1).to_broadcast([P, SPARE, D])).then_inc(spare_cleared, 16)
            next_phase()
            next_phase()
            load_rows(cut(work[:, 2 * T:2 * T + NT * D], NT), x1)
            for n, (name, at) in enumerate((("norm_att_out_2", 0), ("norm_ml_out_2", 512))):
                pool.dma_start(work[:, 10 * T + at:10 * T + at + 512], A[name].partition_broadcast(P)).then_inc(row_in, 16)
                pool.wait_ge(row_in, 16 * (n + 2))
            next_phase()
            CQ, M2, MT, CK, CV, S, PT, OT = cross_area()
            pool.dma_start(M2, A["mem_2"][0].rearrange("(i p) d -> p i d", p=P)).then_inc(row_in, 16)
            store_rows(x2, O)
            tell("dve")
            pool.wait_ge(row_in, 64)
            next_phase()
            load_rows(cut(work[:, 0:NT * D], NT), x2)
            next_phase()
            store_rows(x3_dram, O)
            tell("dve")
            pool.wait_ge(spare_cleared, 16)
            line(pool.memset(ZT, 0.0))
            pool.dma_start(tok_dram.rearrange("(b p) a -> b (p a)", p=P), ZT[0:BLOCKS, :]).then_inc(tok_in, 16)
            pool.wait_ge(tok_in, 16)
            hear("dve")
            store_rows(xn_dram.rearrange("(i p) d -> i p d", p=P), O)
            hear("dve")
            for x in range(2):
                for i in range(NT):
                    pool.indirect_dma_start(tok_dram, bass.IndirectOffsetOnAxis(ap=slot_id[:, x * NT + i:x * NT + i + 1], axis=0),
                                            const("token")[:, i:i + 1], None).then_inc(scattered, 16)
            pool.wait_ge(scattered, 16 * 2 * NT)
            pool.dma_start(TOKF[0:BLOCKS, :], tok_dram.rearrange("(b p) a -> b (p a)", p=P)).then_inc(tok_in, 16)
            pool.wait_ge(tok_in, 32)
            tell("pe")
            next_phase()

            def gather_block(place, x, row, sem):
                pool.indirect_dma_start(row, None, xn_dram, bass.IndirectOffsetOnAxis(ap=index[place][:, :], axis=0))\
                    .then_inc(sem, 16)

            for x in range(2):
                pool.tensor_copy(index[x][:, :], token_list[:, x:x + 1]).then_inc(index_ready, 1)
                pool.wait_ge(index_ready, x + 1)
                gather_block(x, x, XG[x], rows_gathered[x])
            with pool.Fori(0, EXPERTS // 2) as it:
                for x in range(2):
                    pool.wait_ge(tokens_turned, it * 2 + x + 1)
                    pool.tensor_copy(index[x][:, :], token_list[:, bass.ds(it * 2 + x + 2, 1)]).then_inc(index_ready, 1)
                    pool.wait_ge(index_ready, it * 2 + x + 3)
                    pool.sem_inc(pool_passed, 1)
                    gather_block(x, x, XG[x], rows_gathered[x])
            for x in range(2):
                pool.wait_ge(rows_gathered[x], 16 * (EXPERTS // 2 + 1))
            spare = spare_count(pool)
            with pool.If(spare > 0):
                with pool.Fori(0, spare) as s:
                    pool.wait_ge(sp_over, s + 1)
                    pool.tensor_copy(index[2][:, :], token_list[:, bass.ds(s + EXPERTS, 1)]).then_inc(sp_index, 1)
                    pool.wait_ge(sp_index, s + 1)
                    pool.sem_inc(pool_passed, 1)
                    gather_block(2, 0, XG[0], sp_rows)
            pool.wait_ge(moe_over, 1)
            load_rows(O, x3_dram)
            pool.dma_start(FINAL_ROW, A["norm_final_2"].rearrange("(a n) -> a n", a=1).partition_broadcast(P)).then_inc(row_in, 16)
            for i in range(NT):
                for x in range(2):
                    pool.indirect_dma_start(YG[2 * i + x], None, y_dram.rearrange("b p d -> (b p) d"),
                                            bass.IndirectOffsetOnAxis(ap=slot_id[:, x * NT + i:x * NT + i + 1], axis=0))\
                        .then_inc(combined[i], 16)

        @block.sync
        def _(sp):
            used = {n: chunk_over.get(name) for name, n in chunk_of.items()}
            for n, parts in enumerate(chunks):
                if n >= 3:
                    a, v = used[n - 3]
                    if a:
                        sp.wait_ge(ringA.full, a)
                    if v:
                        sp.wait_ge(ringV.full, v)
                at = 0
                for w, lo, hi in parts:
                    to = cut(slots[:, (n % 3) * NK * HALF:(n % 3 + 1) * NK * HALF], w.shape[1])
                    sp.dma_start(to[:, :, at:at + hi - lo], w[:, :, lo:hi])\
                        .then_inc(slot_full[n % 3], 16)
                    at += hi - lo

            def load_expert(x, e, sems):
                wg, wu, wd = expert_weights(x)
                for to, name, s in zip((wg, wu, wd), ("w_e_gate_2", "w_e_up_2", "w_e_down_2"), sems):
                    of = A[name][0][bass.ds(e, 1)].rearrange("e (k p) n -> p (e k) n", p=P)
                    sp.dma_start(to, of).then_inc(s, 16)

            sp.wait_ge(ringV.full, chunk_over["router"][1])
            load_expert(0, 0, weights_in[0])
            sp.wait_ge(phase, 4 * PHASES_BEFORE_ROUTING)
            load_expert(1, 1, weights_in[1])
            with sp.Fori(0, EXPERTS // 2 - 1) as it:
                for x in range(2):
                    for (to, name, arrived), over in zip(
                            zip(expert_weights(x), ("w_e_gate_2", "w_e_up_2", "w_e_down_2"), weights_in[x]),
                            (up_full, up_full, down1_full)):
                        sp.wait_ge(over, it * 2 + x + 1)
                        sp.sem_inc(sp_passed, 1)
                        of = A[name][0][bass.ds(it * 2 + x + 2, 1)].rearrange("e (k p) n -> p (e k) n", p=P)
                        sp.dma_start(to, of).then_inc(arrived, 16)
            sp.wait_ge(phase, 4 * (PHASES_BEFORE_ROUTING + 1))
            spare = spare_count(sp)
            with sp.If(spare > 0):
                with sp.Fori(0, spare) as s:
                    sp.wait_ge(sp_over, s + 1)
                    sp.sem_inc(sp_passed, 1)
                    e = sp.value_load(spare_map[0:1, bass.ds(s, 1)], min_val=0, max_val=EXPERTS - 1)
                    load_expert(0, e, [sp_weights] * 3)
            for n in range(4):
                sp.wait_ge(final_ready, 2 * n + 2)
                sp.dma_start(out[0, 2 * n * P:(2 * n + 2) * P, :].rearrange("(i p) d -> p i d", p=P), O[:, 2 * n:2 * n + 2, :])\
                    .then_inc(out_sem[n], 16)
            for n in range(4):
                sp.wait_ge(out_sem[n], 16)


_INS = ["x", "c", "w_ada", "b_ada", "w_in", "w_gla_gate2", "b_gla_gate", "gla_norm_w", "hgrn_lb_logits", "hgrn_norm_w",
        "w_out", "final_norm_w", "mem_2", "norm_mix_2", "w_in_2", "b_gates_2", "conv_w_2", "conv_b_2", "att_sinks_2",
        "norm_att_out_2", "norm_ml_out_2", "w_out_2", "norm_cross_2", "norm_mem_2", "w_cq_2", "w_ckv_2", "w_co_2",
        "norm_ffn_2", "w_router_group_2", "b_router_group_2", "w_router_expert_2", "b_router_expert_2", "w_e_gate_2",
        "w_e_up_2", "w_e_down_2", "norm_final_2"]


def kernel(**inputs):
    import numpy as _np
    import concourse.bacc as _bacc
    from concourse import mybir as _mybir
    from concourse.bass_utils import run_bass_kernel_spmd as _run

    nc = _bacc.Bacc("TRN2", target_bir_lowering=False, num_devices=1)
    arrays, args = {}, {}
    for name in _INS:
        arrays[f"in_{name}_dram"] = _np.ascontiguousarray(inputs[name])
    for name, table in zip(("consts", "masks"), constants()):
        arrays[f"in_{name}_dram"] = table
    for name in _INS + ["consts", "masks"]:
        a = arrays[f"in_{name}_dram"]
        args[name] = nc.dram_tensor(f"in_{name}_dram", a.shape, _mybir.dt.from_np(a.dtype), kind="ExternalInput").ap()
    out = nc.dram_tensor("out_dram", (1, T, D), F32, kind="ExternalOutput").ap()
    program(nc, args, out)
    r = _run(nc, [arrays], core_ids=[0])
    return r.results[0]["out_dram"]
```

```python
from contextlib import ExitStack

import numpy as np

import concourse.bass as bass
from concourse import mybir

F32 = mybir.dt.float32
U32 = mybir.dt.uint32
I32 = mybir.dt.int32
ALU = mybir.AluOpType
ACT = mybir.ActivationFunctionType
AX_X = mybir.AxisListType.X

P = 128
T = 1024
D = 1024
NT = T // P
NK = D // P
HALF = 512
EPS = 1e-6

GLA_HEADS, GLA_DV, HGRN_HEADS, HGRN_DV, SB_HEADS, DK = 4, 128, 4, 64, 4, 64
RANK = 16
TAU = 16.0
LEVELS = 7

ATT_HEADS, KV_HEADS, ML_HEADS, ML_D, TAPS = 8, 2, 4, 128, 4
VA = ML_D + 1
MEM = 256
GROUPS, PER_GROUP = 4, 8
EXPERTS = GROUPS * PER_GROUP
DE = 512
SPARE = T * 2 // P - 1
BLOCKS = EXPERTS + SPARE
SLOTS = BLOCKS * P
BIG = 1e30
PHASES_BEFORE_ROUTING = 9

CONST = {}
_at = 0
for _name, _n in (("ident", P), ("negtri", P), ("negones", P), ("ones", P), ("strict", P), ("causal", P),
                  ("dist", 2 * P), ("sel", ML_HEADS * P), ("iota32", EXPERTS), ("token", NT)):
    CONST[_name] = (_at, _n)
    _at += _n
CONSTS = _at


def constants():
    c = np.zeros((P, CONSTS), np.float32)
    r, q = np.arange(P)[:, None], np.arange(P)[None, :]

    def put(name, value):
        at, n = CONST[name]
        c[:, at:at + n] = value

    put("ident", r == q)
    put("negtri", -1.0 * (r >= q))
    put("negones", -1.0)
    put("ones", 1.0)
    put("strict", r < q)
    put("causal", r <= q)
    dist = r + P - np.arange(2 * P)[None, :]
    put("dist", np.where((dist >= 0) & (dist < P), -dist, -BIG))
    sel = np.zeros((P, ML_HEADS, P), np.float32)
    for h in range(ML_HEADS):
        sel[h, h] = 1.0
    put("sel", sel.reshape(P, -1))
    put("iota32", np.arange(EXPERTS)[None, :])
    put("token", r + P * np.arange(NT)[None, :])
    masks = np.zeros((P, LEVELS + 1, P), np.uint32)
    for lvl in range(LEVELS):
        h = P // 2 >> lvl
        masks[:, lvl] = (r // (2 * h) == q // (2 * h)) & (r // h % 2 == 0) & (q // h % 2 == 1)
    masks[:, LEVELS] = r == q
    return c, masks.reshape(P, -1)


class Line:

    def __init__(self, eng, own):
        self.eng, self.own, self.count = eng, own, {}

    def __call__(self, ins, sem=None):
        sem = self.own if sem is None else sem
        self.count[sem.name] = self.count.get(sem.name, 0) + 1
        ins.then_inc(sem, 1)
        self.eng.wait_ge(sem, self.count[sem.name])


class Word:

    def __init__(self, sem):
        self.sem, self.told, self.heard = sem, 0, 0

    def tell(self, eng):
        eng.sem_inc(self.sem, 1)
        self.told += 1

    def hear(self, eng):
        self.heard += 1
        eng.wait_ge(self.sem, self.heard)


class Ring:

    def __init__(self, banks, full, free):
        self.banks, self.full, self.free = banks, full, free
        self.filled = self.taken = 0

    def open(self, pe):
        if self.filled >= len(self.banks):
            pe.wait_ge(self.free, self.filled - len(self.banks) + 1)
        return self.banks[self.filled % len(self.banks)]

    def close(self, ins):
        ins.then_inc(self.full, 1)
        self.filled += 1

    def take(self, eng):
        self.taken += 1
        eng.wait_ge(self.full, self.taken)
        return self.banks[(self.taken - 1) % len(self.banks)]


def program(nc, A, out):
    with ExitStack() as ctx:
        def sb(name, n, dt=F32):
            return ctx.enter_context(nc.sbuf_tensor(name, [P, n], dt))[:, :]

        def sem(name):
            return ctx.enter_context(nc.semaphore(name))

        def cut(ap, n):
            return ap.rearrange("p (a b) -> p a b", a=n)

        cst = sb("cst", CONSTS)
        masks = sb("masks", (LEVELS + 1) * P, U32)
        small = sb("small", 1024)
        gate_row = sb("gate_row", D)
        slots = sb("slots", 3 * NK * HALF)
        HT = cut(sb("HT", NK * T), NK)
        O = cut(sb("O", NT * D), NT)
        WORK = 19000
        work = sb("work", WORK)

        def scratch(name, shape, dt=F32):
            return nc.dram_tensor(name, shape, dt, kind="Internal").ap()

        def const(name, rows=P):
            at, n = CONST[name]
            return cst[0:rows, at:at + n]

        small_at = [0]

        def col(n):
            at = small_at[0]
            small_at[0] += n
            assert small_at[0] <= 1024
            return small[:, at:at + n]

        class Area:
            def __init__(self):
                self.at = 0

            def __call__(self, n):
                self.at += n
                assert self.at <= WORK, self.at
                return work[:, self.at - n:self.at]

        ccol, cact = col(NK), col(NK)
        bcol, mod = col(16), col(16)
        bgate = col(2)
        ss, rstd = col(64), col(64)
        one, zero = col(1), col(1)
        two_heads = col(2)
        decay = col(NT)
        gla_w, hgrn_w = col(GLA_DV), col(HGRN_DV)
        normcols = {n: col(NK) for n in ("norm_mix_2", "norm_cross_2", "norm_mem_2", "norm_ffn_2")}

        sinks, mx, es, rden = col(ATT_HEADS), col(16), col(16), col(16)
        b_if = col(2)
        conv_b, conv_w = col(NK), col(NK * TAPS)
        acm = col(NT * 3 * ML_HEADS)
        expm, den = col(NT * ML_HEADS), col(NT)
        wcols, dcols = [col(NT) for _ in range(2)], [col(NT) for _ in range(2)]

        banks = [ctx.enter_context(nc.psum_tensor(f"bank{i}", [P, HALF], F32))[:, :] for i in range(8)]
        ringA = Ring(banks[0:4], sem("act_banks_full"), sem("act_banks_free"))
        ringV = Ring(banks[4:8], sem("dve_banks_full"), sem("dve_banks_free"))

        act_own, dve_own, pool_own = sem("act_own"), sem("dve_own"), sem("pool_own")
        names = ("act", "dve", "pool", "pe")
        words = {(a, b): Word(sem(f"{a}_told_{b}")) for a in names for b in names if a != b and a != "pe"}
        phase = sem("phase_over")
        first_loaded, loaded = sem("first_loaded"), sem("small_loaded")
        dma_in = [sem(f"rows_loaded{i}") for i in range(4)]
        dma_out = sem("rows_stored")
        row_in = sem("weight_row_loaded")
        slot_full = [sem(f"slot_full{i}") for i in range(3)]

        MODROW = work[0:1, 2 * T:4 * T]

        chunks, chunk_of, chunk_over = [], {}, {}

        def add_chunk(name, *parts):
            chunk_of[name] = len(chunks)
            chunks.append(parts)

        w_ada, w_in, w_out = (A[n].rearrange("a (k p) n -> p (a k) n", p=P) for n in ("w_ada", "w_in", "w_out"))
        w_in2, w_out2 = (A[n].rearrange("a (k p) n -> p (a k) n", p=P) for n in ("w_in_2", "w_out_2"))
        for n in range(4):
            add_chunk(f"ada{n}", (w_ada, 512 * n, 512 * n + 512))
        add_chunk("a_qk", (w_in, 0, 512))
        add_chunk("a_v", (w_in, 512, 1024))
        add_chunk("a_rank", (w_in, 1024, 1040))
        for n in range(4, 6):
            add_chunk(f"ada{n}", (w_ada, 512 * n, 512 * n + 512))
        add_chunk("c_qk", (w_in, 2576, 3088))
        add_chunk("b_qf", (w_in, 1552, 2064))
        add_chunk("b_v", (w_in, 2064, 2320))
        add_chunk("c_v", (w_in, 3088, 3344))
        add_chunk("a_gate", (w_in, 1040, 1552))
        add_chunk("bc_gate", (w_in, 2320, 2576), (w_in, 3344, 3600))
        add_chunk("out0", (w_out, 0, 512))
        add_chunk("out1", (w_out, 512, 1024))
        for_heads = [h // 2 + 4 * (h % 2) for h in range(ATT_HEADS)]
        add_chunk("att_q", *[(w_in2, 64 * h, 64 * h + 64) for h in for_heads])
        add_chunk("att_kv", (w_in2, 512, 768))
        add_chunk("ml_v", (w_in2, 1792, 2304))
        IF_STEP = 32
        add_chunk("ml_if", (w_in2, 2816, 2820), (w_in2, 0, IF_STEP - ML_HEADS), (w_in2, 2820, 2824))
        add_chunk("ml_q", (w_in2, 768, 1280))
        add_chunk("ml_k", (w_in2, 1280, 1792))
        add_chunk("ml_gate", (w_in2, 2304, 2816))
        add_chunk("out2_0", (w_out2, 0, 512))
        add_chunk("out2_1", (w_out2, 512, 1024))
        w_cq, w_ckv, w_co = (A[n].rearrange("a (k p) n -> p (a k) n", p=P) for n in ("w_cq_2", "w_ckv_2", "w_co_2"))
        add_chunk("cross_q", (w_cq, 0, 512))
        add_chunk("cross_k", (w_ckv, 0, 512))
        add_chunk("cross_v", (w_ckv, 512, 1024))
        add_chunk("cross_out", (w_co, 0, 1024))
        w_rg, w_re = (A[n].rearrange("a (k p) n -> p (a k) n", p=P) for n in ("w_router_group_2", "w_router_expert_2"))
        add_chunk("router", (w_rg, 0, GROUPS), (w_re, 0, EXPERTS))

        def slot(i):
            return cut(slots[:, i * NK * HALF:(i + 1) * NK * HALF], NK)

        def fm_fills(tiles):
            return [(m, half, ringA if half == 0 else ringV) for m in range(tiles) for half in range(2)]

        def tm_fills():
            return [(i, ringA if i % 2 == 0 else ringV) for i in range(NT)]

        def turn_fills():
            return [(half, f, ringA if f % 2 == 0 else ringV) for half in range(2) for f in range(NK)]

        LIN = {"a": (GLA_DV, 0), "b": (HGRN_DV, GLA_HEADS * GLA_DV)}
        SB0 = GLA_HEADS * GLA_DV + HGRN_HEADS * HGRN_DV

        def lin_area():
            ar = Area()
            Q, K, G = cut(ar(2 * T), 2), cut(ar(2 * T), 2), cut(ar(2 * T), 2)
            V = cut(ar(NT * 512), NT)
            E = [cut(ar(T), NT), cut(ar(T), NT), O[:, :, SB0:SB0 + P]]
            Qe, Ke = [ar(T) for _ in range(2)], [ar(T) for _ in range(2)]
            S = cut(ar(2 * T), 2 * NT)
            return Q, K, G, V, E, Qe, Ke, S

        def level(x, n):
            return x.rearrange("p j (a n) -> p j a n", n=n)

        AHEAD = {"a": "c_qk", "b": "c_v"}
        ahead_dram = scratch("stick_inputs", [P, 2 * 2 * T + NT * 256])
        stages = [O[:, 4 * x:4 * x + 4, SB0 + P:SB0 + 2 * P] for x in range(2)]
        stage_stored = [sem(f"stage_stored{x}") for x in range(2)]
        stick_in = [sem(f"stick_{n}_in") for n in ("first_pair", "values", "second_pair")]

        def sb_area():
            ar = Area()
            Q, K = cut(ar(2 * T), 2), cut(ar(2 * T), 2)
            V = cut(ar(NT * 256), NT)
            Z, L = ([cut(ar(4 * n * HALF), 4 * n) for n in (1, 2)] for _ in range(2))
            R = cut(masks.bitcast(F32), 2)
            return Q, K, V, Z, L, R

        SB_STEPS = [(h, c) for h in range(SB_HEADS) for c in range(2)]
        stick_weights = Word(sem("stick_weights_ready"))
        stick_sums_used = []

        def sb_order():
            for n in range(len(SB_STEPS) + 1):
                if n:
                    yield (*SB_STEPS[n - 1], "weights")
                if n < len(SB_STEPS):
                    yield (*SB_STEPS[n], "logits")
                if n:
                    yield (*SB_STEPS[n - 1], "output")

        def sb_blocks(c):
            n = 4 * c + 4
            first = lambda j: max(0, (j - 4 * c) * P)
            return [(n - 1 - j, j, first(j), first(j + 1)) for j in reversed(range(n))]

        def att_area():
            ar = Area()
            return (cut(ar(4 * T), 4), ar(T), cut(ar(NT * P), NT), [cut(ar(ATT_HEADS * 2 * P), ATT_HEADS) for _ in range(2)],
                    cut(ar(2 * ATT_HEADS * P), 2 * ATT_HEADS))

        def att_range(n):
            return P if n == 0 else 0

        def ml_area():
            ar = Area()
            QK = cut(ar(2 * ML_HEADS * T), 2 * ML_HEADS)
            NMB, DM, QR, KW = ar(T), ar(T), ar(T), ar(T)
            VM = ar(NT * ML_HEADS * VA).rearrange("p (i h v) -> p i h v", i=NT, h=ML_HEADS)
            C, HB = cut(ar(NT * VA), NT), cut(ar(NT * VA), NT)
            return QK, VM, NMB, DM, QR, KW, C, HB

        def head_area(h):
            QK, VM, NMB, DM, QR, KW, C, HB = ml_area()
            nmb, dm = (NMB, DM) if h == 0 else (QK[:, h - 1], QK[:, ML_HEADS + h - 1])
            return nmb, dm, (QR, NMB)[h % 2], wcols[h % 2], dcols[h % 2]

        X = cut(work[:, 2 * T:2 * T + NT * D], NT)
        ROW, BIAS_ROW = work[:, 10 * T:11 * T], work[:, 11 * T:12 * T]
        GATES = [work[:, (12 + i) * T:(13 + i) * T] for i in range(6)]
        NORMED = [work[:, i * T:(i + 1) * T] for i in range(2)]
        NORMED2 = [work[:, (11 + i) * T:(12 + i) * T] for i in range(2)]
        SQUARED = work[:, 13 * T:14 * T]
        GATES2 = [work[:, 14 * T + i * HALF:14 * T + (i + 1) * HALF] for i in range(4)]

        ROUTES = GROUPS + EXPERTS
        LOGITS = gate_row[0:ROUTES, :]
        NORMED3 = [work[:, (15 + i) * T:(16 + i) * T] for i in range(3)]

        def cross_area():
            ar = Area()
            CQ = cut(ar(4 * T), 4)
            M2 = cut(work[:, 16 * T:16 * T + 2 * D], 2)
            MT, CK = cut(ar(NK * MEM), NK), cut(ar(4 * MEM), 4)
            CV = cut(ar(2 * HALF), 2)
            S = [cut(ar(4 * MEM), 4) for _ in range(2)]
            PT = cut(ar(8 * P), 8)
            OT = cut(ar(4 * T), 4)
            assert ar.at <= 15 * T
            return CQ, M2, MT, CK, CV, S, PT, OT

        TAIL = 3 * NK * HALF
        O_flat, HT_flat = O.rearrange("p i d -> p (i d)"), HT.rearrange("p k t -> p (k t)")

        def expert_weights(x):
            at = slots if x == 0 else work
            n = NK * HALF
            return cut(at[:, 0:n], NK), cut(at[:, n:2 * n], NK), cut(at[:, 2 * n:3 * n], DE // P)

        XG = [O_flat[:, 0:D], O_flat[:, D:2 * D]]
        XT = [cut(O_flat[:, 2 * D:3 * D], NK), cut(O_flat[:, 3 * D:4 * D], NK)]
        YO = [O_flat[:, 4 * D:5 * D], O_flat[:, 5 * D:6 * D]]
        SILU, HID = O_flat[:, 6 * D:6 * D + HALF], O_flat[:, 6 * D + HALF:7 * D]
        gates2 = col(2 * NT)
        lg_bias = col(GROUPS + EXPERTS)
        slot_id = ctx.enter_context(nc.sbuf_tensor("slot_id", [P, 2 * NT], U32))
        token_list = ctx.enter_context(nc.sbuf_tensor("token_list", [P, BLOCKS], U32))
        spare_map = ctx.enter_context(nc.sbuf_tensor("spare_map", [P, SPARE + 1], I32))
        index = [ctx.enter_context(nc.sbuf_tensor(f"index{x}", [P, 1], U32)) for x in range(3)]
        tail = work[:, TAIL:WORK]
        at_tail = [0]

        def temp(n):
            at_tail[0] += n
            assert at_tail[0] <= WORK - TAIL
            return tail[:, at_tail[0] - n:at_tail[0]]

        LG, OH1, OH2, EM, TMP, A2, AC, SM = (cut(temp(NT * n), NT) for n in
                                             (GROUPS + EXPERTS, EXPERTS, EXPERTS, EXPERTS, EXPERTS, EXPERTS, EXPERTS, EXPERTS))
        OHG, GT = cut(temp(NT * GROUPS), NT), cut(temp(NT * GROUPS), NT)
        AC9, CN, SPN, INC, KE = temp(EXPERTS), temp(EXPERTS), temp(EXPERTS), temp(EXPERTS), temp(EXPERTS)
        SPM = cut(temp(SPARE * EXPERTS), SPARE)
        R1, R2, R3, R4 = temp(NT), temp(NT), temp(NT), temp(NT)
        TOKF = temp(P)
        tok_dram = scratch("token_of_slot", [SLOTS, 1])
        x3_dram, xn_dram = scratch("x3", [NT, P, D]), scratch("xn", [T, D])
        y_dram = scratch("y_of_slot", [BLOCKS, P, D])
        rows_gathered = [sem(f"rows_gathered{x}") for x in range(2)]
        weights_in = [[sem(f"expert_{n}_in{x}") for n in ("gate", "up", "down")] for x in range(2)]
        y_stored = [sem(f"y_stored{x}") for x in range(2)]
        (tokens_turned, tokens_ready, gate_full, up_full, silu_ready, hidden_ready, down0_full, down1_full,
         y0_out, y1_out, index_ready) = (sem(n) for n in (
             "tokens_turned", "tokens_ready", "gate_full", "up_full", "silu_ready", "hidden_ready", "down0_full",
             "down1_full", "y0_out", "y1_out", "index_ready"))
        (sp_rows, sp_weights, sp_turned, sp_ready, sp_gate, sp_up, sp_silu, sp_hidden, sp_down0, sp_down1, sp_y0, sp_y1,
         sp_stored, sp_over, sp_index, sp_passed) = (sem("spare_" + n) for n in (
             "rows", "weights", "turned", "ready", "gate_full", "up_full", "silu", "hidden", "down0", "down1", "y0", "y1",
             "stored", "over", "index", "passed"))
        pool_passed, spare_cleared = sem("pool_passed"), sem("spare_cleared")
        moe_over, final_ready = sem("moe_over"), sem("final_ready")
        scattered, tok_in = sem("tokens_scattered"), sem("token_list_in")
        combined = [sem(f"combine_rows{i}") for i in range(NT)]
        out_sem = [sem(f"out_stored{i}") for i in range(4)]
        YG = [work[:, i * D:(i + 1) * D] for i in range(16)]
        spare_count = lambda eng: eng.value_load(spare_map[0:1, SPARE:SPARE + 1], min_val=0, max_val=SPARE)
        roots, normed_ready = Word(sem("tile_roots")), Word(sem("normed_tile_ready"))
        final_squares = Word(sem("final_squares"))
        FINAL_ROW = slots[:, 0:D]

        block = ctx.enter_context(nc.Block())

        @block.tensor
        def _(pe):
            loads = [0] * 3
            phases = [0]

            def hear(who):
                words[who, "pe"].hear(pe)

            def weights(name):
                n = chunk_of[name]
                pe.wait_ge(slot_full[n % 3], 16 * sum(len(chunks[m]) for m in range(n % 3, n + 1, 3)))
                return slot(n % 3)

            def used(name):
                chunk_over[name] = (ringA.filled, ringV.filled)

            def emptied():
                pe.wait_ge(ringA.free, ringA.filled)
                if ringV.filled:
                    pe.wait_ge(ringV.free, ringV.filled)

            def next_phase():
                emptied()
                phases[0] += 1
                pe.sem_inc(phase, 1)
                pe.wait_ge(phase, 4 * phases[0])

            def chain(bank, pairs):
                for n, (lhsT, rhs) in enumerate(pairs):
                    ins = pe.matmul(bank, lhsT, rhs, start=(n == 0), stop=(n == len(pairs) - 1))
                return ins

            def product_fm(name, cols, fills, at=0):
                w = weights(name)
                for m, half, ring in fills:
                    n = min(P, cols - m * P)
                    bank = ring.open(pe)[0:n, :]
                    ring.close(chain(bank, [(w[:, k, at + m * P:at + m * P + n], HT[:, k, half * HALF:(half + 1) * HALF])
                                            for k in range(NK)]))
                used(name)

            def product_tm(name, cols, fills, x=None, at=0):
                w = weights(name)
                x = HT if x is None else x
                for i, ring in fills:
                    bank = ring.open(pe)[:, 0:cols]
                    ring.close(chain(bank, [(x[:, k, i * P:(i + 1) * P], w[:, k, at:at + cols]) for k in range(NK)]))
                used(name)

            def turn(heard):
                ident = const("ident")
                for half, f, ring in turn_fills():
                    if heard and f == 0:
                        hear("dve")
                    bank = ring.open(pe)
                    for q in range(4):
                        ins = pe.transpose(bank[:, q * P:(q + 1) * P], O[:, 4 * half + q, f * P:(f + 1) * P], ident)
                    ring.close(ins)

            def turn_tile(i, x, ring):
                for half in range(2):
                    bank = ring.open(pe)
                    for q in range(4):
                        f = 4 * half + q
                        ins = pe.transpose(bank[:, q * P:(q + 1) * P], x[:, f * P:(f + 1) * P], const("ident"))
                    ring.close(ins)

            def projected(names, x, lag):
                for i in range(NT + lag):
                    if i < NT:
                        for name in names:
                            product_tm(name, 512, [(i, ringV)])
                    if i >= lag:
                        hear("dve")
                        turn_tile(i - lag, x[(i - lag) % len(x)], ringV)

            pe.wait_ge(first_loaded, 32)
            hear("act")
            for n in range(4):
                w = weights(f"ada{n}")
                ringV.close(chain(ringV.open(pe)[0:1, :], [(cact[:, k:k + 1], w[:, k, :]) for k in range(NK)]))
                used(f"ada{n}")
            for _ in range(3):
                hear("dve")
            bank = ringV.open(pe)
            for m in range(16):
                ins = pe.transpose(bank[:, m:m + 1], MODROW[:, m * P:(m + 1) * P], const("ident", 1)[:, 0:1])
            ringV.close(ins)
            turn(False)
            next_phase()

            def linear(name):
                dv, o0 = LIN[name]
                Q, K, G, V, E, Qe, Ke, S = lin_area()
                done = [0]

                def ahead():
                    n = done[0]
                    if name == "a":
                        product_fm("c_qk", 512, [(n // 2, n % 2, ringA)])
                    else:
                        product_tm("c_v", 256, [(n, ringA)])
                    done[0] += 1

                for pair in range(2):
                    ahead()
                    hear("pool")
                    bank = ringV.open(pe)
                    for j in range(NT):
                        ins = pe.matmul(bank[:, 2 * j:2 * j + 2], Ke[1][:, j * P:(j + 1) * P], two_heads,
                                        start=True, stop=True)
                    ringV.close(ins)
                    for lvl in range(LEVELS):
                        hear("dve")
                        hear("pool")
                        q, k = Qe[lvl % 2], Ke[lvl % 2]
                        for j0 in range(0, NT, 4):
                            bank = ringV.open(pe)
                            for j in range(j0, j0 + 4):
                                ins = pe.matmul(bank[:, (j - j0) * P:(j - j0 + 1) * P], k[:, j * P:(j + 1) * P],
                                                q[:, j * P:(j + 1) * P], start=True, stop=True)
                            ringV.close(ins)
                        if lvl in (3, LEVELS - 1):
                            ahead()
                    hear("pool")
                    for half in range(2):
                        bank = ringA.open(pe)
                        for j in range(4):
                            t = slice(half * HALF + j * P, half * HALF + (j + 1) * P)
                            ins = pe.transpose(bank[:, j * P:(j + 1) * P], Ke[0][:, t], const("ident"))
                        ringA.close(ins)
                    pe.wait_ge(ringA.free, ringA.filled)
                    KT, St = cut(Qe[1], NT), cut(Ke[1][:, 0:NT * dv], NT)
                    per = HALF // dv
                    for j0 in range(0, NT - 1, per):
                        bank = ringV.open(pe)
                        for j in range(j0, min(j0 + per, NT - 1)):
                            for hh in range(2):
                                v = V[:, j, (2 * pair + hh) * dv:(2 * pair + hh + 1) * dv]
                                ins = pe.matmul(bank[64 * hh:64 * hh + 64, (j - j0) * dv:(j - j0 + 1) * dv],
                                                KT[:, j, 64 * hh:64 * hh + 64], v, start=True, stop=True)
                        ringV.close(ins)
                    ahead()
                    hear("dve")
                    for hh in range(2):
                        d = slice(64 * hh, 64 * hh + 64)
                        for j0 in range(0, NT, per):
                            bank = ringA.open(pe)
                            for j in range(j0, j0 + per):
                                to, t = bank[:, (j - j0) * dv:(j - j0 + 1) * dv], slice(j * P, (j + 1) * P)
                                v = V[:, j, (2 * pair + hh) * dv:(2 * pair + hh + 1) * dv]
                                ins = pe.matmul(to, S[:, 2 * j + hh, :], v, start=True, stop=(j == 0))
                                if j:
                                    ins = pe.matmul(to, Qe[0][d, t], St[d, j, :], start=False, stop=True)
                            ringA.close(ins)

            product_fm("a_qk", 512, fm_fills(4))
            product_tm("a_v", 512, tm_fills())
            product_fm("a_rank", RANK, fm_fills(1))
            emptied()
            Q, K, G, V, E, Qe, Ke, S = lin_area()
            for m in range(2):
                for half in range(2):
                    ringV.close(pe.matmul(ringV.open(pe), Ke[0][0:RANK, m * P:(m + 1) * P],
                                          Ke[1][0:RANK, half * HALF:(half + 1) * HALF], start=True, stop=True))
            for n in range(2):
                w = weights(f"ada{4 + n}")
                ringA.close(chain(ringA.open(pe), [(cact[:, k:k + 1].to_broadcast([P, P]), w[:, k, :]) for k in range(NK)]))
                used(f"ada{4 + n}")
            emptied()
            linear("a")
            next_phase()
            product_fm("b_qf", 512, fm_fills(4))
            product_tm("b_v", 256, tm_fills())
            emptied()
            linear("b")
            next_phase()

            Q, K, V, Z, L, R = sb_area()
            pe.wait_ge(stick_in[0], 16)
            for h, c, part in sb_order():
                pair, d, z, l = h // 2, slice(64 * (h % 2), 64 * (h % 2) + 64), Z[c], L[c]
                if part == "logits":
                    if h == 2:
                        pe.wait_ge(stick_in[2], 16)
                    for at, j, t0, above in sb_blocks(c):
                        bank = ringA.open(pe)
                        ringA.close(pe.matmul(bank[:, t0:HALF], K[d, pair, j * P:(j + 1) * P],
                                              Q[d, pair, c * HALF + t0:(c + 1) * HALF], start=True, stop=True))
                    continue
                for at, j, t0, above in sb_blocks(c) if part == "weights" else ():
                    hear("dve")
                    bank = ringV.open(pe)
                    ins = pe.matmul(bank[:, t0:HALF], const("negtri"), l[:, at, t0:HALF], start=True, stop=(at == 0))
                    if at:
                        hear("pool")
                        ins = pe.matmul(bank[:, above:HALF], const("negones"), R[:, len(stick_sums_used) % 2, above:HALF],
                                        start=False, stop=True)
                    ringV.close(ins)
                    if at:
                        stick_sums_used.append(ringV.filled)
                if part == "weights":
                    continue
                stick_weights.hear(pe)
                pe.wait_ge(stick_in[1], 16)
                bank = ringA.open(pe)
                for tb in range(4):
                    n = 4 * c + 4
                    ins = chain(bank[:, tb * 64:tb * 64 + 64],
                                [(z[:, n - 1 - j, tb * P:(tb + 1) * P], V[:, j, h * 64:h * 64 + 64])
                                 for j in range(4 * c + tb + 1)])
                ringA.close(ins)
            next_phase()

            for i in range(NT + 1):
                if i < NT:
                    product_tm("a_gate", 512, [(i, ringA)])
                    product_tm("bc_gate", 512, [(i, ringA)])
                if i:
                    hear("dve")
                    turn_tile(i - 1, O[:, i - 1, :], ringA)
            emptied()
            projected(("out0", "out1"), NORMED, 1)
            next_phase()

            product_fm("att_q", 512, fm_fills(4))
            product_fm("att_kv", P, fm_fills(1))
            product_tm("att_kv", P, tm_fills(), at=P)
            emptied()
            QA, KA, VT, S, PT = att_area()
            for n in range(NT + 1):
                if n < NT:
                    o = att_range(n)
                    for kv in range(KV_HEADS):
                        d = slice(64 * kv, 64 * kv + 64)
                        for mm in range(2):
                            bank = ringV.open(pe)
                            for x in range(2):
                                ins = pe.matmul(bank[:, 256 * x + o:256 * x + 256], QA[d, 2 * mm + x, n * P:(n + 1) * P],
                                                KA[d, (n - 1) * P + o:(n + 1) * P], start=True, stop=True)
                            ringV.close(ins)
                    product_tm("ml_v", 512, [(n, ringA)])
                if n:
                    b, o = n - 1, att_range(n - 1)
                    hear("dve")
                    turns = [(h, kb) for h in range(ATT_HEADS) for kb in range(o // P, 2)]
                    for at in range(0, len(turns), 4):
                        bank = ringA.open(pe)
                        for x, (h, kb) in enumerate(turns[at:at + 4]):
                            ins = pe.transpose(bank[:, x * P:(x + 1) * P], S[b % 2][:, h, kb * P:(kb + 1) * P],
                                               const("ident"))
                        ringA.close(ins)
                    pe.wait_ge(ringA.free, ringA.filled)
                    bank = ringV.open(pe)
                    for h in range(ATT_HEADS):
                        kv = h // 4
                        ins = chain(bank[:, h * 64:h * 64 + 64],
                                    [(PT[:, turns.index((h, kb)), :], VT[:, b - 1 + kb, kv * 64:kv * 64 + 64])
                                     for kb in range(o // P, 2)])
                    ringV.close(ins)
            next_phase()

            n = IF_STEP + ML_HEADS
            product_fm("ml_if", n, [(0, half, ringV) for half in range(2)])
            product_fm("ml_q", 512, [(m, half, ringV) for m in range(4) for half in range(2)])
            product_fm("ml_k", 512, [(m, half, ringV) for m in range(4) for half in range(2)])
            QK, VM, NMB, DM, QR, KW, C, HB = ml_area()
            MROW = gate_row
            hear("dve")
            bank = ringV.open(pe)
            for i in range(NT):
                for x, row in enumerate((KW, NMB, MROW)):
                    at = (3 * i + x) * ML_HEADS
                    ins = pe.transpose(bank[:, at:at + ML_HEADS], row[0:ML_HEADS, i * P:(i + 1) * P],
                                       const("ident", ML_HEADS)[:, 0:ML_HEADS])
            ringV.close(ins)
            emptied()

            def maxima_of(h):
                for half in range(2):
                    ringA.close(pe.matmul(ringA.open(pe), const("sel", ML_HEADS)[:, h * P:(h + 1) * P],
                                          MROW[0:ML_HEADS, half * HALF:(half + 1) * HALF], start=True, stop=True))

            def scores_of(h):
                for half in range(2):
                    bank = ringV.open(pe)
                    for j in range(4):
                        t = slice(half * HALF + j * P, half * HALF + (j + 1) * P)
                        ins = pe.matmul(bank[:, j * P:(j + 1) * P], QK[:, 4 + h, t], QK[:, h, t], start=True, stop=True)
                    ringV.close(ins)
                for half in range(2):
                    bank = ringV.open(pe)
                    for j in range(4):
                        t = slice(half * HALF + j * P, half * HALF + (j + 1) * P)
                        ins = pe.transpose(bank[:, j * P:(j + 1) * P], QK[:, 4 + h, t], const("ident"))
                    ringV.close(ins)

            maxima_of(0)
            hear("act")
            scores_of(0)
            for h in range(ML_HEADS):
                pe.wait_ge(ringV.free, ringV.filled)
                if h + 1 < ML_HEADS:
                    maxima_of(h + 1)
                for j in range(0, NT - 1, 2):
                    bank = ringV.open(pe)
                    for x in range(min(2, NT - 1 - j)):
                        ins = pe.matmul(bank[:, x * VA:(x + 1) * VA], cut(KW, NT)[:, j + x, :], VM[:, j + x, h, :],
                                        start=True, stop=True)
                    ringV.close(ins)
                if h + 1 < ML_HEADS:
                    scores_of(h + 1)
                hear("dve")
                nmb, dm, qr, _, _ = head_area(h)
                for j in range(0, NT, 2):
                    bank = ringA.open(pe)
                    for x in range(2):
                        to = bank[:, x * VA:(x + 1) * VA]
                        t = slice((j + x) * P, (j + x + 1) * P)
                        ins = pe.matmul(to, dm[:, t], VM[:, j + x, h, :], start=True, stop=(j + x == 0))
                        if j + x:
                            ins = pe.matmul(to, qr[:, t], C[:, j + x, :], start=False, stop=True)
                    ringA.close(ins)
            next_phase()

            for i in range(NT + 2):
                if i < NT:
                    product_tm("ml_gate", 512, [(i, ringA)])
                if i >= 2:
                    hear("dve")
                    turn_tile(i - 2, O[:, i - 2, :], ringA)
            emptied()
            projected(("out2_0", "out2_1"), NORMED2, 1)
            next_phase()

            CQ, M2, MT, CK, CV, S, PT, OT = cross_area()
            product_fm("cross_q", 512, fm_fills(4))
            hear("dve")
            for f in range(NK):
                bank = ringV.open(pe)
                for q in range(2):
                    ins = pe.transpose(bank[:, q * P:(q + 1) * P], M2[:, q, f * P:(f + 1) * P], const("ident"))
                ringV.close(ins)
            emptied()
            w = weights("cross_k")
            for m in range(4):
                ringA.close(chain(ringA.open(pe)[:, 0:MEM], [(w[:, k, m * P:(m + 1) * P], MT[:, k, :]) for k in range(NK)]))
            used("cross_k")
            product_tm("cross_v", 512, [(i, ringA) for i in range(2)], x=MT)
            emptied()
            attended, turned_banks = [], []
            n = chunk_of["cross_out"] % 3
            weights("cross_out")
            w_co_slot = cut(slots[:, n * NK * HALF:(n + 1) * NK * HALF], 4)
            for n in range(NT + 3):
                if n < NT:
                    for x in range(2):
                        bank = ringV.open(pe)
                        for y in range(2):
                            h = 2 * x + y
                            ins = pe.matmul(bank[:, y * MEM:(y + 1) * MEM], CQ[:, h, n * P:(n + 1) * P], CK[:, h, :],
                                            start=True, stop=True)
                        ringV.close(ins)
                if 1 <= n <= NT:
                    b = n - 1
                    hear("dve")
                    for x in range(2):
                        bank = ringA.open(pe)
                        for y in range(4):
                            h, m = 2 * x + y // 2, y % 2
                            ins = pe.transpose(bank[:, y * P:(y + 1) * P], S[b % 2][:, h, m * P:(m + 1) * P],
                                               const("ident"))
                        ringA.close(ins)
                if 2 <= n <= NT + 1:
                    pe.wait_ge(ringA.free, attended[n - 2])
                    for half in range(2):
                        ringV.close(chain(ringV.open(pe), [(OT[:, k, (n - 2) * P:(n - 1) * P],
                                                            w_co_slot[:, k, half * HALF:(half + 1) * HALF])
                                                           for k in range(4)]))
                    used("cross_out")
                if 1 <= n <= NT:
                    pe.wait_ge(ringA.free, ringA.filled)
                    bank = ringA.open(pe)
                    for h in range(4):
                        ins = chain(bank[:, h * P:(h + 1) * P],
                                    [(CV[:, m, h * P:(h + 1) * P], PT[:, 2 * h + m, :]) for m in range(2)])
                    ringA.close(ins)
                    attended.append(ringA.filled)
                if n >= 3:
                    normed_ready.hear(pe)
                    turn_tile(n - 3, NORMED3[n % 3], ringV)
                    turned_banks.append(ringV.filled)
                if n == NT:
                    pe.wait_ge(ringV.free, turned_banks[3])
                    product_fm("router", ROUTES, [(0, 0, ringA)])
            next_phase()

            product_fm("router", ROUTES, [(0, 1, ringA)])
            emptied()
            bank = ringV.open(pe)
            for i in range(NT):
                ins = pe.transpose(bank[:, i * ROUTES:(i + 1) * ROUTES], LOGITS[:, i * P:(i + 1) * P],
                                   const("ident", ROUTES)[:, 0:ROUTES])
            ringV.close(ins)
            hear("dve")
            bank = ringV.open(pe)
            for i in range(NT):
                to = bank[:, i * EXPERTS:(i + 1) * EXPERTS]
                ins = pe.matmul(to, const("strict"), A2[:, i, :], start=True, stop=(i == 0))
                if i:
                    ins = pe.matmul(to, const("ones"), AC[:, i, :], start=False, stop=True)
            ins = pe.matmul(bank[:, NT * EXPERTS:(NT + 1) * EXPERTS], const("ones"), AC9, start=True, stop=True)
            ringV.close(ins)
            hear("pool")
            ringV.close(pe.transpose(ringV.open(pe)[:, 0:BLOCKS], TOKF[0:BLOCKS, :], const("ident", BLOCKS)[:, 0:BLOCKS]))
            next_phase()

            A0, A1, V0, V1, V2, V3 = banks[0], banks[1], banks[4], banks[5], banks[6], banks[7]

            def turn_block(x, last):
                for half, bank in ((0, V1), (1, V2)):
                    for q in range(4):
                        f = 4 * half + q
                        ins = pe.transpose(bank[:, q * P:(q + 1) * P], XG[x][:, f * P:(f + 1) * P], const("ident"))
                ins.then_inc(last, 1)

            def hidden_products(w, bank, x, last):
                for f in range(DE // P):
                    ins = chain(bank[:, f * P:(f + 1) * P], [(w[:, k, f * P:(f + 1) * P], XT[x][:, k, :]) for k in range(NK)])
                ins.then_inc(last, 1)

            def down_products(w, last0, last1):
                for half, bank, last in ((0, A1, last0), (1, V3, last1)):
                    chain(bank, [(HID[:, f * P:(f + 1) * P], w[:, f, half * HALF:(half + 1) * HALF])
                                 for f in range(DE // P)]).then_inc(last, 1)

            pe.wait_ge(rows_gathered[0], 16)
            turn_block(0, tokens_turned)
            with pe.Fori(0, EXPERTS // 2) as it:
                for x in range(2):
                    wg, wu, wd = expert_weights(x)
                    pe.wait_ge(tokens_ready, it * 4 + 2 * (x + 1))
                    pe.wait_ge(weights_in[x][0], it * 16 + 16)
                    hidden_products(wg, A0, x, gate_full)
                    pe.wait_ge(weights_in[x][1], it * 16 + 16)
                    hidden_products(wu, V0, x, up_full)
                    pe.wait_ge(rows_gathered[1 - x], it * 16 + 16 * (x + 1))
                    turn_block(1 - x, tokens_turned)
                    pe.wait_ge(hidden_ready, it * 2 + x + 1)
                    pe.wait_ge(weights_in[x][2], it * 16 + 16)
                    pe.wait_ge(y0_out, it * 2 + x + 1)
                    pe.wait_ge(y1_out, it * 2 + x + 1)
                    down_products(wd, down0_full, down1_full)
            spare = spare_count(pe)
            with pe.If(spare > 0):
                with pe.Fori(0, spare) as s:
                    wg, wu, wd = expert_weights(0)
                    pe.wait_ge(sp_rows, s * 16 + 16)
                    turn_block(0, sp_turned)
                    pe.wait_ge(sp_ready, s * 2 + 2)
                    pe.wait_ge(sp_weights, s * 48 + 48)
                    hidden_products(wg, A0, 0, sp_gate)
                    hidden_products(wu, V0, 0, sp_up)
                    pe.wait_ge(sp_hidden, s + 1)
                    down_products(wd, sp_down0, sp_down1)
            pe.nop()

        @block.scalar
        def _(act):
            line = Line(act, act_own)
            phases = [0]

            def tell(who):
                words["act", who].tell(act)

            def hear(who):
                words[who, "act"].hear(act)

            def empty(fn):
                bank = ringA.take(act)
                line(fn(bank), ringA.free)

            def func(o, i, f, bias=0.0, scale=1.0, **more):
                return act.activation(o, i, f, bias=bias, scale=scale, **more)

            def do(*args, **more):
                line(func(*args, **more))

            def next_phase():
                phases[0] += 1
                act.sem_inc(phase, 1)
                act.wait_ge(phase, 4 * phases[0])

            def log_sigmoid_part(x, tmp):
                act.preload_act_table_set("natural_log_exp_and_others")
                do(tmp, x, ACT.Abs)
                do(tmp, tmp, ACT.Exp, scale=-1.0)
                do(tmp, tmp, ACT.Ln, bias=1.0)

            def squares(half, junk, scale=None):
                for i in range(4 * half, 4 * half + 4):
                    if i % 2 == 0 and scale is not None:
                        act.wait_ge(dma_in[i // 2], scale)
                    do(junk, O[:, i, :], ACT.Square, accum_out=ss[:, i:i + 1])
                tell("dve")
                hear("dve")
                do(rstd[:, 4 * half:4 * half + 4], rstd[:, 4 * half:4 * half + 4], ACT.Sqrt)
                tell("dve")

            def turned(scale=None, bias=None):
                for half, f, ring in turn_fills():
                    if ring is ringA:
                        to = HT[:, f, half * HALF:(half + 1) * HALF]
                        if scale is None:
                            empty(lambda b: func(to, b, ACT.Copy))
                        else:
                            empty(lambda b: func(to, b, ACT.Identity, scale=scale[:, f:f + 1],
                                                 bias=0.0 if bias is None else bias[:, f:f + 1]))

            def turned_tile(i):
                for half in range(2):
                    empty(lambda b: func(HT[:, 4 * half:4 * half + 4, i * P:(i + 1) * P], cut(b, 4), ACT.Copy))

            def root_of(i, junk):
                square_of(i, junk)
                take_root(i)

            def square_of(i, junk):
                hear("dve")
                do(junk, O[:, i, :], ACT.Square, accum_out=ss[:, i:i + 1])
                roots.tell(act)

            def take_root(i):
                hear("dve")
                do(rstd[:, i:i + 1], rstd[:, i:i + 1], ACT.Sqrt)
                roots.tell(act)

            with nc.allow_non_contiguous_dma(reason="columns of small weights"):
                k_cols = lambda n: A[n].rearrange("a (k p) -> p (a k)", p=P)
                small_loads = [
                    (bcol, A["b_ada"][:, 0:2 * D].rearrange("a (k p) -> p (a k)", p=P)),
                    (bgate, k_cols("b_gla_gate")),
                    (gla_w, A["gla_norm_w"].partition_broadcast(P)),
                    (hgrn_w, A["hgrn_norm_w"].partition_broadcast(P)),
                    (masks, A["masks"]),
                    (sinks, A["att_sinks_2"].partition_broadcast(P)),
                    (b_if[0:ML_HEADS, :], A["b_gates_2"].rearrange("a (c p) -> p (a c)", p=ML_HEADS)),
                    (conv_b, k_cols("conv_b_2")),
                    (lg_bias[:, 0:GROUPS], A["b_router_group_2"].partition_broadcast(P)),
                    (lg_bias[:, GROUPS:], A["b_router_expert_2"].partition_broadcast(P)),
                    (conv_w, A["conv_w_2"].rearrange("a t (k p) -> p (a t k)", p=P)),
                ] + [(normcols[n], k_cols(n)) for n in normcols]
                for to, of in ((ccol, k_cols("c")), (cst, A["consts"])):
                    act.dma_start(to, of).then_inc(first_loaded, 16)
                for to, of in small_loads:
                    act.dma_start(to, of).then_inc(loaded, 16)
            act.wait_ge(first_loaded, 32)
            do(cact, ccol, ACT.Silu)
            tell("pe")
            junk = work[:, 1024:2048]
            hear("dve")
            squares(0, junk, 16)
            squares(1, junk, 16)
            act.wait_ge(loaded, 16 * len(small_loads))
            tell("dve")
            hear("dve")
            turned(mod[:, 8:16], mod[:, 0:8])
            next_phase()

            def linear(name):
                dv, o0 = LIN[name]
                Q, K, G, V, E, Qe, Ke, S = lin_area()
                done = [0]

                def ahead():
                    n = done[0]
                    x, k = n % 2, n // 2 + (4 if name == "b" else 0)
                    if k:
                        act.wait_ge(stage_stored[x], 16 * k)
                    cols, at = (HALF, n * HALF) if name == "a" else (256, 4 * T + n * 256)
                    to, scale = stages[x][:, 0:cols // P, :], (DK ** -0.5 if name == "a" and n < 4 else 1.0)
                    empty(lambda b: func(to, cut(b[:, 0:cols], cols // P), ACT.Copy, scale=scale))
                    act.dma_start(cut(ahead_dram[:, at:at + cols], cols // P), to).then_inc(stage_stored[x], 16)
                    done[0] += 1

                for pair in range(2):
                    B = G[:, pair]
                    for lvl in range(LEVELS):
                        hear("pool")
                        do(E[lvl % 3], E[lvl % 3], ACT.Abs)
                        do(E[lvl % 3], E[lvl % 3], ACT.Exp, scale=-1.0)
                        tell("dve")
                        tell("pool")
                        if lvl in (2, 5):
                            ahead()
                    hear("pool")
                    do(E[0], E[0], ACT.Exp)
                    do(E[1], cut(B, NT), ACT.Exp)
                    do(decay, cut(B, NT)[:, :, P - 1], ACT.Exp)
                    tell("dve")
                    tell("pool")
                    ahead()
                    for half in range(2):
                        if half == 0:
                            hear("dve")
                        to = Qe[1][:, half * HALF:(half + 1) * HALF]
                        empty(lambda b: func(to, b, ACT.Copy))
                    ahead()
                    per = HALF // dv
                    for hh in range(2):
                        for j0 in range(0, NT, per):
                            at = o0 + (2 * pair + hh) * dv
                            empty(lambda b: func(O[:, j0:j0 + per, at:at + dv], cut(b, per), ACT.Copy))
                    tell("dve")
                    tell("pool")

            Q, K, G, V, E, Qe, Ke, S = lin_area()
            for m, half, ring in fm_fills(4):
                if ring is ringA:
                    t = slice(half * HALF, (half + 1) * HALF)
                    if m < 2:
                        empty(lambda b: func(Q[:, m, t], b, ACT.Copy, scale=DK ** -0.5))
                    else:
                        empty(lambda b: func(K[:, m - 2, t], b, ACT.Copy))
            for i, ring in tm_fills():
                if ring is ringA:
                    empty(lambda b: func(V[:, i, :], b, ACT.Copy))
            act.dma_start(Ke[0][0:RANK, 0:2 * P], A["w_gla_gate2"].rearrange("a r n -> (a r) n")).then_inc(loaded, 16)
            act.wait_ge(loaded, 16 * (len(small_loads) + 1))
            empty(lambda b: func(Ke[1][0:RANK, 0:HALF], b[0:RANK, :], ACT.Copy))
            hear("dve")
            for pair in range(2):
                log_sigmoid_part(cut(G[:, pair], NT), E[pair])
            tell("dve")
            for n in range(2):
                empty(lambda b: func(gate_row[:, n * HALF:(n + 1) * HALF], b, ACT.Copy))
            linear("a")
            next_phase()

            for m, half, ring in fm_fills(4):
                if ring is ringA:
                    t = slice(half * HALF, (half + 1) * HALF)
                    if m < 2:
                        empty(lambda b: func(Q[:, m, t], b, ACT.Silu))
                    else:
                        empty(lambda b: func(G[:, m - 2, t], b, ACT.Copy))
            hear("dve")
            for m in range(2):
                do(Q[:, m, HALF:T], Q[:, m, HALF:T], ACT.Silu)
            for m in range(2):
                do(K[:, m], G[:, m], ACT.Sigmoid, scale=-1.0)
            for m in range(2):
                log_sigmoid_part(cut(G[:, m], NT), E[m])
            tell("dve")
            for i, ring in tm_fills():
                if ring is ringA:
                    empty(lambda b: func(V[:, i, 0:256], b[:, 0:256], ACT.Copy))
            linear("b")
            next_phase()

            Q, K, V, Z, L, R = sb_area()
            for x in range(2):
                act.wait_ge(stage_stored[x], 16 * 8)
            qk = ahead_dram[:, 0:4 * T].rearrange("p (a m t) -> p a m t", a=2, m=2)
            to = work[:, 0:4 * T].rearrange("p (a m t) -> p a m t", a=2, m=2)
            act.dma_start(to[:, :, 0], qk[:, :, 0]).then_inc(stick_in[0], 16)
            act.dma_start(work[:, 4 * T:4 * T + NT * 256], ahead_dram[:, 4 * T:]).then_inc(stick_in[1], 16)
            act.dma_start(to[:, :, 1], qk[:, :, 1]).then_inc(stick_in[2], 16)
            act.preload_act_table_set("natural_log_exp_and_others")
            for h, c, part in sb_order():
                blocks, z, l = sb_blocks(c), Z[c], L[c]
                if part == "logits":
                    for n in range(len(blocks) + 2):
                        if n < len(blocks):
                            at, _, t0, _ = blocks[n]
                            empty(lambda b: func(z[:, at, t0:HALF], b[:, t0:HALF], ACT.Copy))
                            tell("dve")
                        if n >= 2:
                            at, _, t0, _ = blocks[n - 2]
                            hear("dve")
                            do(l[:, at, t0:HALF], l[:, at, t0:HALF], ACT.Exp, scale=-1.0)
                            do(l[:, at, t0:HALF], l[:, at, t0:HALF], ACT.Ln, bias=1.0)
                            tell("dve")
                    continue
                if part == "weights":
                    for at, j, t0, above in blocks:
                        hear("dve")
                        do(z[:, at, t0:HALF], z[:, at, t0:HALF], ACT.Exp)
                        tell("dve")
                    continue
                empty(lambda b: func(O[:, 4 * c:4 * c + 4, SB0 + h * 64:SB0 + h * 64 + 64],
                                     cut(b[:, 0:256], 4), ACT.Copy))
            next_phase()

            hear("dve")
            do(rstd[:, :], rstd[:, :], ACT.Sqrt)
            tell("dve")
            for i in range(NT + 1):
                if i < NT:
                    if i >= len(GATES):
                        hear("dve")
                    for n in range(2):
                        empty(lambda b: func(GATES[i % len(GATES)][:, n * HALF:(n + 1) * HALF], b, ACT.Silu))
                    tell("dve")
                if i:
                    turned_tile(i - 1)
            for i in range(NT):
                root_of(i, GATES[0])
                root_of(i, GATES[0])
            next_phase()

            QA, KA, VT, S, PT = att_area()
            for m, half, ring in fm_fills(4):
                if ring is ringA:
                    empty(lambda b: func(QA[:, m, half * HALF:(half + 1) * HALF], b, ACT.Copy, scale=DK ** -0.5))
            empty(lambda b: func(KA[:, 0:HALF], b, ACT.Copy))
            for i, ring in tm_fills():
                if ring is ringA:
                    empty(lambda b: func(VT[:, i, :], b[:, 0:P], ACT.Copy))
            VM = ml_area()[1]
            for n in range(NT + 1):
                if n < NT:
                    o = att_range(n)
                    m = slice(8 * (n % 2), 8 * (n % 2) + 8)
                    hear("dve")
                    do(S[n % 2][:, :, o:2 * P], S[n % 2][:, :, o:2 * P], ACT.Exp)
                    do(es[:, m], es[:, m], ACT.Exp)
                    tell("dve")
                    empty(lambda b: func(VM[:, n, :, 0:ML_D], cut(b, ML_HEADS), ACT.Copy))
                if n:
                    turns = (2 if n > 1 else 1) * ATT_HEADS
                    for at in range(0, turns, 4):
                        empty(lambda b: func(PT[:, at:at + 4, :], cut(b, 4), ACT.Copy))
            next_phase()

            QK, VM, NMB, DM, QR, KW, C, HB = ml_area()
            hear("dve")
            log_sigmoid_part(QR[0:ML_HEADS, :], DM[0:ML_HEADS, :])
            tell("dve")
            for m in range(2 * ML_HEADS):
                hear("dve")
                do(QK[:, m], QK[:, m], ACT.Silu)
                if m < ML_HEADS:
                    do(QK[:, m], QK[:, m], ACT.Copy, scale=ML_D ** -0.5)
            tell("pe")
            hear("dve")
            do(cut(expm, NT), acm.rearrange("p (i x h) -> p i x h", i=NT, x=3)[:, :, 1, :], ACT.Exp, scale=-1.0)

            def decays_of(h):
                nmb, dm, qr, w, d = head_area(h)
                for half in range(2):
                    empty(lambda b: func(nmb[:, half * HALF:(half + 1) * HALF], b, ACT.Copy, scale=-1.0))
                tell("dve")
                hear("dve")
                do(dm, dm, ACT.Exp)
                do(w, w, ACT.Exp)
                do(d, d, ACT.Exp)
                do(qr[:, P:T], qr[:, P:T], ACT.Exp)
                tell("dve")

            decays_of(0)
            for h in range(ML_HEADS):
                if h:
                    hear("dve")
                if h + 1 < ML_HEADS:
                    decays_of(h + 1)
                for j in range(0, NT, 2):
                    empty(lambda b: func(HB[:, j:j + 2, :], cut(b[:, 0:2 * VA], 2), ACT.Copy))
                tell("dve")
            next_phase()

            for i in range(NT + 2):
                if i < NT:
                    empty(lambda b: func(GATES2[i % len(GATES2)], b, ACT.Sigmoid))
                    tell("dve")
                    hear("dve")
                    r = rstd[:, 5 * i:5 * i + 5]
                    do(r, r, ACT.Sqrt)
                    tell("dve")
                if i >= 2:
                    turned_tile(i - 2)
            for i in range(NT):
                root_of(i, work[:, 0:T])
            next_phase()

            CQ, M2, MT, CK, CV, S, PT, OT = cross_area()
            act.wait_ge(row_in, 80)
            for i in range(2):
                do(OT[:, i, :], M2[:, i, :], ACT.Square, accum_out=ss[:, 8 + i:9 + i])
            tell("dve")
            hear("dve")
            do(rstd[:, 8:10], rstd[:, 8:10], ACT.Sqrt)
            tell("dve")
            for m, half, ring in fm_fills(4):
                if ring is ringA:
                    empty(lambda b: func(CQ[:, m, half * HALF:(half + 1) * HALF], b, ACT.Copy, scale=P ** -0.5))
            for m in range(4):
                empty(lambda b: func(CK[:, m, :], b[:, 0:MEM], ACT.Copy))
            for i in range(2):
                empty(lambda b: func(CV[:, i, :], b, ACT.Copy))
            for n in range(NT + 3):
                if n < NT:
                    hear("dve")
                    do(S[n % 2], S[n % 2], ACT.Exp)
                    tell("dve")
                if n >= 3:
                    take_root(n - 3)
                if 1 <= n <= NT:
                    for x in range(2):
                        empty(lambda b: func(PT[:, 4 * x:4 * x + 4, :], cut(b, 4), ACT.Copy))
                    empty(lambda b: func(OT[:, :, (n - 1) * P:n * P], cut(b, 4), ACT.Copy))
                if 2 <= n <= NT + 1:
                    square_of(n - 2, MT.rearrange("p a b -> p (a b)")[:, 0:D])
                if n == NT:
                    empty(lambda b: func(LOGITS[:, 0:HALF], b[0:ROUTES, :], ACT.Copy))
            next_phase()

            empty(lambda b: func(LOGITS[:, HALF:T], b[0:ROUTES, :], ACT.Copy))
            hear("dve")
            do(GT, GT, ACT.Exp)
            do(R3, R3, ACT.Exp)
            tell("dve")
            next_phase()

            A0, A1 = banks[0], banks[1]
            with act.Fori(0, EXPERTS // 2) as it:
                for x in range(2):
                    act.wait_ge(gate_full, it * 2 + x + 1)
                    func(SILU, A0, ACT.Silu).then_inc(silu_ready, 1)
                    act.wait_ge(down0_full, it * 2 + x + 1)
                    act.wait_ge(y_stored[x], it * 16 + 16)
                    func(YO[x][:, 0:HALF], A1, ACT.Copy).then_inc(y0_out, 1)
                    act.wait_ge(y0_out, it * 2 + x + 2)
                    act.wait_ge(y1_out, it * 2 + x + 2)
                    act.dma_start(y_dram[bass.ds(it * 2 + x, 1)].rearrange("a p d -> p (a d)"), YO[x])\
                        .then_inc(y_stored[x], 16)
            for x in range(2):
                act.wait_ge(y_stored[x], 16 * (EXPERTS // 2 + 1))
            spare = spare_count(act)
            act.sem_inc(sp_over, 1)
            with act.If(spare > 0):
                with act.Fori(0, spare) as s:
                    act.wait_ge(sp_gate, s + 1)
                    func(SILU, A0, ACT.Silu).then_inc(sp_silu, 1)
                    act.wait_ge(sp_down0, s + 1)
                    func(YO[0][:, 0:HALF], A1, ACT.Copy).then_inc(sp_y0, 1)
                    act.wait_ge(sp_y0, s + 1)
                    act.wait_ge(sp_y1, s + 1)
                    act.dma_start(y_dram[bass.ds(s + EXPERTS, 1)].rearrange("a p d -> p (a d)"), YO[0])\
                        .then_inc(sp_stored, 16)
                    act.wait_ge(sp_stored, s * 16 + 16)
                    act.sem_inc(sp_over, 1)
            act.sem_inc(moe_over, 1)
            for i in range(NT + 1):
                if i < NT:
                    hear("dve")
                    do(YG[2 * i], O[:, i, :], ACT.Square, accum_out=ss[:, i:i + 1])
                    final_squares.tell(act)
                if i:
                    hear("dve")
                    do(rstd[:, i - 1:i], rstd[:, i - 1:i], ACT.Sqrt)
                    tell("dve")

        @block.vector
        def _(dve):
            line = Line(dve, dve_own)
            phases = [0]

            def tell(who):
                words["dve", who].tell(dve)

            def hear(who):
                words[who, "dve"].hear(dve)

            def empty(fn):
                bank = ringV.take(dve)
                line(fn(bank), ringV.free)

            def copy(o, i):
                line(dve.tensor_copy(o, i))

            def tt(o, a, b, op):
                line(dve.tensor_tensor(o, a, b, op))

            def ts(o, a, s1, s2, op0, *op1):
                line(dve.tensor_scalar(o, a, s1, s2, op0, *op1))

            def stt(o, a, s, b, op0, op1):
                line(dve.scalar_tensor_tensor(out=o, in0=a, scalar=s, in1=b, op0=op0, op1=op1))

            def bcast(ap, shape):
                return ap.to_broadcast(shape)

            def next_phase():
                phases[0] += 1
                dve.sem_inc(phase, 1)
                dve.wait_ge(phase, 4 * phases[0])

            def inverse_root(half, scale=1.0 / D):
                hear("act")
                r = rstd[:, 4 * half:4 * half + 4]
                ts(r, ss[:, 4 * half:4 * half + 4], scale, EPS, ALU.mult, ALU.add)
                line(dve.reciprocal(r, r))
                tell("act")
                hear("act")

            def normed(told=True):
                for half in range(2):
                    inverse_root(half)
                    for i in range(4 * half, 4 * half + 4):
                        ts(O[:, i, :], O[:, i, :], rstd[:, i:i + 1], None, ALU.mult)
                    if told:
                        tell("pe")

            def turned(scale=None, bias=None):
                for half, f, ring in turn_fills():
                    if ring is ringV:
                        to = HT[:, f, half * HALF:(half + 1) * HALF]
                        if scale is None:
                            empty(lambda b: dve.tensor_copy(to, b))
                        elif bias is None:
                            empty(lambda b: dve.tensor_scalar(to, b, scale[:, f:f + 1], None, ALU.mult))
                        else:
                            empty(lambda b: dve.tensor_scalar(to, b, scale[:, f:f + 1], bias[:, f:f + 1],
                                                              ALU.mult, ALU.add))

            def turned_tile(i, scale):
                for half in range(2):
                    k = slice(4 * half, 4 * half + 4)
                    empty(lambda b: dve.tensor_tensor(HT[:, k, i * P:(i + 1) * P], cut(b, 4),
                                                      bcast(scale[:, k].unsqueeze(2), [P, 4, P]), ALU.mult))

            def root(i):
                tell("act")
                root_at(i)

            def root_at(i):
                roots.hear(dve)
                r = rstd[:, i:i + 1]
                ts(r, ss[:, i:i + 1], 1.0 / D, EPS, ALU.mult, ALU.add)
                line(dve.reciprocal(r, r))
                tell("act")
                roots.hear(dve)

            line(dve.memset(one, 1.0))
            line(dve.memset(zero, 0.0))
            line(dve.memset(two_heads, 0.0))
            for hh in range(2):
                line(dve.memset(two_heads[64 * hh:64 * hh + 64, hh:hh + 1], 1.0))
            line(dve.memset(ss[:, :], 0.0))
            line(dve.memset(rstd[:, :], 1.0))
            tell("act")
            normed()
            for n in range(4):
                empty(lambda b: dve.tensor_copy(MODROW[:, n * HALF:(n + 1) * HALF], b[0:1, :]))
            tell("pe")
            hear("act")
            empty(lambda b: dve.tensor_tensor(mod, b[:, 0:16], bcol, ALU.add))
            ts(mod[:, 8:16], mod[:, 8:16], 1.0, None, ALU.add)
            tell("act")
            turned(mod[:, 8:16], mod[:, 0:8])
            next_phase()

            def linear(name):
                dv, o0 = LIN[name]
                Q, K, G, V, E, Qe, Ke, S = lin_area()
                for pair in range(2):
                    B = G[:, pair]
                    for j in range(NT):
                        g = B[:, j * P:(j + 1) * P]
                        line(dve.tensor_tensor_scan(g, bcast(one, [P, P]), g, 0.0, ALU.mult, ALU.add))
                    tell("pool")
                    if pair:
                        hear("act")

                    def itself():
                        empty(lambda b: dve.tensor_tensor(S, bcast(const("ident").unsqueeze(1), [P, 2 * NT, P]),
                                                          bcast(b[:, 0:2 * NT].unsqueeze(2), [P, 2 * NT, P]), ALU.mult))

                    def scores(lvl):
                        n = P >> lvl
                        m = cut(cut(masks, LEVELS + 1)[:, lvl, :], P // n)[:, :, n // 2:n]
                        for half in range(2):
                            s = S[:, 8 * half:8 * half + 8, :].rearrange("p j (a n) -> p j a n", n=n)[:, :, :, n // 2:n]
                            empty(lambda b: dve.copy_predicated(
                                s, bcast(m.unsqueeze(1), [P, NT, P // n, n // 2]),
                                b.rearrange("p (j a h) -> p j a h", j=NT, h=n // 2)))

                    for x in range(2):
                        for hh in range(2):
                            other = Qe[x].rearrange("p (j c h) -> p j c h", j=NT, c=2)[64 * hh:64 * hh + 64, :, 1 - hh]
                            line(dve.memset(other, 0.0))
                    itself()
                    for lvl in range(LEVELS):
                        n = P >> lvl
                        hear("act")
                        for hh in range(2):
                            d = slice(64 * hh, 64 * hh + 64)
                            to = Qe[lvl % 2].rearrange("p (j c a h) -> p j c a h", j=NT, c=2, h=n // 2)[d, :, hh]
                            q, e = (level(x[d], n)[:, :, :, n // 2:n] for x in (cut(Q[:, pair], NT), E[lvl % 3]))
                            tt(to, q, e, ALU.mult)
                        tell("pe")
                        tell("pool")
                        if lvl >= 1:
                            scores(lvl - 1)
                    scores(LEVELS - 1)
                    tell("pool")
                    hear("act")
                    tt(cut(Qe[0], NT), cut(Q[:, pair], NT), E[1], ALU.mult)
                    tell("act")
                    St = cut(Ke[1][:, 0:NT * dv], NT)
                    line(dve.memset(St[:, 0, :], 0.0))
                    per = HALF // dv
                    for j0 in range(0, NT - 1, per):
                        bank = ringV.take(dve)
                        n = min(j0 + per, NT - 1)
                        for j in range(j0, n):
                            ins = dve.scalar_tensor_tensor(
                                out=St[:, j + 1, :], in0=St[:, j, :], scalar=decay[:, j:j + 1],
                                in1=bank[:, (j - j0) * dv:(j - j0 + 1) * dv], op0=ALU.mult, op1=ALU.add)
                            line(ins, ringV.free if j == n - 1 else None)
                    tell("pe")
                hear("act")

            def copies(fills, to):
                for *at, ring in fills:
                    if ring is ringV:
                        dst, n = to(*at)
                        empty(lambda b: dve.tensor_copy(dst, b[:, 0:n]))

            Q, K, G, V, E, Qe, Ke, S = lin_area()
            for m, half, ring in fm_fills(4):
                if ring is ringV:
                    t = slice(half * HALF, (half + 1) * HALF)
                    if m < 2:
                        empty(lambda b: dve.tensor_scalar(Q[:, m, t], b, DK ** -0.5, None, ALU.mult))
                    else:
                        empty(lambda b: dve.tensor_copy(K[:, m - 2, t], b))
            copies(tm_fills(), lambda i: (V[:, i, :], 512))
            empty(lambda b: dve.tensor_copy(Ke[1][0:RANK, HALF:T], b[0:RANK, :]))
            for m in range(2):
                for half in range(2):
                    t = slice(half * HALF, (half + 1) * HALF)
                    empty(lambda b: dve.tensor_scalar(G[:, m, t], b, bgate[:, m:m + 1], None, ALU.add))
            tell("act")
            hear("act")
            for m in range(2):
                g = cut(G[:, m], NT)
                stt(g, g, 0.0, E[m], ALU.min, ALU.subtract)
                ts(G[:, m], G[:, m], 1.0 / TAU, None, ALU.mult)
            linear("a")
            next_phase()

            for m, half, ring in fm_fills(4):
                if ring is ringV:
                    t = slice(half * HALF, (half + 1) * HALF)
                    to = Q[:, m, t] if m < 2 else G[:, m - 2, t]
                    empty(lambda b: dve.tensor_copy(to, b))
            tell("act")
            copies(tm_fills(), lambda i: (V[:, i, 0:256], 256))
            hear("act")
            for m in range(2):
                g = cut(G[:, m], NT)
                stt(g, g, 0.0, E[m], ALU.min, ALU.subtract)
            linear("b")
            next_phase()

            Q, K, V, Z, L, R = sb_area()
            strict = const("strict")
            for h, c, part in sb_order():
                blocks, z, l = sb_blocks(c), Z[c], L[c]
                if part == "logits":
                    for n in range(len(blocks) + 2):
                        if n < len(blocks):
                            at, _, t0, _ = blocks[n]
                            hear("act")
                            stt(l[:, at, t0:HALF], z[:, at, t0:HALF], -1.0, z[:, at, t0:HALF], ALU.mult, ALU.max)
                            tell("act")
                        if n >= 2:
                            at, j, t0, _ = blocks[n - 2]
                            hear("act")
                            stt(l[:, at, t0:HALF], z[:, at, t0:HALF], 0.0, l[:, at, t0:HALF], ALU.max, ALU.add)
                            if j >= 4 * c:
                                tt(l[:, at, t0:t0 + P], l[:, at, t0:t0 + P], strict, ALU.mult)
                            tell("pe")
                            tell("pool")
                if part != "weights":
                    continue
                for at, j, t0, above in blocks:
                    zb = z[:, at, t0:HALF]
                    empty(lambda b: dve.tensor_tensor(zb, zb, b[:, t0:HALF], ALU.add))
                    tell("act")
                for at, j, t0, above in blocks:
                    hear("act")
                    if j >= 4 * c:
                        tt(z[:, at, t0:t0 + P], z[:, at, t0:t0 + P], strict, ALU.mult)
                stick_weights.tell(dve)
            next_phase()

            ssh, rh = cut(ss, NT), cut(rstd, NT)
            sq = work[:, 2 * HALF:2 * HALF + SB0]
            NG = GLA_HEADS * GLA_DV
            for i in range(NT):
                o = O[:, i, 0:SB0]
                tt(sq, o, o, ALU.mult)
                line(dve.tensor_reduce(ssh[:, i, 0:4], cut(sq[:, 0:NG], 4), AX_X, ALU.add))
                line(dve.tensor_reduce(ssh[:, i, 4:8], cut(sq[:, NG:SB0], 4), AX_X, ALU.add))
            ts(rh[:, :, 0:4], ssh[:, :, 0:4], 1.0 / GLA_DV, EPS, ALU.mult, ALU.add)
            ts(rh[:, :, 4:8], ssh[:, :, 4:8], 1.0 / HGRN_DV, EPS, ALU.mult, ALU.add)
            line(dve.reciprocal(rstd[:, :], rstd[:, :]))
            tell("act")
            hear("act")
            for i in range(NT):
                for at, n, dv, w in ((0, 0, GLA_DV, gla_w), (NG, 4, HGRN_DV, hgrn_w)):
                    o = cut(O[:, i, at:at + 4 * dv], 4)
                    tt(o, o, bcast(rh[:, i, n:n + 4].unsqueeze(2), [P, 4, dv]), ALU.mult)
                    tt(o, o, bcast(w.unsqueeze(1), [P, 4, dv]), ALU.mult)
                hear("act")
                tt(O[:, i, :], O[:, i, :], GATES[i % len(GATES)], ALU.mult)
                tell("pe")
                if i + len(GATES) < NT:
                    tell("act")
            dve.wait_ge(row_in, 32)
            tt(gate_row, gate_row, BIAS_ROW, ALU.add)
            for i in range(NT + 1):
                if i < NT:
                    if i % 2 == 0:
                        dve.wait_ge(dma_in[i // 2], 32)
                    for n in range(2):
                        c = slice(n * HALF, (n + 1) * HALF)
                        empty(lambda b: dve.tensor_tensor(O[:, i, c], b, gate_row[:, c], ALU.mult))
                    tt(O[:, i, :], O[:, i, :], X[:, i, :], ALU.add)
                    root(i)
                    stt(O[:, i, :], O[:, i, :], rstd[:, i:i + 1], ROW, ALU.mult, ALU.mult)
                    tell("pool")
                    root(i)
                    ts(NORMED[i % 2], O[:, i, :], rstd[:, i:i + 1], None, ALU.mult)
                    tell("pe")
                if i:
                    turned_tile(i - 1, normcols["norm_mix_2"])
            next_phase()

            QA, KA, VT, S, PT = att_area()
            for m, half, ring in fm_fills(4):
                if ring is ringV:
                    empty(lambda b: dve.tensor_scalar(QA[:, m, half * HALF:(half + 1) * HALF], b, DK ** -0.5, None, ALU.mult))
            empty(lambda b: dve.tensor_copy(KA[:, HALF:T], b))
            copies(tm_fills(), lambda i: (VT[:, i, :], P))
            for n in range(NT + 1):
                if n < NT:
                    o, s = att_range(n), S[n % 2]
                    m = slice(8 * (n % 2), 8 * (n % 2) + 8)
                    for kv in range(KV_HEADS):
                        for mm in range(2):
                            bank = ringV.take(dve)
                            for x in range(2):
                                h = 4 * kv + 2 * mm + x
                                line(dve.scalar_tensor_tensor(
                                    out=s[:, h, o:2 * P], in0=const("dist")[:, o:2 * P],
                                    scalar=2.0 ** (-8.0 * (h + 1) / ATT_HEADS), in1=bank[:, 256 * x + o:256 * x + 256],
                                    op0=ALU.mult, op1=ALU.add), ringV.free if x else None)
                    line(dve.tensor_reduce(mx[:, m], s[:, :, o:2 * P], AX_X, ALU.max))
                    tt(mx[:, m], mx[:, m], sinks, ALU.max)
                    tt(es[:, m], sinks, mx[:, m], ALU.subtract)
                    tt(s[:, :, o:2 * P], s[:, :, o:2 * P], bcast(mx[:, m].unsqueeze(2), [P, ATT_HEADS, 2 * P - o]),
                       ALU.subtract)
                    tell("act")
                if n:
                    o, s = att_range(n - 1), S[(n - 1) % 2]
                    m = slice(8 * ((n - 1) % 2), 8 * ((n - 1) % 2) + 8)
                    hear("act")
                    tell("pe")
                    line(dve.tensor_reduce(rden[:, m], s[:, :, o:2 * P], AX_X, ALU.add))
                    tt(rden[:, m], rden[:, m], es[:, m], ALU.add)
                    line(dve.reciprocal(rden[:, m], rden[:, m]))
                    empty(lambda b: dve.tensor_tensor(cut(O[:, n - 1, 0:512], ATT_HEADS), cut(b, ATT_HEADS),
                                                      bcast(rden[:, m].unsqueeze(2), [P, ATT_HEADS, 64]), ALU.mult))
            next_phase()

            QK, VM, NMB, DM, QR, KW, C, HB = ml_area()
            at_c = 2 * ML_HEADS * T + 4 * T + NT * ML_HEADS * VA
            raw = [work[:, at_c:at_c + T + 3], work[:, at_c + T + 3:at_c + 2 * T + 6]]
            cw = cut(conv_w, TAPS)
            line(dve.memset(VM[:, :, :, ML_D:VA], 1.0))
            heads = slice(0, ML_HEADS)
            for half in range(2):
                bank = ringV.take(dve)
                for row, x in ((KW, 0), (QR, 1)):
                    line(dve.tensor_scalar(row[heads, half * HALF:(half + 1) * HALF],
                                           bank[x * IF_STEP:x * IF_STEP + ML_HEADS, :], b_if[heads, x:x + 1], None, ALU.add),
                         ringV.free if x else None)
            tell("act")
            for m in range(2 * ML_HEADS):
                if m == 1:
                    hear("act")
                    F, a, MROW, MT_ROW = QR[heads, :], KW[heads, :], gate_row[heads, :], NMB[heads, :]
                    stt(F, F, 0.0, DM[heads, :], ALU.min, ALU.subtract)
                    line(dve.tensor_tensor_scan(F, bcast(one[heads, :], [ML_HEADS, T]), F, 0.0, ALU.mult, ALU.add))
                    tt(a, a, F, ALU.subtract)
                    line(dve.tensor_tensor_scan(MROW, a, bcast(zero[heads, :], [ML_HEADS, T]), 0.0, ALU.max, ALU.add))
                    tt(MT_ROW, MROW, F, ALU.add)
                    tell("pe")
                r = raw[m % 2]
                line(dve.memset(r[:, 0:TAPS - 1], 0.0))
                for half in range(2):
                    empty(lambda b: dve.tensor_copy(r[:, TAPS - 1 + half * HALF:TAPS - 1 + (half + 1) * HALF], b))
                ts(QK[:, m], r[:, TAPS - 1:TAPS - 1 + T], cw[:, TAPS - 1, m:m + 1], conv_b[:, m:m + 1], ALU.mult, ALU.add)
                for k in range(TAPS - 1):
                    stt(QK[:, m], r[:, k:k + T], cw[:, k, m:m + 1], QK[:, m], ALU.mult, ALU.add)
                tell("act")
            empty(lambda b: dve.tensor_copy(acm, b[:, 0:NT * 3 * ML_HEADS]))
            tell("act")
            acm4 = acm.rearrange("p (i x h) -> p i x h", i=NT, x=3)
            kw, causal = cut(KW, NT), const("causal")

            def decays_of(h):
                NMBh, DMh, QRh, wcol, dcol = head_area(h)
                nmb, dm, qr = cut(NMBh, NT), cut(DMh, NT), cut(QRh, NT)
                hear("act")
                a_h = acm4[:, :, 0, h]
                tt(dm, nmb, bcast(a_h.unsqueeze(2), [P, NT, P]), ALU.add)
                ts(DMh, DMh, 0.0, None, ALU.min)
                tt(wcol, a_h, nmb[:, :, P - 1], ALU.add)
                line(dve.memset(dcol[:, 0:1], 0.0))
                tt(dcol[:, 1:NT], nmb[:, 1:NT, P - 1], nmb[:, 0:NT - 1, P - 1], ALU.subtract)
                tt(qr[:, 1:NT, :], nmb[:, 1:NT, :], bcast(nmb[:, 0:NT - 1, P - 1:P], [P, NT - 1, P]), ALU.subtract)
                tell("act")

            def decayed(h):
                NMBh, DMh, QRh, wcol, dcol = head_area(h)
                dm = cut(DMh, NT)
                hear("act")
                tt(dm, dm, bcast(causal.unsqueeze(1), [P, NT, P]), ALU.mult)
                for half in range(2):
                    d = DMh[:, half * HALF:(half + 1) * HALF]
                    empty(lambda b: dve.tensor_tensor(d, d, b, ALU.mult))
                tt(QRh[:, P:T], QRh[:, P:T], QK[:, h, P:T], ALU.mult)
                for half in range(2):
                    j = slice(4 * half, 4 * half + 4)
                    empty(lambda b: dve.tensor_tensor(kw[:, j, :], cut(b, 4), bcast(wcol[:, j].unsqueeze(2), [P, 4, P]),
                                                      ALU.mult))

            decays_of(0)
            decayed(0)
            for h in range(ML_HEADS):
                if h + 1 < ML_HEADS:
                    decays_of(h + 1)
                dcol = dcols[h % 2]
                for j0 in range(0, NT - 1, 2):
                    bank = ringV.take(dve)
                    n = min(2, NT - 1 - j0)
                    for x in range(n):
                        j, u = j0 + x, bank[:, x * VA:(x + 1) * VA]
                        if j == 0:
                            line(dve.tensor_copy(C[:, 1, :], u))
                        else:
                            line(dve.scalar_tensor_tensor(out=C[:, j + 1, :], in0=C[:, j, :], scalar=dcol[:, j:j + 1],
                                                          in1=u, op0=ALU.mult, op1=ALU.add),
                                 ringV.free if x == n - 1 else None)
                tell("pe")
                if h + 1 < ML_HEADS:
                    decayed(h + 1)
                hear("act")
                stt(den, HB[:, :, ML_D], -1.0, HB[:, :, ML_D], ALU.mult, ALU.max)
                tt(den, den, cut(expm, NT)[:, :, h], ALU.max)
                line(dve.reciprocal(den, den))
                tt(O[:, :, 512 + h * ML_D:512 + (h + 1) * ML_D], HB[:, :, 0:ML_D], bcast(den.unsqueeze(2), [P, NT, ML_D]),
                   ALU.mult)
                if h + 1 < ML_HEADS:
                    tell("act")
            next_phase()

            ss5, r5 = cut(ss[:, 0:5 * NT], NT), cut(rstd[:, 0:5 * NT], NT)
            for i in range(NT):
                o, heads = O[:, i, 512:1024], cut(O[:, i, 512:1024], 4)
                hear("act")
                tt(o, o, GATES2[i % len(GATES2)], ALU.mult)
                tt(SQUARED, O[:, i, :], O[:, i, :], ALU.mult)
                line(dve.tensor_reduce(ss5[:, i, 0:1], SQUARED[:, 0:512], AX_X, ALU.add))
                line(dve.tensor_reduce(ss5[:, i, 1:5], cut(SQUARED[:, 512:1024], 4), AX_X, ALU.add))
                ts(r5[:, i, 0:1], ss5[:, i, 0:1], 1.0 / 512, EPS, ALU.mult, ALU.add)
                ts(r5[:, i, 1:5], ss5[:, i, 1:5], 1.0 / ML_D, EPS, ALU.mult, ALU.add)
                line(dve.reciprocal(r5[:, i, :], r5[:, i, :]))
                tell("act")
                hear("act")
                if i == 0:
                    dve.wait_ge(row_in, 64)
                stt(O[:, i, 0:512], O[:, i, 0:512], r5[:, i, 0:1], ROW[:, 0:512], ALU.mult, ALU.mult)
                tt(heads, heads, bcast(r5[:, i, 1:5].unsqueeze(2), [P, 4, ML_D]), ALU.mult)
                tt(o, o, ROW[:, 512:1024], ALU.mult)
                tell("pe")
            for i in range(NT + 1):
                if i < NT:
                    if i % 2 == 0:
                        dve.wait_ge(dma_in[i // 2], 48)
                    for n in range(2):
                        c = slice(n * HALF, (n + 1) * HALF)
                        empty(lambda b: dve.tensor_tensor(O[:, i, c], b, X[:, i, c], ALU.add))
                    root(i)
                    ts(NORMED2[i % 2], O[:, i, :], rstd[:, i:i + 1], None, ALU.mult)
                    tell("pe")
                if i:
                    turned_tile(i - 1, normcols["norm_cross_2"])
            next_phase()

            CQ, M2, MT, CK, CV, S, PT, OT = cross_area()
            hear("act")
            ts(rstd[:, 8:10], ss[:, 8:10], 1.0 / D, EPS, ALU.mult, ALU.add)
            line(dve.reciprocal(rstd[:, 8:10], rstd[:, 8:10]))
            tell("act")
            hear("act")
            for i in range(2):
                ts(M2[:, i, :], M2[:, i, :], rstd[:, 8 + i:9 + i], None, ALU.mult)
            tell("pe")
            for m, half, ring in fm_fills(4):
                if ring is ringV:
                    empty(lambda b: dve.tensor_scalar(CQ[:, m, half * HALF:(half + 1) * HALF], b, P ** -0.5, None, ALU.mult))
            for f in range(NK):
                empty(lambda b: dve.tensor_scalar(MT[:, f, :], b[:, 0:MEM], normcols["norm_mem_2"][:, f:f + 1], None,
                                                  ALU.mult))
            for n in range(NT + 3):
                if 1 <= n <= NT:
                    s = S[(n - 1) % 2]
                    m = slice(4 * ((n - 1) % 2), 4 * ((n - 1) % 2) + 4)
                    hear("act")
                    line(dve.tensor_reduce(rden[:, m], s, AX_X, ALU.add))
                    line(dve.reciprocal(rden[:, m], rden[:, m]))
                    tt(s, s, bcast(rden[:, m].unsqueeze(2), [P, 4, MEM]), ALU.mult)
                    tell("pe")
                if n < NT:
                    s = S[n % 2]
                    m = slice(4 * (n % 2), 4 * (n % 2) + 4)
                    for x in range(2):
                        empty(lambda b: dve.tensor_copy(s[:, 2 * x:2 * x + 2, :], cut(b, 2)))
                    line(dve.tensor_reduce(mx[:, m], s, AX_X, ALU.max))
                    tt(s, s, bcast(mx[:, m].unsqueeze(2), [P, 4, MEM]), ALU.subtract)
                    tell("act")
                if n >= 3:
                    i = n - 3
                    root_at(i)
                    if i >= 3:
                        hear("pool")
                    ts(NORMED3[i % 3], O[:, i, :], rstd[:, i:i + 1], None, ALU.mult)
                    normed_ready.tell(dve)
                    tell("pool")
                if 2 <= n <= NT + 1:
                    i = n - 2
                    for half in range(2):
                        c = slice(half * HALF, (half + 1) * HALF)
                        empty(lambda b: dve.tensor_tensor(O[:, i, c], O[:, i, c], b, ALU.add))
                    tell("act")
                if n >= 3:
                    turned_tile(n - 3, normcols["norm_ffn_2"])
            next_phase()

            n = GROUPS + EXPERTS
            empty(lambda b: dve.tensor_tensor(LG, cut(b[:, 0:NT * n], NT), bcast(lg_bias.unsqueeze(1), [P, NT, n]), ALU.add))
            iota = const("iota32")

            def reduce(to, of, op):
                line(dve.tensor_reduce(to, of, AX_X, op))

            def wide(ap, n):
                return bcast(ap.unsqueeze(2), [P, NT, n])

            def first_of(onehot, values, best, n):
                tt(onehot, values, wide(best, n), ALU.is_equal)
                stt(onehot, onehot, -1024.0, bcast(iota[:, 0:n].unsqueeze(1), [P, NT, n]), ALU.mult, ALU.add)
                reduce(R4, onehot, ALU.min)
                tt(onehot, onehot, wide(R4, n), ALU.is_equal)

            g, e = LG[:, :, 0:GROUPS], LG[:, :, GROUPS:]
            reduce(R1, g, ALU.max)
            first_of(OHG, g, R1, GROUPS)
            tt(GT, g, wide(R1, GROUPS), ALU.subtract)
            ts(cut(TMP.rearrange("p i e -> p (i e)")[:, 0:NT * GROUPS], NT), OHG, BIG, -BIG, ALU.mult, ALU.add)
            em, pen = EM.rearrange("p i e -> p (i e)"), TMP.rearrange("p i e -> p (i e)")[:, 0:NT * GROUPS]
            line(dve.tensor_copy(EM, e))
            tt(cut(em, NT * GROUPS), cut(em, NT * GROUPS), bcast(pen.unsqueeze(2), [P, NT * GROUPS, PER_GROUP]), ALU.add)
            reduce(R1, EM, ALU.max)
            first_of(OH1, EM, R1, EXPERTS)
            stt(EM, OH1, -3 * BIG, EM, ALU.mult, ALU.add)
            reduce(R2, EM, ALU.max)
            first_of(OH2, EM, R2, EXPERTS)
            tt(R3, R2, R1, ALU.subtract)
            tell("act")
            tt(A2, OH1, OH2, ALU.add)
            line(dve.memset(AC[:, 0, :], 0.0))
            for i in range(NT):
                tt(AC[:, i + 1, :] if i < NT - 1 else AC9, AC[:, i, :], A2[:, i, :], ALU.add)
            tell("pe")
            hear("act")
            reduce(R1, GT, ALU.add)
            ts(R2, R3, 1.0, None, ALU.add)
            tt(R1, R1, R2, ALU.mult)
            line(dve.reciprocal(gates2[:, 0:NT], R1))
            tt(gates2[:, NT:], gates2[:, 0:NT], R3, ALU.mult)
            bank = ringV.take(dve)
            line(dve.tensor_copy(TMP, cut(bank[:, 0:NT * EXPERTS], NT)))
            line(dve.tensor_copy(CN, bank[:, NT * EXPERTS:(NT + 1) * EXPERTS]), ringV.free)
            ts(SPN, CN, float(P), None, ALU.is_gt)
            for k in range(2, NT):
                stt(SPN, CN, float(k * P), SPN, ALU.is_gt, ALU.add)
            line(dve.tensor_tensor_scan(INC, bcast(one, [P, EXPERTS]), SPN, 0.0, ALU.mult, ALU.add))
            tt(KE, INC, SPN, ALU.subtract)
            tt(KE, KE, iota, ALU.subtract)
            ts(KE, KE, float(EXPERTS - 1), float(P), ALU.add, ALU.mult)
            ts(SM, TMP, float(P), None, ALU.is_ge)
            tt(SM, SM, bcast(KE.unsqueeze(1), [P, NT, EXPERTS]), ALU.mult)
            tt(SM, SM, TMP, ALU.add)
            stt(SM, bcast(iota.unsqueeze(1), [P, NT, EXPERTS]), float(P), SM, ALU.mult, ALU.add)
            for x, oh in ((0, OH1), (1, OH2)):
                tt(TMP, SM, oh, ALU.mult)
                reduce(R4, TMP, ALU.add)
                copy(slot_id[:, x * NT:(x + 1) * NT], R4)
            tell("pool")
            tt(SPM, bcast(INC.unsqueeze(1), [P, SPARE, EXPERTS]), bcast(iota[:, 0:SPARE].unsqueeze(2), [P, SPARE, EXPERTS]),
               ALU.is_le)
            reduce(CN[:, 0:SPARE], SPM, ALU.add)
            ts(CN[:, 0:SPARE], CN[:, 0:SPARE], float(EXPERTS - 1), None, ALU.min)
            copy(CN[:, SPARE:SPARE + 1], INC[:, EXPERTS - 1:EXPERTS])
            copy(spare_map[:, :], CN[:, 0:SPARE + 1])
            empty(lambda b: dve.tensor_copy(token_list[:, :], b[:, 0:BLOCKS]))
            for x in range(2):
                dve.sem_inc(y_stored[x], 16)
            dve.sem_inc(y0_out, 1)
            dve.sem_inc(y1_out, 1)
            next_phase()

            V0, V1, V2, V3 = banks[4:8]
            ffn = normcols["norm_ffn_2"]

            def block_ready(x, sem):
                for half, bank in ((0, V1), (1, V2)):
                    k = slice(4 * half, 4 * half + 4)
                    dve.tensor_tensor(XT[x][:, k, :], cut(bank, 4), bcast(ffn[:, k].unsqueeze(2), [P, 4, P]), ALU.mult)\
                        .then_inc(sem, 1)

            dve.wait_ge(tokens_turned, 1)
            block_ready(0, tokens_ready)
            with dve.Fori(0, EXPERTS // 2) as it:
                for x in range(2):
                    dve.wait_ge(up_full, it * 2 + x + 1)
                    dve.wait_ge(silu_ready, it * 2 + x + 1)
                    dve.tensor_tensor(HID, SILU, V0, ALU.mult).then_inc(hidden_ready, 1)
                    dve.wait_ge(tokens_turned, it * 2 + x + 2)
                    block_ready(1 - x, tokens_ready)
                    dve.wait_ge(down1_full, it * 2 + x + 1)
                    dve.wait_ge(y_stored[x], it * 16 + 16)
                    dve.tensor_copy(YO[x][:, HALF:D], V3).then_inc(y1_out, 1)
            spare = spare_count(dve)
            with dve.If(spare > 0):
                with dve.Fori(0, spare) as s:
                    dve.wait_ge(sp_turned, s + 1)
                    block_ready(0, sp_ready)
                    dve.wait_ge(sp_up, s + 1)
                    dve.wait_ge(sp_silu, s + 1)
                    dve.tensor_tensor(HID, SILU, V0, ALU.mult).then_inc(sp_hidden, 1)
                    dve.wait_ge(sp_down1, s + 1)
                    dve.tensor_copy(YO[0][:, HALF:D], V3).then_inc(sp_y1, 1)
            dve.wait_ge(moe_over, 1)
            for i in range(NT + 1):
                if i < NT:
                    if i % 2 == 0:
                        dve.wait_ge(dma_in[i // 2], 64)
                    dve.wait_ge(combined[i], 32)
                    for x in range(2):
                        stt(O[:, i, :], YG[2 * i + x], gates2[:, x * NT + i:x * NT + i + 1], O[:, i, :], ALU.mult, ALU.add)
                    tell("act")
                if i:
                    final_squares.hear(dve)
                    r = rstd[:, i - 1:i]
                    ts(r, ss[:, i - 1:i], 1.0 / D, EPS, ALU.mult, ALU.add)
                    line(dve.reciprocal(r, r))
                    tell("act")
                    hear("act")
                    if i == 1:
                        dve.wait_ge(row_in, 96)
                    stt(O[:, i - 1, :], O[:, i - 1, :], r, FINAL_ROW, ALU.mult, ALU.mult)
                    dve.sem_inc(final_ready, 1)

        x1 = scratch("x1", [NT, P, D])

        @block.gpsimd
        def _(pool):
            line = Line(pool, pool_own)
            phases = [0]
            stored = [0]

            def tell(who):
                words["pool", who].tell(pool)

            def hear(who):
                words[who, "pool"].hear(pool)

            def tt(o, a, b, op):
                line(pool.tensor_tensor(o, a, b, op))

            def next_phase():
                phases[0] += 1
                pool.sem_inc(phase, 1)
                pool.wait_ge(phase, 4 * phases[0])

            def bcast(ap, shape):
                return ap.to_broadcast(shape)

            def load_rows(to, of, pairs=range(4)):
                for n in pairs:
                    pool.dma_start(to[:, 2 * n:2 * n + 2, :], of[2 * n:2 * n + 2].rearrange("i p d -> p i d"))\
                        .then_inc(dma_in[n], 16)

            def store_rows(to, of):
                pool.dma_start(to.rearrange("i p d -> p i d"), of).then_inc(dma_out, 16)
                stored[0] += 1
                pool.wait_ge(dma_out, 16 * stored[0])

            x_rows = A["x"][0].rearrange("(i p) d -> i p d", p=P)
            load_rows(O, x_rows)
            next_phase()

            def linear(name):
                Q, K, G, V, E, Qe, Ke, S = lin_area()
                for pair in range(2):
                    B = G[:, pair]
                    hear("dve")

                    def differ(lvl):
                        n = P >> lvl
                        b = level(cut(B, NT), n)
                        tt(level(E[lvl % 3], n), b, bcast(b[:, :, :, n // 2 - 1:n // 2], [P, NT, P // n, n]), ALU.subtract)
                        tell("act")

                    differ(0)
                    if pair:
                        hear("act")
                    tt(Ke[1], K[:, pair], Q[:, pair], ALU.mult)
                    tell("pe")
                    differ(1)
                    for lvl in range(LEVELS):
                        if lvl + 2 < LEVELS:
                            differ(lvl + 2)
                        hear("act")
                        hear("dve")
                        n = P >> lvl
                        h = n if lvl < 2 else n // 2
                        tt(level(cut(Ke[lvl % 2], NT), n)[:, :, :, 0:h], level(cut(K[:, pair], NT), n)[:, :, :, 0:h],
                           level(E[lvl % 3], n)[:, :, :, 0:h], ALU.mult)
                        tell("pe")
                    b = cut(B, NT)
                    tt(E[0], bcast(b[:, :, P - 1:P], [P, NT, P]), b, ALU.subtract)
                    tell("act")
                    hear("act")
                    hear("dve")
                    tt(cut(Ke[0], NT), cut(K[:, pair], NT), E[0], ALU.mult)
                    tell("pe")

            linear("a")
            words["act", "pool"].hear(pool)
            next_phase()
            linear("b")
            words["act", "pool"].hear(pool)
            next_phase()

            Q, K, V, Z, L, R = sb_area()
            sums = 0
            for h, c in SB_STEPS:
                l = L[c]
                for at, j, t0, above in sb_blocks(c):
                    if at:
                        if sums >= 2:
                            pool.wait_ge(ringV.full, stick_sums_used[sums - 2])
                        new = min(above + P, HALF) if j >= 4 * c - 1 else above
                        if new > above:
                            line(pool.tensor_copy(R[:, sums % 2, above:new], l[:, at - 1, above:new]))
                        if new < HALF:
                            tt(R[:, sums % 2, new:HALF], R[:, 1 - sums % 2, new:HALF], l[:, at - 1, new:HALF], ALU.add)
                        tell("pe")
                        sums += 1
                    hear("dve")
            next_phase()

            load_rows(X, x_rows)
            pool.dma_start(ROW, A["final_norm_w"].rearrange("(a n) -> a n", a=1).partition_broadcast(P)).then_inc(row_in, 16)
            pool.dma_start(BIAS_ROW, A["b_ada"][:, 2 * D:3 * D].partition_broadcast(P)).then_inc(row_in, 16)
            for i in range(NT):
                hear("dve")
                pool.dma_start(x1[i], O[:, i, :]).then_inc(dma_out, 16)
                stored[0] += 1
            pool.wait_ge(dma_out, 16 * stored[0])
            next_phase()

            zeros = masks.bitcast(F32)
            line(pool.memset(zeros, 0.0))
            pool.dma_start(y_dram[EXPERTS:BLOCKS].rearrange("b p d -> p b d"),
                           zeros.unsqueeze(1).to_broadcast([P, SPARE, D])).then_inc(spare_cleared, 16)
            pool.dma_start(tok_dram.rearrange("(b p) a -> b (p a)", p=P), zeros[0:BLOCKS, 0:P]).then_inc(tok_in, 16)
            next_phase()
            next_phase()
            for n, (name, at) in enumerate((("norm_att_out_2", 0), ("norm_ml_out_2", 512))):
                pool.dma_start(ROW[:, at:at + 512], A[name].partition_broadcast(P)).then_inc(row_in, 16)
                pool.wait_ge(row_in, 16 * (n + 3))
            load_rows(X, x1)
            CQ, M2, MT, CK, CV, S, PT, OT = cross_area()
            pool.dma_start(M2, A["mem_2"][0].rearrange("(i p) d -> p i d", p=P)).then_inc(row_in, 16)
            pool.wait_ge(row_in, 80)
            next_phase()
            xn_rows = xn_dram.rearrange("(i p) d -> i p d", p=P)
            for i in range(NT):
                hear("dve")
                for to, of in ((x3_dram[i], O[:, i, :]), (xn_rows[i], NORMED3[i % 3])):
                    pool.dma_start(to, of).then_inc(dma_out, 16)
                    stored[0] += 1
                pool.wait_ge(dma_out, 16 * stored[0])
                if i + 3 < NT:
                    tell("dve")
            next_phase()
            pool.wait_ge(spare_cleared, 16)
            pool.wait_ge(tok_in, 16)
            hear("dve")
            for x in range(2):
                for i in range(NT):
                    pool.indirect_dma_start(tok_dram, bass.IndirectOffsetOnAxis(ap=slot_id[:, x * NT + i:x * NT + i + 1], axis=0),
                                            const("token")[:, i:i + 1], None).then_inc(scattered, 16)
            pool.wait_ge(scattered, 16 * 2 * NT)
            pool.dma_start(TOKF[0:BLOCKS, :], tok_dram.rearrange("(b p) a -> b (p a)", p=P)).then_inc(tok_in, 16)
            pool.wait_ge(tok_in, 32)
            tell("pe")
            next_phase()

            def gather_block(place, x, row, sem):
                pool.indirect_dma_start(row, None, xn_dram, bass.IndirectOffsetOnAxis(ap=index[place][:, :], axis=0))\
                    .then_inc(sem, 16)

            for x in range(2):
                pool.tensor_copy(index[x][:, :], token_list[:, x:x + 1]).then_inc(index_ready, 1)
                pool.wait_ge(index_ready, x + 1)
                gather_block(x, x, XG[x], rows_gathered[x])
            with pool.Fori(0, EXPERTS // 2) as it:
                for x in range(2):
                    pool.wait_ge(tokens_turned, it * 2 + x + 1)
                    pool.tensor_copy(index[x][:, :], token_list[:, bass.ds(it * 2 + x + 2, 1)]).then_inc(index_ready, 1)
                    pool.wait_ge(index_ready, it * 2 + x + 3)
                    pool.sem_inc(pool_passed, 1)
                    gather_block(x, x, XG[x], rows_gathered[x])
            for x in range(2):
                pool.wait_ge(rows_gathered[x], 16 * (EXPERTS // 2 + 1))
            spare = spare_count(pool)
            with pool.If(spare > 0):
                with pool.Fori(0, spare) as s:
                    pool.wait_ge(sp_over, s + 1)
                    pool.tensor_copy(index[2][:, :], token_list[:, bass.ds(s + EXPERTS, 1)]).then_inc(sp_index, 1)
                    pool.wait_ge(sp_index, s + 1)
                    pool.sem_inc(pool_passed, 1)
                    gather_block(2, 0, XG[0], sp_rows)
            pool.wait_ge(moe_over, 1)
            for i in range(NT):
                if i % 2 == 0:
                    load_rows(O, x3_dram, [i // 2])
                for x in range(2):
                    pool.indirect_dma_start(YG[2 * i + x], None, y_dram.rearrange("b p d -> (b p) d"),
                                            bass.IndirectOffsetOnAxis(ap=slot_id[:, x * NT + i:x * NT + i + 1], axis=0))\
                        .then_inc(combined[i], 16)
                if i == 0:
                    pool.dma_start(FINAL_ROW, A["norm_final_2"].rearrange("(a n) -> a n", a=1).partition_broadcast(P))\
                        .then_inc(row_in, 16)

        @block.sync
        def _(sp):
            used = {n: chunk_over.get(name) for name, n in chunk_of.items()}
            for n, parts in enumerate(chunks):
                if n >= 3:
                    a, v = used[n - 3]
                    if a:
                        sp.wait_ge(ringA.full, a)
                    if v:
                        sp.wait_ge(ringV.full, v)
                at = 0
                for w, lo, hi in parts:
                    to = cut(slots[:, (n % 3) * NK * HALF:(n % 3 + 1) * NK * HALF], w.shape[1])
                    sp.dma_start(to[:, :, at:at + hi - lo], w[:, :, lo:hi])\
                        .then_inc(slot_full[n % 3], 16)
                    at += hi - lo

            def load_expert(x, e, sems):
                wg, wu, wd = expert_weights(x)
                for to, name, s in zip((wg, wu, wd), ("w_e_gate_2", "w_e_up_2", "w_e_down_2"), sems):
                    of = A[name][0][bass.ds(e, 1)].rearrange("e (k p) n -> p (e k) n", p=P)
                    sp.dma_start(to, of).then_inc(s, 16)

            sp.wait_ge(ringA.full, chunk_over["router"][0])
            sp.wait_ge(ringV.full, chunk_over["router"][1])
            load_expert(0, 0, weights_in[0])
            sp.wait_ge(phase, 4 * PHASES_BEFORE_ROUTING)
            load_expert(1, 1, weights_in[1])
            with sp.Fori(0, EXPERTS // 2 - 1) as it:
                for x in range(2):
                    for (to, name, arrived), over in zip(
                            zip(expert_weights(x), ("w_e_gate_2", "w_e_up_2", "w_e_down_2"), weights_in[x]),
                            (up_full, up_full, down1_full)):
                        sp.wait_ge(over, it * 2 + x + 1)
                        sp.sem_inc(sp_passed, 1)
                        of = A[name][0][bass.ds(it * 2 + x + 2, 1)].rearrange("e (k p) n -> p (e k) n", p=P)
                        sp.dma_start(to, of).then_inc(arrived, 16)
            sp.wait_ge(phase, 4 * (PHASES_BEFORE_ROUTING + 1))
            spare = spare_count(sp)
            with sp.If(spare > 0):
                with sp.Fori(0, spare) as s:
                    sp.wait_ge(sp_over, s + 1)
                    sp.sem_inc(sp_passed, 1)
                    e = sp.value_load(spare_map[0:1, bass.ds(s, 1)], min_val=0, max_val=EXPERTS - 1)
                    load_expert(0, e, [sp_weights] * 3)
            for i in range(NT):
                sp.wait_ge(final_ready, i + 1)
                sp.dma_start(out[0, i * P:(i + 1) * P, :], O[:, i, :]).then_inc(out_sem[i % 4], 16)
            for n in range(4):
                sp.wait_ge(out_sem[n], 32)


_INS = ["x", "c", "w_ada", "b_ada", "w_in", "w_gla_gate2", "b_gla_gate", "gla_norm_w", "hgrn_lb_logits", "hgrn_norm_w",
        "w_out", "final_norm_w", "mem_2", "norm_mix_2", "w_in_2", "b_gates_2", "conv_w_2", "conv_b_2", "att_sinks_2",
        "norm_att_out_2", "norm_ml_out_2", "w_out_2", "norm_cross_2", "norm_mem_2", "w_cq_2", "w_ckv_2", "w_co_2",
        "norm_ffn_2", "w_router_group_2", "b_router_group_2", "w_router_expert_2", "b_router_expert_2", "w_e_gate_2",
        "w_e_up_2", "w_e_down_2", "norm_final_2"]


def kernel(**inputs):
    import numpy as _np
    import concourse.bacc as _bacc
    from concourse import mybir as _mybir
    from concourse.bass_utils import run_bass_kernel_spmd as _run

    nc = _bacc.Bacc("TRN2", target_bir_lowering=False, num_devices=1)
    arrays, args = {}, {}
    for name in _INS:
        arrays[f"in_{name}_dram"] = _np.ascontiguousarray(inputs[name])
    for name, table in zip(("consts", "masks"), constants()):
        arrays[f"in_{name}_dram"] = table
    for name in _INS + ["consts", "masks"]:
        a = arrays[f"in_{name}_dram"]
        args[name] = nc.dram_tensor(f"in_{name}_dram", a.shape, _mybir.dt.from_np(a.dtype), kind="ExternalInput").ap()
    out = nc.dram_tensor("out_dram", (1, T, D), F32, kind="ExternalOutput").ap()
    program(nc, args, out)
    r = _run(nc, [arrays], core_ids=[0])
    return r.results[0]["out_dram"]
```
